# Optimizing a Trainium2 kernel written in Bass

```python
import math
import jax
import jax.numpy as jnp
from jax import lax
import numpy as np
import jax, jax.numpy as jnp

D_MODEL = 1024
BATCH = 1
SEQ = 256
DEPTH = 2

N_MIXERS = 3
HEAD_DIM = 64
DIFF_HEADS = D_MODEL // (2 * HEAD_DIM)
ATTN_QBLOCK = 128
DIL_HEADS = D_MODEL // HEAD_DIM
DIL_PATTERNS = ((128, 1), (512, 4), (2048, 16))
DIL_QBLOCK = 64
RWKV_HEADS = D_MODEL // HEAD_DIM
DECAY_LORA = 64
AAA_LORA = 64
GATE_LORA = 128
MEM_LEN = 256
XATT_HEADS = 4
D_FF = 2816
CONV_WIDTH = 3
ALPHA = (2 * DEPTH) ** 0.25
BETA = (8 * DEPTH) ** -0.25
LN_EPS = 1e-5
GN_EPS = 64e-5
NEG_INF = -1e30
N_A = len(range(0, DEPTH, N_MIXERS))
N_B = len(range(1, DEPTH, N_MIXERS))
N_C = len(range(2, DEPTH, N_MIXERS))


def layer_norm(x, g, b):
    xf = x.astype(jnp.float32)
    mu = jnp.mean(xf, -1, keepdims=True)
    var = jnp.mean(jnp.square(xf - mu), -1, keepdims=True)
    return ((xf - mu) * lax.rsqrt(var + LN_EPS) * g + b).astype(x.dtype)

def rms_norm(x, g):
    xf = x.astype(jnp.float32)
    return (xf * lax.rsqrt(jnp.mean(jnp.square(xf), -1, keepdims=True) + LN_EPS) * g).astype(x.dtype)

def alibi_slopes(n):
    return jnp.exp2(-8.0 * jnp.arange(1, n + 1, dtype=jnp.float32) / n)

def diff_attention(x, w_qkv, lam, subln, w_o, lambda_init):
    B, S, D = x.shape
    H, E = DIFF_HEADS, HEAD_DIM
    q, k, v = jnp.split(x @ w_qkv, 3, axis=-1)
    q = q.reshape(B, S, H, 2, E)
    k = k.reshape(B, S, H, 2, E)
    v = v.reshape(B, S, H, 2 * E)
    lamf = lam.astype(jnp.float32)
    lam_full = jnp.exp(jnp.sum(lamf[0] * lamf[1])) - jnp.exp(jnp.sum(lamf[2] * lamf[3])) + lambda_init
    slopes = alibi_slopes(H)
    pos = jnp.arange(S)
    nblk = S // ATTN_QBLOCK
    qb = q.reshape(B, nblk, ATTN_QBLOCK, H, 2, E).transpose(1, 0, 2, 3, 4, 5)
    starts = jnp.arange(nblk) * ATTN_QBLOCK

    def block(args):
        q_blk, start = args
        s = jnp.einsum('bqhce,bkhce->bhcqk', q_blk, k,
                       preferred_element_type=jnp.float32) * (E ** -0.5)
        dist = jnp.abs((start + jnp.arange(ATTN_QBLOCK))[:, None] - pos[None, :]).astype(jnp.float32)
        s = s - slopes[None, :, None, None, None] * dist[None, None, None]
        p = jax.nn.softmax(s, axis=-1)
        attn = p[:, :, 0] - lam_full * p[:, :, 1]
        return jnp.einsum('bhqk,bkhe->bqhe', attn.astype(v.dtype), v)

    o = lax.map(block, (qb, starts))
    o = o.transpose(1, 0, 2, 3, 4).reshape(B, S, H, 2 * E)
    o = rms_norm(o, subln) * (1.0 - lambda_init)
    return o.reshape(B, S, D) @ w_o

def dilated_group(q, k, v, window, dilation, slopes):
    B, S, H, E = q.shape
    half = window // (2 * dilation)
    L = S // dilation
    nblk = -(-L // DIL_QBLOCK)
    Lp = nblk * DIL_QBLOCK
    KB = DIL_QBLOCK + 2 * half

    def to_res(a):
        return a.reshape(B, L, dilation, H, E).transpose(0, 2, 1, 3, 4)

    qr = jnp.pad(to_res(q), ((0, 0), (0, 0), (0, Lp - L), (0, 0), (0, 0)))
    pad_k = ((0, 0), (0, 0), (half, Lp - L + half), (0, 0), (0, 0))
    kr = jnp.pad(to_res(k), pad_k)
    vr = jnp.pad(to_res(v), pad_k)
    starts = jnp.arange(nblk) * DIL_QBLOCK
    idx = starts[:, None] + jnp.arange(KB)[None, :]
    kb = kr[:, :, idx]
    vb = vr[:, :, idx]
    qb = qr.reshape(B, dilation, nblk, DIL_QBLOCK, H, E)
    s = jnp.einsum('brnqhe,brnkhe->brnhqk', qb, kb,
                   preferred_element_type=jnp.float32) * (E ** -0.5)
    u_q = starts[:, None] + jnp.arange(DIL_QBLOCK)[None, :]
    u_k = idx - half
    rel = u_k[:, None, :] - u_q[:, :, None]
    valid = (jnp.abs(rel) <= half) & (u_k[:, None, :] >= 0) & (u_k[:, None, :] < L)
    dist = (dilation * jnp.abs(rel)).astype(jnp.float32)
    bias = -slopes[None, :, None, None] * dist[:, None]
    s = jnp.where(valid[:, None], s + bias, NEG_INF)
    lse = jax.nn.logsumexp(s, axis=-1)
    p = jnp.exp(s - lse[..., None])
    o = jnp.einsum('brnhqk,brnkhe->brnqhe', p.astype(v.dtype), vb)
    o = o.reshape(B, dilation, Lp, H, E)[:, :, :L].transpose(0, 2, 1, 3, 4).reshape(B, S, H, E)
    lse = lse.transpose(0, 1, 2, 4, 3).reshape(B, dilation, Lp, H)[:, :, :L]
    lse = lse.transpose(0, 2, 1, 3).reshape(B, S, H)
    return o, lse

def dilated_attention(x, w_qkv, w_o):
    B, S, D = x.shape
    H, E, G = DIL_HEADS, HEAD_DIM, len(DIL_PATTERNS)
    qkv = (x @ w_qkv).reshape(B, S, G, 3, H, E)
    slopes = alibi_slopes(H)
    outs, lses = [], []
    for g, (window, dilation) in enumerate(DIL_PATTERNS):
        o, l = dilated_group(qkv[:, :, g, 0], qkv[:, :, g, 1], qkv[:, :, g, 2], window, dilation, slopes)
        outs.append(o)
        lses.append(l)
    wts = jax.nn.softmax(jnp.stack(lses), axis=0)
    o = jnp.sum(wts[..., None] * jnp.stack(outs).astype(jnp.float32), axis=0)
    return o.astype(x.dtype).reshape(B, S, D) @ w_o

def token_shift(x, reverse):
    if reverse:
        return jnp.pad(x[:, 1:], ((0, 0), (0, 1), (0, 0)))
    return jnp.pad(x[:, :-1], ((0, 0), (1, 0), (0, 0)))

def wkv7_scan(r, w, k, v, kk, a, reverse):
    B, S, H, N = r.shape
    seq = tuple(t.transpose(1, 0, 2, 3) for t in (r, w, k, v, kk, a))

    def step(state, inp):
        r_t, w_t, k_t, v_t, kk_t, a_t = inp
        sa = jnp.einsum('bhij,bhj->bhi', state, -kk_t)
        state = (state * w_t[:, :, None, :] + sa[..., None] * (kk_t * a_t)[:, :, None, :]
                 + v_t[..., None] * k_t[:, :, None, :])
        return state, jnp.einsum('bhij,bhj->bhi', state, r_t)

    _, y = lax.scan(step, jnp.zeros((B, H, N, N), jnp.float32), seq, reverse=reverse)
    return y.transpose(1, 0, 2, 3)

def head_group_norm(y, g, b):
    H, N = y.shape[-2], y.shape[-1]
    mu = jnp.mean(y, -1, keepdims=True)
    var = jnp.mean(jnp.square(y - mu), -1, keepdims=True)
    return (y - mu) * lax.rsqrt(var + GN_EPS) * g.reshape(H, N) + b.reshape(H, N)

def rwkv7_direction(x, mu, w_r, w_k, w_v, w0, w1, w2, a0, a1, a2, g1, g2, k_k, k_a, r_k,
                    gn_g, gn_b, reverse):
    B, S, D = x.shape
    H, N = RWKV_HEADS, HEAD_DIM
    xx = token_shift(x, reverse) - x
    xr, xw, xk, xv, xa, xg = (x + xx * mu[j] for j in range(6))
    r = xr @ w_r
    k = xk @ w_k
    v = xv @ w_v
    w_log = -jax.nn.softplus(-(w0 + jnp.tanh(xw @ w1) @ w2).astype(jnp.float32)) - 0.5
    w = jnp.exp(-jnp.exp(w_log))
    a = jax.nn.sigmoid((a0 + (xa @ a1) @ a2).astype(jnp.float32))
    g = jax.nn.sigmoid(xg @ g1) @ g2

    def heads(t):
        return t.astype(jnp.float32).reshape(B, S, H, N)

    r, k, v, w, a = heads(r), heads(k), heads(v), heads(w), heads(a)
    kk = k * k_k.astype(jnp.float32).reshape(H, N)
    kk = kk / jnp.maximum(jnp.linalg.norm(kk, axis=-1, keepdims=True), 1e-12)
    k = k * (1.0 + (a - 1.0) * k_a.astype(jnp.float32).reshape(H, N))
    y = wkv7_scan(r, w, k, v, kk, a, reverse)
    y = head_group_norm(y, gn_g, gn_b) + jnp.sum(r * k * r_k.astype(jnp.float32), -1, keepdims=True) * v
    return (y.reshape(B, S, D) * g).astype(x.dtype)

def rwkv7_time_mix(x, mu, w_rkv, w0, w1, w2, a0, a1, a2, g1, g2, k_k, k_a, r_k, gn_g, gn_b, w_o):
    fwd = rwkv7_direction(x, mu[0], w_rkv[0], w_rkv[1], w_rkv[2], w0[0], w1[0], w2[0], a0[0], a1[0], a2[0],
                          g1[0], g2[0], k_k[0], k_a[0], r_k, gn_g, gn_b, False)
    bwd = rwkv7_direction(x, mu[1], w_rkv[0], w_rkv[1], w_rkv[2], w0[1], w1[1], w2[1], a0[1], a1[1], a2[1],
                          g1[1], g2[1], k_k[1], k_a[1], r_k, gn_g, gn_b, True)
    return (fwd + bwd) @ w_o

def memory_cross_attention(x, mem, w_q, w_kv, w_o):
    B, S, D = x.shape
    M = mem.shape[1]
    H = XATT_HEADS
    E = D // H
    q = (x @ w_q).reshape(B, S, H, E)
    kv = (mem @ w_kv).reshape(B, M, 2, H, E)
    s = jnp.einsum('bshe,bmhe->bhsm', q, kv[:, :, 0], preferred_element_type=jnp.float32) * (E ** -0.5)
    p = jax.nn.softmax(s, axis=-1).astype(x.dtype)
    o = jnp.einsum('bhsm,bmhe->bshe', p, kv[:, :, 1])
    return o.reshape(B, S, D) @ w_o

def conv_glu(x, w_in, conv_w, conv_b, w_out):
    gate, val = jnp.split(x @ w_in, 2, axis=-1)
    gate = lax.conv_general_dilated(gate, conv_w[:, None, :], window_strides=(1,),
                                    padding=((CONV_WIDTH // 2, CONV_WIDTH // 2),),
                                    dimension_numbers=('NWC', 'WIO', 'NWC'),
                                    feature_group_count=gate.shape[-1]) + conv_b
    return (jax.nn.gelu(gate, approximate=False) * val) @ w_out

def first_inputs(seed: int = 0) -> dict:
    key = jax.random.key(seed)
    keys = iter(jax.random.split(key, 48))
    D, F, H, N = D_MODEL, D_FF, RWKV_HEADS, HEAD_DIM
    G = len(DIL_PATTERNS)
    inv = D ** -0.5

    def normal(shape, scale):
        return jax.random.normal(next(keys), shape, jnp.float32) * scale

    def uniform(shape, lo, hi):
        return jax.random.uniform(next(keys), shape, jnp.float32, lo, hi)

    return {
        "x": normal((BATCH, SEQ, D), 1.0),
        "mem": normal((BATCH, MEM_LEN, D), 1.0),
        "diff_w_qkv": normal((N_A, D, 3 * D), inv),
        "diff_lambda": normal((N_A, 4, HEAD_DIM), 0.1),
        "diff_subln": 1.0 + normal((N_A, 2 * HEAD_DIM), 0.02),
        "diff_w_o": normal((N_A, D, D), inv * BETA),
        "dil_w_qkv": normal((N_B, D, G * 3 * D), inv),
        "dil_w_o": normal((N_B, D, D), inv * BETA),
        "rwkv_mu": uniform((N_C, 2, 6, D), 0.0, 1.0),
        "rwkv_w_rkv": normal((N_C, 3, D, D), inv),
        "rwkv_w0": uniform((N_C, 2, D), -5.0, 0.0),
        "rwkv_w1": normal((N_C, 2, D, DECAY_LORA), inv),
        "rwkv_w2": normal((N_C, 2, DECAY_LORA, D), 0.1 * DECAY_LORA ** -0.5),
        "rwkv_a0": normal((N_C, 2, D), 0.1),
        "rwkv_a1": normal((N_C, 2, D, AAA_LORA), inv),
        "rwkv_a2": normal((N_C, 2, AAA_LORA, D), 0.1 * AAA_LORA ** -0.5),
        "rwkv_g1": normal((N_C, 2, D, GATE_LORA), inv),
        "rwkv_g2": normal((N_C, 2, GATE_LORA, D), GATE_LORA ** -0.5),
        "rwkv_k_k": 0.85 + normal((N_C, 2, D), 0.02),
        "rwkv_k_a": 1.0 + normal((N_C, 2, D), 0.02),
        "rwkv_r_k": normal((N_C, H, N), 0.1),
        "rwkv_gn_g": 1.0 + normal((N_C, D), 0.02),
        "rwkv_gn_b": normal((N_C, D), 0.02),
        "rwkv_w_o": normal((N_C, D, D), inv * BETA),
        "xatt_w_q": normal((DEPTH, D, D), inv),
        "xatt_w_kv": normal((DEPTH, D, 2 * D), inv),
        "xatt_w_o": normal((DEPTH, D, D), inv * BETA),
        "ffn_w_in": normal((DEPTH, D, 2 * F), inv),
        "ffn_conv_w": normal((DEPTH, CONV_WIDTH, F), CONV_WIDTH ** -0.5),
        "ffn_conv_b": normal((DEPTH, F), 0.02),
        "ffn_w_out": normal((DEPTH, F, D), F ** -0.5 * BETA),
        "ln_g": 1.0 + normal((DEPTH, 3, D), 0.02),
        "ln_b": normal((DEPTH, 3, D), 0.02),
    }

def first_block(x, mem, diff_w_qkv, diff_lambda, diff_subln, diff_w_o, dil_w_qkv, dil_w_o,
              rwkv_mu, rwkv_w_rkv, rwkv_w0, rwkv_w1, rwkv_w2, rwkv_a0, rwkv_a1, rwkv_a2,
              rwkv_g1, rwkv_g2, rwkv_k_k, rwkv_k_a, rwkv_r_k, rwkv_gn_g, rwkv_gn_b, rwkv_w_o,
              xatt_w_q, xatt_w_kv, xatt_w_o, ffn_w_in, ffn_conv_w, ffn_conv_b, ffn_w_out,
              ln_g, ln_b):
    for i in range(DEPTH):
        m, j = i % N_MIXERS, i // N_MIXERS
        if m == 0:
            lambda_init = 0.8 - 0.6 * math.exp(-0.3 * i)
            h = diff_attention(x, diff_w_qkv[j], diff_lambda[j], diff_subln[j], diff_w_o[j], lambda_init)
        elif m == 1:
            h = dilated_attention(x, dil_w_qkv[j], dil_w_o[j])
        else:
            h = rwkv7_time_mix(x, rwkv_mu[j], rwkv_w_rkv[j], rwkv_w0[j], rwkv_w1[j], rwkv_w2[j],
                               rwkv_a0[j], rwkv_a1[j], rwkv_a2[j], rwkv_g1[j], rwkv_g2[j],
                               rwkv_k_k[j], rwkv_k_a[j], rwkv_r_k[j], rwkv_gn_g[j], rwkv_gn_b[j],
                               rwkv_w_o[j])
        x = layer_norm(ALPHA * x + h, ln_g[i, 0], ln_b[i, 0])
        x = layer_norm(ALPHA * x + memory_cross_attention(x, mem, xatt_w_q[i], xatt_w_kv[i], xatt_w_o[i]),
                       ln_g[i, 1], ln_b[i, 1])
        x = layer_norm(ALPHA * x + conv_glu(x, ffn_w_in[i], ffn_conv_w[i], ffn_conv_b[i], ffn_w_out[i]),
                       ln_g[i, 2], ln_b[i, 2])
    return x


GRID_W = 64
CTX_LEN = 256
N_MIXERS_2 = 2
EPS = 1e-6

SSD_EXPAND = 2
D_INNER = SSD_EXPAND * D_MODEL
SSD_HEADDIM = 64
SSD_HEADS = D_INNER // SSD_HEADDIM
SSD_GROUPS = 8
SSD_HPG = SSD_HEADS // SSD_GROUPS
SSD_STATE = 128
SSD_CONV_K = 5
SSD_CHUNK = 64
SSD_GN = SSD_GROUPS * SSD_STATE
SSD_CONV_DIM = D_INNER + 2 * SSD_GN
SSD_PROJ_DIM = D_INNER + SSD_CONV_DIM + 2 * SSD_HEADS

CONF_K = 31
CONF_DIM = D_MODEL
CONF_H = CONF_DIM // 2

FFN_HIDDEN = (((8 * D_MODEL + 2) // 3 + 255) // 256) * 256

N_SSD_LAYERS = (DEPTH + 1) // 2
N_CONF_LAYERS = DEPTH // 2


def rmsnorm(x, g):
    xf = x.astype(jnp.float32)
    y = xf * lax.rsqrt(jnp.mean(xf * xf, axis=-1, keepdims=True) + EPS)
    return (y * g.astype(jnp.float32)).astype(x.dtype)

def layernorm(x, g, b):
    xf = x.astype(jnp.float32)
    mu = jnp.mean(xf, axis=-1, keepdims=True)
    var = jnp.mean(jnp.square(xf - mu), axis=-1, keepdims=True)
    y = (xf - mu) * lax.rsqrt(var + EPS) * g.astype(jnp.float32) + b.astype(jnp.float32)
    return y.astype(x.dtype)

def modulate(h, shift, scale):
    return h * (1 + scale) + shift

def ada_params(sc, w, b):
    mod = sc @ w + b
    return [t[:, None, :] for t in jnp.split(mod, 6, axis=-1)]

def dwconv1d(x, w, b):
    k = w.shape[0]
    y = lax.conv_general_dilated(
        x, w[:, None, :].astype(x.dtype), window_strides=(1,),
        padding=[(k // 2, k // 2)], dimension_numbers=("NWC", "WIO", "NWC"),
        feature_group_count=x.shape[-1])
    return y + b

def axial_dwconv(u, rows, w, b):
    n, l, ch = u.shape
    g = u.reshape(n, rows, GRID_W, ch)
    hor = dwconv1d(g[..., :CONF_H].reshape(n * rows, GRID_W, CONF_H), w[:, :CONF_H], b[:CONF_H])
    hor = hor.reshape(n, rows, GRID_W, CONF_H)
    cv = ch - CONF_H
    ver_in = jnp.swapaxes(g[..., CONF_H:], 1, 2).reshape(n * GRID_W, rows, cv)
    ver = dwconv1d(ver_in, w[:, CONF_H:], b[CONF_H:]).reshape(n, GRID_W, rows, cv)
    ver = jnp.swapaxes(ver, 1, 2)
    return jnp.concatenate([hor, ver], axis=-1).reshape(n, l, ch)

def ssd_chunked(xh, dt, A, Bm, Cm, h0):
    n, l = xh.shape[:2]
    nc, q = l // SSD_CHUNK, SSD_CHUNK
    x = (xh * dt[..., None]).reshape(n, nc, q, SSD_GROUPS, SSD_HPG, SSD_HEADDIM)
    a_cum = jnp.cumsum((dt * A).reshape(n, nc, q, SSD_GROUPS, SSD_HPG), axis=2)
    Bc = Bm.reshape(n, nc, q, SSD_GROUPS, SSD_STATE)
    Cc = Cm.reshape(n, nc, q, SSD_GROUPS, SSD_STATE)
    idx = jnp.arange(q)
    lower = (idx[:, None] >= idx[None, :])[None, None, :, :, None, None]
    seg = a_cum[:, :, :, None] - a_cum[:, :, None, :]
    decay = jnp.exp(jnp.where(lower, seg, -jnp.inf))
    scores = jnp.einsum("bcqgn,bcsgn->bcqsg", Cc, Bc)
    y_diag = jnp.einsum("bcqsg,bcqsgj,bcsgjp->bcqgjp", scores, decay, x)
    decay_to_end = jnp.exp(a_cum[:, :, -1:] - a_cum)
    states = jnp.einsum("bcsgn,bcsgj,bcsgjp->bcgjpn", Bc, decay_to_end, x)
    chunk_decay = jnp.exp(a_cum[:, :, -1])

    def step(h, inp):
        st, dec = inp
        return h * dec[..., None, None] + st, h

    h_init = h0.reshape(n, SSD_GROUPS, SSD_HPG, SSD_HEADDIM, SSD_STATE)
    h_final, h_prev = lax.scan(step, h_init, (jnp.moveaxis(states, 1, 0), jnp.moveaxis(chunk_decay, 1, 0)))
    h_prev = jnp.moveaxis(h_prev, 0, 1)
    y_off = jnp.einsum("bcqgn,bcgjpn,bcqgj->bcqgjp", Cc, h_prev, jnp.exp(a_cum))
    y = (y_diag + y_off).reshape(n, l, SSD_HEADS, SSD_HEADDIM)
    return y, h_final.reshape(n, SSD_HEADS, SSD_HEADDIM, SSD_STATE)

def ssd_mixer(h, h0_f, h0_b, w_in, conv_w, conv_b, dt_bias_f, dt_bias_b, a_log_f, a_log_b,
              d_skip, norm_w, w_out):
    n, l, _ = h.shape
    f32 = jnp.float32
    zxbcdt = h @ w_in
    z = zxbcdt[..., :D_INNER].astype(f32)
    xbc = jax.nn.silu(dwconv1d(zxbcdt[..., D_INNER:D_INNER + SSD_CONV_DIM], conv_w, conv_b)).astype(f32)
    dt = zxbcdt[..., D_INNER + SSD_CONV_DIM:].astype(f32)
    xs = xbc[..., :D_INNER].reshape(n, l, SSD_HEADS, SSD_HEADDIM)
    Bm = xbc[..., D_INNER:D_INNER + SSD_GN].reshape(n, l, SSD_GROUPS, SSD_STATE)
    Cm = xbc[..., D_INNER + SSD_GN:].reshape(n, l, SSD_GROUPS, SSD_STATE)
    dt_f = jax.nn.softplus(dt[..., :SSD_HEADS] + dt_bias_f.astype(f32))
    dt_b = jax.nn.softplus(dt[..., SSD_HEADS:] + dt_bias_b.astype(f32))
    A_f = -jnp.exp(a_log_f.astype(f32))
    A_b = -jnp.exp(a_log_b.astype(f32))
    y_f, hf = ssd_chunked(xs, dt_f, A_f, Bm, Cm, h0_f)
    flip = lambda t: jnp.flip(t, axis=1)
    y_b, hb = ssd_chunked(flip(xs), flip(dt_b), A_b, flip(Bm), flip(Cm), h0_b)
    y = y_f + flip(y_b) + d_skip.astype(f32)[:, None] * xs
    y = rmsnorm(y.reshape(n, l, D_INNER) * jax.nn.silu(z), norm_w)
    return y.astype(h.dtype) @ w_out, hf, hb

def conformer_conv_module(h, rows, w_pw1, b_pw1, dw_w, dw_b, ln_g, ln_b, w_pw2, b_pw2):
    u = h @ w_pw1 + b_pw1
    u = u[..., :CONF_DIM] * jax.nn.sigmoid(u[..., CONF_DIM:])
    v = dwconv1d(u, dw_w, dw_b) if rows is None else axial_dwconv(u, rows, dw_w, dw_b)
    v = jax.nn.silu(layernorm(v, ln_g, ln_b))
    return v @ w_pw2 + b_pw2

def swiglu(h, w_in, w_out):
    u = h @ w_in
    return (jax.nn.silu(u[..., :FFN_HIDDEN]) * u[..., FFN_HIDDEN:]) @ w_out

def second_inputs(seed: int = 0) -> dict:
    key = jax.random.key(seed)
    ks = jax.random.split(key, 40)
    f32 = jnp.float32
    nrm = lambda k, shape, s: jax.random.normal(k, shape, f32) * s
    NS, NC, D = N_SSD_LAYERS, N_CONF_LAYERS, D_MODEL
    dt0 = jnp.exp(jax.random.uniform(ks[0], (2, NS, SSD_HEADS), f32,
                                     float(np.log(1e-3)), float(np.log(1e-1))))
    dt_bias = dt0 + jnp.log(-jnp.expm1(-dt0))
    a_log = jnp.log(jax.random.uniform(ks[1], (2, NS, SSD_HEADS), f32, 1.0, 16.0))
    return {
        "x": nrm(ks[2], (BATCH, SEQ, D), 1.0),
        "c": nrm(ks[3], (BATCH, D), 1.0),
        "ctx": nrm(ks[4], (BATCH, CTX_LEN, D), 1.0),
        "c_ctx": nrm(ks[5], (D,), 1.0),
        "ada_w": nrm(ks[6], (DEPTH, D, 6 * D), 0.5 * D ** -0.5),
        "ada_b": nrm(ks[7], (DEPTH, 6 * D), 0.01),
        "norm_mix_g": 1.0 + nrm(ks[8], (DEPTH, D), 0.02),
        "norm_ffn_g": 1.0 + nrm(ks[9], (DEPTH, D), 0.02),
        "final_norm_g": 1.0 + nrm(ks[10], (D,), 0.02),
        "ssd_w_in": nrm(ks[11], (NS, D, SSD_PROJ_DIM), D ** -0.5),
        "ssd_conv_w": nrm(ks[12], (NS, SSD_CONV_K, SSD_CONV_DIM), SSD_CONV_K ** -0.5),
        "ssd_conv_b": nrm(ks[13], (NS, SSD_CONV_DIM), 0.01),
        "ssd_dt_bias_f": dt_bias[0],
        "ssd_dt_bias_b": dt_bias[1],
        "ssd_a_log_f": a_log[0],
        "ssd_a_log_b": a_log[1],
        "ssd_d_skip": 1.0 + nrm(ks[14], (NS, SSD_HEADS), 0.02),
        "ssd_norm_w": 1.0 + nrm(ks[15], (NS, D_INNER), 0.02),
        "ssd_w_out": nrm(ks[16], (NS, D_INNER, D), D_INNER ** -0.5),
        "conf_w_pw1": nrm(ks[17], (NC, D, 2 * CONF_DIM), D ** -0.5),
        "conf_b_pw1": nrm(ks[18], (NC, 2 * CONF_DIM), 0.01),
        "conf_dw_w": nrm(ks[19], (NC, CONF_K, CONF_DIM), CONF_K ** -0.5),
        "conf_dw_b": nrm(ks[20], (NC, CONF_DIM), 0.01),
        "conf_ln_g": 1.0 + nrm(ks[21], (NC, CONF_DIM), 0.02),
        "conf_ln_b": nrm(ks[22], (NC, CONF_DIM), 0.01),
        "conf_w_pw2": nrm(ks[23], (NC, CONF_DIM, D), CONF_DIM ** -0.5),
        "conf_b_pw2": nrm(ks[24], (NC, D), 0.01),
        "ffn_w_in": nrm(ks[25], (DEPTH, D, 2 * FFN_HIDDEN), D ** -0.5),
        "ffn_w_out": nrm(ks[26], (DEPTH, FFN_HIDDEN, D), FFN_HIDDEN ** -0.5),
    }

def second_block(x, c, ctx, c_ctx, ada_w, ada_b, norm_mix_g, norm_ffn_g, final_norm_g,
              ssd_w_in, ssd_conv_w, ssd_conv_b, ssd_dt_bias_f, ssd_dt_bias_b, ssd_a_log_f,
              ssd_a_log_b, ssd_d_skip, ssd_norm_w, ssd_w_out,
              conf_w_pw1, conf_b_pw1, conf_dw_w, conf_dw_b, conf_ln_g, conf_ln_b,
              conf_w_pw2, conf_b_pw2, ffn_w_in, ffn_w_out):
    n, l, _ = x.shape
    rows = l // GRID_W
    h_lat, h_ctx = x, ctx
    sc_lat = jax.nn.silu(c)
    sc_ctx = jax.nn.silu(c_ctx)[None, :]
    for i in range(DEPTH):
        need_ctx_out = i < DEPTH - 1
        j = i // N_MIXERS_2
        sh1, s1, g1, sh2, s2, g2 = ada_params(sc_lat, ada_w[i], ada_b[i])
        xn_lat = modulate(rmsnorm(h_lat, norm_mix_g[i]), sh1, s1)
        if i % N_MIXERS_2 == 0:
            p = (ssd_w_in[j], ssd_conv_w[j], ssd_conv_b[j], ssd_dt_bias_f[j], ssd_dt_bias_b[j],
                 ssd_a_log_f[j], ssd_a_log_b[j], ssd_d_skip[j], ssd_norm_w[j], ssd_w_out[j])
            csh1, cs1, cg1, csh2, cs2, cg2 = ada_params(sc_ctx, ada_w[i], ada_b[i])
            xn_ctx = modulate(rmsnorm(h_ctx, norm_mix_g[i]), csh1, cs1)
            h_zero = jnp.zeros((n, SSD_HEADS, SSD_HEADDIM, SSD_STATE), jnp.float32)
            y_ctx, hf_ctx, hb_ctx = ssd_mixer(xn_ctx, h_zero, h_zero, *p)
            y_lat, _, _ = ssd_mixer(xn_lat, hf_ctx, hb_ctx, *p)
            if need_ctx_out:
                h_ctx = h_ctx + cg1 * y_ctx
        else:
            p = (conf_w_pw1[j], conf_b_pw1[j], conf_dw_w[j], conf_dw_b[j], conf_ln_g[j],
                 conf_ln_b[j], conf_w_pw2[j], conf_b_pw2[j])
            y_lat = conformer_conv_module(xn_lat, rows, *p)
            if need_ctx_out:
                csh1, cs1, cg1, csh2, cs2, cg2 = ada_params(sc_ctx, ada_w[i], ada_b[i])
                xn_ctx = modulate(rmsnorm(h_ctx, norm_mix_g[i]), csh1, cs1)
                h_ctx = h_ctx + cg1 * conformer_conv_module(xn_ctx, None, *p)
        h_lat = h_lat + g1 * y_lat
        h_lat = h_lat + g2 * swiglu(modulate(rmsnorm(h_lat, norm_ffn_g[i]), sh2, s2), ffn_w_in[i], ffn_w_out[i])
        if need_ctx_out:
            h_ctx = h_ctx + cg2 * swiglu(modulate(rmsnorm(h_ctx, norm_ffn_g[i]), csh2, cs2),
                                         ffn_w_in[i], ffn_w_out[i])
    return rmsnorm(h_lat, final_norm_g)


_first_inputs = second_inputs


def second_inputs(seed=0):
    import zlib

    import numpy as np

    out = dict(_first_inputs(seed))
    spreads = {}
    factors = {'ctx': 2.811,
     'ada_b': 3.345,
     'norm_mix_g': 6.576,
     'norm_ffn_g': 7.28,
     'final_norm_g': 8.626,
     'ssd_conv_b': 21.855,
     'ssd_d_skip': 64.0,
     'ssd_norm_w': 8.0,
     'conf_b_pw1': 64.0,
     'conf_dw_b': 64.0,
     'conf_ln_g': 64.0,
     'conf_ln_b': 64.0,
     'conf_b_pw2': 64.0}
    for name, (base, spread) in spreads.items():
        noise = np.random.default_rng([zlib.crc32(name.encode()), seed]).standard_normal(out[name].shape)
        drawn = base * np.exp(spread * noise) if base else spread * noise
        out[name] = __import__('jax').numpy.asarray(drawn.astype(out[name].dtype))
    for name, factor in factors.items():
        out[name] = (out[name] * factor).astype(out[name].dtype)
    return out


_narrow_inputs = second_inputs


def second_inputs(seed=0):

    out = dict(_narrow_inputs(seed))
    wider = {'final_norm_g': 3.23,
     'ssd_d_skip': 12.0,
     'conf_ln_g': 3.87,
     'conf_ln_b': 7.83,
     'conf_b_pw2': 5.64}
    for name, times in wider.items():
        mean = out[name].mean()
        out[name] = (mean + times * (out[name] - mean)).astype(out[name].dtype)
    return out


def setup_inputs(seed=0):
    out = dict(first_inputs(seed))
    for name, value in second_inputs(seed + 1).items():
        if name != "x":
            out[name + "_2"] = value
    return out


def reference(
    x, mem, diff_w_qkv, diff_lambda, diff_subln, diff_w_o, dil_w_qkv, dil_w_o, rwkv_mu,
    rwkv_w_rkv, rwkv_w0, rwkv_w1, rwkv_w2, rwkv_a0, rwkv_a1, rwkv_a2, rwkv_g1, rwkv_g2,
    rwkv_k_k, rwkv_k_a, rwkv_r_k, rwkv_gn_g, rwkv_gn_b, rwkv_w_o, xatt_w_q, xatt_w_kv, xatt_w_o,
    ffn_w_in, ffn_conv_w, ffn_conv_b, ffn_w_out, ln_g, ln_b, c_2, ctx_2, c_ctx_2, ada_w_2,
    ada_b_2, norm_mix_g_2, norm_ffn_g_2, final_norm_g_2, ssd_w_in_2, ssd_conv_w_2, ssd_conv_b_2,
    ssd_dt_bias_f_2, ssd_dt_bias_b_2, ssd_a_log_f_2, ssd_a_log_b_2, ssd_d_skip_2, ssd_norm_w_2,
    ssd_w_out_2, conf_w_pw1_2, conf_b_pw1_2, conf_dw_w_2, conf_dw_b_2, conf_ln_g_2, conf_ln_b_2,
    conf_w_pw2_2, conf_b_pw2_2, ffn_w_in_2, ffn_w_out_2,
):
    x = first_block(
        x, mem, diff_w_qkv, diff_lambda, diff_subln, diff_w_o, dil_w_qkv, dil_w_o, rwkv_mu,
        rwkv_w_rkv, rwkv_w0, rwkv_w1, rwkv_w2, rwkv_a0, rwkv_a1, rwkv_a2, rwkv_g1, rwkv_g2,
        rwkv_k_k, rwkv_k_a, rwkv_r_k, rwkv_gn_g, rwkv_gn_b, rwkv_w_o, xatt_w_q, xatt_w_kv,
        xatt_w_o, ffn_w_in, ffn_conv_w, ffn_conv_b, ffn_w_out, ln_g, ln_b,
    )
    return second_block(
        x, c_2, ctx_2, c_ctx_2, ada_w_2, ada_b_2, norm_mix_g_2, norm_ffn_g_2, final_norm_g_2,
        ssd_w_in_2, ssd_conv_w_2, ssd_conv_b_2, ssd_dt_bias_f_2, ssd_dt_bias_b_2, ssd_a_log_f_2,
        ssd_a_log_b_2, ssd_d_skip_2, ssd_norm_w_2, ssd_w_out_2, conf_w_pw1_2, conf_b_pw1_2,
        conf_dw_w_2, conf_dw_b_2, conf_ln_g_2, conf_ln_b_2, conf_w_pw2_2, conf_b_pw2_2,
        ffn_w_in_2, ffn_w_out_2,
    )


_drawn_inputs = setup_inputs


def setup_inputs(seed=0):
    import zlib

    import numpy as np

    out = dict(_drawn_inputs(seed))
    spreads = {}
    factors = {'diff_lambda': 5.956, 'ssd_d_skip_2': 8.0}
    for name, (base, spread) in spreads.items():
        noise = np.random.default_rng([zlib.crc32(name.encode()), seed]).standard_normal(out[name].shape)
        drawn = base * np.exp(spread * noise) if base else spread * noise
        out[name] = jnp.asarray(drawn.astype(out[name].dtype))
    for name, factor in factors.items():
        out[name] = (out[name] * factor).astype(out[name].dtype)
    return out
```

```python
import math
from contextlib import ExitStack, contextmanager

import concourse.bass as bass
import numpy as np
from concourse import mybir

F32 = mybir.dt.float32
I32 = mybir.dt.int32
ALU = mybir.AluOpType
ACT = mybir.ActivationFunctionType
AX = mybir.AxisListType

P = 128
D = 1024
T = 256
NT = T // P
KC = D // P
SLAB = 2048
RING = 4
FF = 2816
FC = FF // P
HEAD = 64
DIFF_HEADS = 8
DIL_HEADS = 16
GROUPS = 3
DILATION = (1, 4, 16)
HALF = 64
XH = 4
ALPHA = 4 ** 0.25
LN_EPS = 1e-5
EPS = 1e-6
LAMBDA_INIT = 0.8 - 0.6 * math.exp(-0.3 * 0)
NEG = 1e30
DI = 2048
SH = 32
SG = 8
CONF_K = 31
GRID_W = 64
ROWS = T // GRID_W
HC = KC // 2

STAGES = [("dq", 4), ("dk", 4), ("dv", 4), ("dwo", 4),
          ("xk0", 4), ("xv0", 4), ("xq0", 4), ("xwo0", 4), ("f0", 46), ("fo0", 11),
          ("gq0", 4), ("gk0", 4), ("gv0", 4), ("gq1", 4), ("gk1", 4), ("gv1", 4),
          ("gq2", 4), ("gk2", 4), ("gv2", 4), ("gwo", 4),
          ("xk1", 4), ("xv1", 4), ("xq1", 4), ("xwo1", 4), ("f1", 46), ("fo1", 11),
          ("sxb", 12), ("sc", 4), ("sz", 8), ("swo", 8),
          ("h0", 22), ("ho0", 11),
          ("pw1", 8), ("pw2", 4), ("h1", 22), ("ho1", 11)]
FIRST = {}
_at = 0
for _name, _n in STAGES:
    FIRST[_name] = _at
    _at += _n
SLABS = _at
assert SLABS % RING == 0

PT = {}
_at = 0
for _name, _n in [("ada_b0", 48), ("ada_b1", 48), ("cw0", 3 * FC), ("cw1", 3 * FC), ("cb0", FC),
                  ("cb1", FC), ("nm0", 8), ("nm1", 8), ("nf0", 8), ("nf1", 8), ("scw", 5 * 32),
                  ("scb", 32), ("snw", 16), ("pb1", 16), ("dww", CONF_K * 8), ("dwb", 8),
                  ("clg", 8), ("clb", 8), ("c", 16)]:
    PT[_name] = slice(_at, _at + _n)
    _at += _n
NPT = _at

ROW = {}
_at = 0
for _name, _n in [("lambda", 256), ("subln", 128), ("dt_bias", 64), ("a_log", 64), ("d_skip", 32)]:
    ROW[_name] = slice(_at, _at + _n)
    _at += _n
NROW = _at
LNROWS = 14
MORE_SEMS = ["in_ctx", "in_wdt", "mod_ready", "n_ready", "abs_ready", "e_ready", "dA_ready",
             "cum_ready", "ean_ready", "cact_ready", "conv_done", "xw_ready", "dec_ready",
             "m_ready", "m_used", "v_ready", "row_used", "out_ready"]


class Ledger:

    def __init__(self, eng, sems):
        self.eng, self.sems = eng, sems
        self.n, self.local, self.per, self.i = {}, {}, None, None

    def now(self, key):
        base = self.n.get(key, 0)
        if self.per is None:
            return base
        step = self.per.get(key, 0)
        here = base + self.local.get(key, 0)
        return here + self.i * step if step else here

    def up(self, key, k=1):
        if self.per is None:
            self.n[key] = self.n.get(key, 0) + k
        else:
            assert key in self.per, f"{key} is not declared for this loop"
            self.local[key] = self.local.get(key, 0) + k
        return self.now(key)

    @contextmanager
    def rounds(self, count, per):
        with self.eng.Fori(0, count) as i:
            self.i, self.per, self.local = i, per, {}
            yield i
            assert self.local == per, (self.local, per)
        self.i, self.per = None, None
        for key, k in per.items():
            self.n[key] = self.n.get(key, 0) + k * count

    def took(self, name, k=1):
        return self.up(("took", name), k)

    def own(self, name):
        return self.up(("own", name))

    def filled(self, b):
        return self.up(("bank", b))

    def freed(self, b):
        return self.up(("freed", b))


def build(nc, slabs, x_in, xT_in, memT_in, ctx_in, pt_in, row_in, ln_in, wdt_in, out):
    with ExitStack() as ctx:
        def sb(name, shape, dt=F32):
            return ctx.enter_context(nc.sbuf_tensor(name, shape, dt))

        SEMS = ["v_step", "a_step", "g_step", "slab_begun", "in_x", "in_xT", "in_mem", "in_pt",
                "in_row", "in_ln", "iota", "consts", "x_ready", "y_ready", "var_ready",
                "rstd_ready", "lam_ready", "exp_ready", "s_ready", "p_ready", "r_ready", "a_ready",
                "pre_ready", "act_ready", "hT_ready", "sc_ready", "stored"] + MORE_SEMS
        S = {name: ctx.enter_context(nc.semaphore(name)) for name in SEMS}
        landed = [ctx.enter_context(nc.semaphore(f"slab_landed{s}")) for s in range(RING)]
        full = {r: [ctx.enter_context(nc.semaphore(f"full_{r}{b}")) for b in range(8)]
                for r in ("act", "dve")}
        free = {r: [ctx.enter_context(nc.semaphore(f"free_{r}{b}")) for b in range(8)]
                for r in ("act", "dve")}

        bank = [ctx.enter_context(nc.psum_tensor(f"bank{b}", [P, 512], F32)) for b in range(8)]

        ring = sb("ring", [P, RING, SLAB])
        x = sb("x", [P, NT, D])
        xt2 = sb("xt2", [P, KC, 2 * T])
        xT = xt2[:, :, T:2 * T]
        sideT = xt2[:, :, 0:T]
        ident = sb("ident", [P, P])
        dist0 = sb("dist0", [P, 2 * T])
        dist = sb("dist", [P, GROUPS, 2 * T])
        tri = sb("tri", [P, 4, NT, T])
        lnrow = sb("lnrow", [P, 2, D])
        pt = sb("pt", [P, NPT])
        row = sb("row", [P, NROW])
        small = sb("small", [P, 640])
        mod = sb("mod", [P, 2, 6, 8, 2])
        arena = sb("arena", [P, 28800])

        def cut(at, *dims):
            n = int(np.prod(dims))
            assert at + n <= 28800, (at, dims)
            v = arena[:, at:at + n]
            if len(dims) == 2:
                return v.rearrange("p (a b) -> p a b", a=dims[0])
            if len(dims) == 3:
                return v.rearrange("p (a b c) -> p a b c", a=dims[0], b=dims[1])
            return v

        st_bn = small[:, 0:24].rearrange("p (t s c) -> p t s c", t=2, s=2)
        st_mv = small[:, 24:28].rearrange("p (t c) -> p t c", t=2)
        st_var = small[:, 28:30]
        st_rstd = small[:, 30:32]
        neg_half = small[:, 32:34]
        nlam = small[:, 34:35]
        lam2 = small[:, 35:39]
        mx = small[:, 40:56]
        nmx = small[:, 56:72]
        sm = small[:, 72:88]
        rs = small[:, 88:104]
        ss16 = small[:, 104:120]
        rs16 = small[:, 120:136]
        half16 = small[:, 136:152]
        sc_in = small[:, 152:168]
        modA = small[:, 168:184]
        lamp = small[:, 184:312]
        dtn = small[:, 312:568].rearrange("p (t h) -> p t h", t=4)
        epsb = small[:, 568:569]

        qT = cut(0, 8, T)
        kT = cut(2048, 8, T)
        vN = cut(4096, NT, D)
        sS = cut(6144, 2, 1024)
        aS = cut(8192, 2, 512)
        aT = cut(9216, 2, 512)
        oN = cut(10240, NT, D)
        oT = cut(12288, 8, T)
        tmpN = cut(14336, NT, D)
        xkT = cut(16384, 8, T)
        xvN = cut(18432, NT, D)
        xP = cut(20480, XH, 512)
        xPT = cut(22528, XH, 512)
        gqT = cut(0, 24, T)
        gkT = cut(6144, 24, T)
        gvN = cut(12288, NT, 3 * D)
        gS = cut(18432, 2, 1536)
        gPT = cut(21504, 2, 1536)
        goN = cut(24576, NT, D)
        goT = cut(26624, 8, T)
        hT = cut(0, FC, T)
        raw = cut(5632, 4, 512)
        pre = cut(7680, 4, T)
        act = cut(8704, 4, T)
        xn = cut(10240, NT, D)

        diff_i = cut(15360, 512).bitcast(I32)
        mask_i = cut(15872, 512).bitcast(I32)

        block = ctx.enter_context(nc.Block())

        xsN = cut(0, 4, DI)
        xs_ctx, xs_lat = xsN[:, 0:2, :], xsN[:, 2:4, :]
        zN = cut(0, NT, DI)
        bN = cut(8192, NT, D)
        xdt = cut(8192, 2, 2, 512)
        bT = cut(10240, SG, T)
        cT = cut(12288, SG, T)
        h0T = cut(14336, SG, 512)
        yT = cut(14336, 16, T)
        craw = cut(18432, 4, 512)
        xw = [cut(18432, NT, DI), cut(22528, NT, DI)]
        yN = cut(18432, NT, DI)
        ctxN = cut(20480, NT, D)
        wdt = cut(22528, KC, 64)
        xn2 = cut(23040, NT, D)
        cpre = cut(23040, 4, 512)
        cact = cut(25088, 4, 512)
        seg = cut(22528, 2, 768)
        mT = cut(24064, 2, 768)
        gT = cut(25600, 2, 768)
        t1 = dist[:, 0, :]
        t2 = dist[:, 1, :]
        dA = cut(27136, 4, 64)
        cumN = cut(27392, 256)
        eN = cut(27648, 256)
        nac = cut(27904, NT, 64)
        acT = cut(28032, 256)
        expA = cut(28288, 64)
        wend = cut(28352, NT, 64)
        tmp = [cut(12288 + 256 * i, 4, 64) for i in range(6)]
        acc = small[:, 570:571]
        squares = dist[:, 0:2, :].rearrange("p a b -> p (a b)")
        uraw = cut(0, 8, 512)
        uT = cut(4096, 2, T)
        vT = cut(6144, KC, T)
        vN2 = cut(8192, NT, D)
        wT = cut(12288, KC, T)
        gate_row, bias_row = lnrow[:, 0, :], lnrow[:, 1, :]

        def mod_col(layer, part, c, s):
            return mod[:, layer, part, c, s:s + 1]

        modA_v = modA.rearrange("p (c s) -> p c s", s=2)

        def modulation(v, L, layer):
            v.wait_ge(full["dve"][4], L.filled(4))
            bias = pt[:, PT[f"ada_b{layer}"]].unsqueeze(2).to_broadcast([P, 48, 2])
            v.tensor_tensor(mod[:, layer, :, :, :].rearrange("p a c s -> p (a c) s"),
                            bank[4][:, 0:96].rearrange("p (a s) -> p a s", s=2), bias,
                            ALU.add).then_inc(free["dve"][4], 1)
            v.wait_ge(free["dve"][4], L.freed(4))

        def more_pool(pool, L, rstd, ln_rows):
            pool.dma_start(ctxN[:, :, :], ctx_in).then_inc(S["in_ctx"], 16)
            pool.dma_start(wdt[:, :, :], wdt_in).then_inc(S["in_wdt"], 16)
            rstd()
            rstd()
            pool.wait_ge(S["x_ready"], L.took("x_ready", NT))

            def bias_load(k):
                pool.dma_start(lnrow[:, 1:2, :], ln_in[:, k:k + 1, :].to_broadcast([P, 1, D])
                               ).then_inc(S["in_ln"], 16)
            bias_load(12)
            for _ in range(5):
                rstd()
                rstd()
            pool.wait_ge(S["row_used"], L.took("row_used"))
            bias_load(13)
            rstd()
            rstd()
            for tt in range(NT):
                rstd()
                pool.wait_ge(S["out_ready"], L.took("out_ready"))
                pool.dma_start(out[:, tt, :], x[:, tt, :]).then_inc(S["stored"], 16)
            pool.wait_ge(S["stored"], 16 * NT)

        def more_vector(v, L, step, network):
            def rms(src, dst, width, ready, tiles=range(NT), junk=None):
                for tt in tiles:
                    step(v.scalar_tensor_tensor(out=squares if junk is None else junk, in0=src[:, tt, :],
                                                scalar=1.0 / width, in1=src[:, tt, :],
                                                op0=ALU.mult, op1=ALU.mult, accum_out=acc))
                    v.tensor_scalar(st_var, acc.to_broadcast([P, 2]), EPS, None, ALU.add) \
                        .then_inc(S["var_ready"], 1)
                    v.wait_ge(S["var_ready"], L.own("var_ready"))
                    v.wait_ge(S["rstd_ready"], L.took("rstd_ready"))
                    v.tensor_scalar(dst[:, tt, :], src[:, tt, :], st_rstd[:, 0:1], None,
                                    ALU.mult).then_inc(S[ready], 1)
                    v.wait_ge(S[ready], L.own(ready))

            def gains(layer, part, name):
                g = pt[:, PT[name]].unsqueeze(2).to_broadcast([P, KC, 2])
                v.scalar_tensor_tensor(out=modA_v, in0=mod[:, layer, part, :, :], scalar=1.0,
                                       in1=g, op0=ALU.add, op1=ALU.mult).then_inc(S["mod_ready"], 1)
                v.wait_ge(S["mod_ready"], L.own("mod_ready"))

            def residual(n, bias=False):
                for b in (4, 5):
                    v.wait_ge(free["act"][b], marks["gate"][n][b])
                if bias:
                    v.wait_ge(S["in_ln"], 16 * 7)
                for tt in range(NT):
                    for h in range(2):
                        b = 2 * tt + h
                        c = slice(h * 512, (h + 1) * 512)
                        v.wait_ge(full["dve"][b], L.filled(b))
                        t = dist[:, h, :]
                        if bias:
                            v.tensor_tensor(t, bank[b][:, :], bias_row[:, c], ALU.add) \
                                .then_inc(free["dve"][b], 1)
                            v.wait_ge(free["dve"][b], L.freed(b))
                            step(v.tensor_tensor(t, t, gate_row[:, c], ALU.mult))
                        else:
                            v.tensor_tensor(t, bank[b][:, :], gate_row[:, c], ALU.mult) \
                                .then_inc(free["dve"][b], 1)
                            v.wait_ge(free["dve"][b], L.freed(b))
                        ins = v.tensor_tensor(x[:, tt, c], x[:, tt, c], t, ALU.add)
                        if bias and b == 3:
                            ins.then_inc(S["row_used"], 1)
                            v.wait_ge(S["row_used"], L.own("row_used"))
                        else:
                            step(ins)

            gains(0, 1, "nm0")
            v.wait_ge(S["in_ctx"], 16)
            rms(ctxN, ctxN, D, "n_ready")
            rms(x, xn2, D, "n_ready")
            v.wait_ge(full["dve"][4], L.filled(4))
            u, m, z, z2, s, e = tmp
            v.tensor_tensor(u, bank[4][:, 0:256].rearrange("p (t h) -> p t h", t=4),
                            row[:, ROW["dt_bias"]].unsqueeze(1).to_broadcast([P, 4, 64]),
                            ALU.add).then_inc(free["dve"][4], 1)
            v.wait_ge(free["dve"][4], L.freed(4))
            step(v.tensor_scalar(m, u, 0.0, None, ALU.max))
            step(v.tensor_scalar(s, u, -1.0, None, ALU.mult))
            v.tensor_tensor(s, s, u, ALU.max).then_inc(S["abs_ready"], 1)
            v.wait_ge(S["abs_ready"], L.own("abs_ready"))
            v.wait_ge(S["e_ready"], L.took("e_ready"))
            step(v.tensor_scalar(z2, e, 2.0, None, ALU.add))
            step(v.reciprocal(z2, z2))
            step(v.tensor_tensor(z, e, z2, ALU.mult))
            step(v.tensor_tensor(z2, z, z, ALU.mult))
            step(v.tensor_scalar(s, z2, 1.0 / 17, None, ALU.mult))
            for k in (15, 13, 11, 9, 7, 5, 3):
                step(v.scalar_tensor_tensor(out=s, in0=s, scalar=1.0 / k, in1=z2, op0=ALU.add,
                                            op1=ALU.mult))
            step(v.scalar_tensor_tensor(out=s, in0=s, scalar=1.0, in1=z, op0=ALU.add, op1=ALU.mult))
            step(v.scalar_tensor_tensor(out=dtn, in0=s, scalar=2.0, in1=m, op0=ALU.mult, op1=ALU.add))
            v.scalar_tensor_tensor(out=dA, in0=dtn, scalar=-1.0,
                                   in1=expA.unsqueeze(1).to_broadcast([P, 4, 64]),
                                   op0=ALU.mult, op1=ALU.mult).then_inc(S["dA_ready"], 1)
            v.wait_ge(S["dA_ready"], L.own("dA_ready"))

            def taps(dst, src, n, w, b):
                d3 = dst.rearrange("p (n t) -> p n t", n=n)
                s3 = src.rearrange("p (n t) -> p n t", n=n)
                step(v.tensor_scalar(dst, src, w(2), b, ALU.mult, ALU.add))
                for k in (0, 1, 3, 4):
                    o = k - 2
                    lo, hi = max(0, -o), T - max(0, o)
                    ins = v.scalar_tensor_tensor(out=d3[:, :, lo:hi], in0=s3[:, :, lo + o:hi + o],
                                                 scalar=w(k), in1=d3[:, :, lo:hi], op0=ALU.mult,
                                                 op1=ALU.add)
                    if k < 4:
                        step(ins)
                return ins

            def wcol(j):
                scw, scb = PT["scw"].start, PT["scb"].start
                return (lambda k: pt[:, scw + k * 32 + j:scw + k * 32 + j + 1]), \
                    pt[:, scb + j:scb + j + 1]

            for j in range(24):
                if j == 1:
                    v.wait_ge(full["dve"][5], L.filled(5))
                    v.tensor_copy(cumN, bank[5][:, 0:256]).then_inc(free["dve"][5], 1)
                    v.wait_ge(free["dve"][5], L.freed(5))
                    v.tensor_scalar(nac, cumN[:, 0:128].rearrange("p (t h) -> p t h", t=NT),
                                    -1.0, None, ALU.mult).then_inc(S["cum_ready"], 1)
                    v.wait_ge(S["cum_ready"], L.own("cum_ready"))
                    v.wait_ge(full["dve"][6], L.filled(6))
                    v.tensor_copy(acT[0:64, :], bank[6][0:64, 0:T]).then_inc(free["dve"][6], 1)
                    v.wait_ge(free["dve"][6], L.freed(6))
                    v.wait_ge(S["ean_ready"], L.took("ean_ready"))
                    step(v.tensor_tensor(wend, dtn[:, 0:2, :],
                                         eN[:, 128:256].rearrange("p (t h) -> p t h", t=NT),
                                         ALU.mult))
                v.wait_ge(free["act"][j % 4], marks["conv"][j % 4] + j // 4 + 1)
                w, b = wcol(j)
                taps(cpre[:, j % 4, :], craw[:, j % 4, :], 2, w, b).then_inc(S["pre_ready"], 1)
                v.wait_ge(S["pre_ready"], L.own("pre_ready"))
            for j in range(4):
                v.wait_ge(free["act"][j], marks["conv"][j] + 6 + 1)
                for c in range(2):
                    w, b = wcol(24 + 2 * j + c)
                    part = slice(c * T, (c + 1) * T)
                    ins = taps(cpre[:, j, part], craw[:, j, part], 1, w, b)
                    if c == 0:
                        step(ins)
                    else:
                        ins.then_inc(S["pre_ready"], 1)
                        v.wait_ge(S["pre_ready"], L.own("pre_ready"))
            step(v.tensor_scalar(tri[:, 0:2, :, :], tri[:, 0:2, :, :], 1.0, NEG, ALU.subtract,
                                 ALU.mult))
            for b in range(4, 8):
                v.wait_ge(free["act"][b], marks["xs"][b])
            v.wait_ge(S["conv_done"], L.took("conv_done"))
            for d in range(2):
                for tt in range(NT):
                    wv = wend[:, tt, 32 * d:32 * d + 32].unsqueeze(2).to_broadcast([P, 32, 64])
                    v.tensor_tensor(xw[d][:, tt, :].rearrange("p (h e) -> p h e", e=64),
                                    xs_ctx[:, tt, :].rearrange("p (h e) -> p h e", e=64),
                                    wv, ALU.mult).then_inc(S["xw_ready"], 1)
                    v.wait_ge(S["xw_ready"], L.own("xw_ready"))

            def heads4(ap):
                return ap.rearrange("p t (h e) -> p t h e", h=4)

            def combine(g):
                c4 = slice(g * 256, (g + 1) * 256)
                y = yN[:, :, c4]
                ea = eN[:, 0:128].rearrange("p (t h) -> p t h", t=NT)
                for d, t in ((0, t1), (1, t2)):
                    b = 5 + d
                    v.wait_ge(full["dve"][b], L.filled(b))
                    w = ea[:, :, 32 * d + 4 * g:32 * d + 4 * g + 4].unsqueeze(3) \
                        .to_broadcast([P, NT, 4, 64])
                    v.tensor_tensor(
                t.rearrange("p (t h e) -> p t h e", t=NT, h=4),
                bank[b][:, :].rearrange("p (t h e) -> p t h e", t=NT, h=4), w,
                ALU.mult).then_inc(free["dve"][b], 1)
                    v.wait_ge(free["dve"][b], L.freed(b))
                step(v.tensor_tensor(t1, t1, t2, ALU.add))
                v.wait_ge(full["dve"][4], L.filled(4))
                v.tensor_tensor(y, bank[4][:, :].rearrange("p (t c) -> p t c", t=NT),
                                t1.rearrange("p (t c) -> p t c", t=NT), ALU.add) \
                                    .then_inc(free["dve"][4], 1)
                v.wait_ge(free["dve"][4], L.freed(4))
                w = row[:, ROW["d_skip"]][:, 4 * g:4 * g + 4].unsqueeze(1).unsqueeze(3) \
                    .to_broadcast([P, NT, 4, 64])
                step(v.tensor_tensor(t2.rearrange("p (t h e) -> p t h e", t=NT, h=4),
                                     heads4(xs_lat[:, :, c4]), w, ALU.mult))
                step(v.tensor_tensor(y, y, t2.rearrange("p (t c) -> p t c", t=NT), ALU.add))

            blocks = [(0, 0, 0, T, 0), (0, 1, P, T, 256), (1, 0, 0, P, 384), (1, 1, 0, T, 512)]
            for q in range(SH + 2):
                g, j = q // 4, q % 4
                if q < SH:
                    b = q % 2
                    v.wait_ge(full["dve"][b], L.filled(b))
                    for n, (d, st, lo, hi, at) in enumerate(blocks):
                        ins = v.scalar_tensor_tensor(
                            out=seg[:, q % 2, at:at + hi - lo],
                            in0=bank[b][:, d * T + lo:d * T + hi],
                            scalar=nac[:, st, 32 * d + q:32 * d + q + 1],
                            in1=tri[:, d, st, lo:hi], op0=ALU.add, op1=ALU.min)
                        if n < 3:
                            step(ins)
                        else:
                            ins.then_inc(free["dve"][b], 1)
                            v.wait_ge(free["dve"][b], L.freed(b))
                    if j == 0:
                        for d in range(2):
                            w = dtn[:, 2:4, 32 * d + q:32 * d + q + 4].unsqueeze(3) \
                                .to_broadcast([P, NT, 4, 64])
                            step(v.tensor_tensor(
                                xdt[:, g % 2, d, :].rearrange("p (t h e) -> p t h e", t=NT, h=4),
                                heads4(xs_lat[:, :, g * 256:(g + 1) * 256]), w, ALU.mult))
                if 1 <= q <= SH:
                    k = q - 1
                    v.wait_ge(S["dec_ready"], L.took("dec_ready"))
                    if k == SH - 1:
                        v.wait_ge(S["m_used"], L.took("m_used"))
                    v.wait_ge(free["act"][2], marks["heads_act"][2] + k // 4 + 1)
                    v.tensor_tensor(mT[:, k % 2, :], seg[:, k % 2, :],
                                    gT[:, (k // 4) % 2, :], ALU.mult).then_inc(S["m_ready"], 1)
                    v.wait_ge(S["m_ready"], L.own("m_ready"))
                if q % 4 == 1 and q > 1:
                    combine(g - 1)
            v.wait_ge(free["act"][3], marks["z"][3])
            for tt in range(NT):
                step(v.tensor_tensor(yN[:, tt, :], yN[:, tt, :], zN[:, tt, :], ALU.mult))
                rms(yN, yN, DI, "n_ready", [tt], zN[:, tt, :])
            residual(0)
            gains(0, 4, "nf0")
            rms(x, xn, D, "n_ready")
            network("h0")
            residual(1)
            gains(1, 1, "nm1")
            rms(x, xn, D, "n_ready")
            dww, dwb = PT["dww"].start, PT["dwb"].start
            for j in range(KC):
                v.wait_ge(free["act"][j % 4], marks["pw1"][j % 4] + j // 4 + 1)
                u2 = uT[:, j % 2, :]
                step(v.tensor_tensor(u2, uraw[:, j, 0:T], uraw[:, j, T:2 * T], ALU.mult))
                vv = vT[:, j, :]
                wk = lambda k: pt[:, dww + k * KC + j:dww + k * KC + j + 1]
                mid = CONF_K // 2
                step(v.tensor_scalar(vv, u2, wk(mid), pt[:, dwb + j:dwb + j + 1], ALU.mult, ALU.add))
                reach = mid if j < HC else ROWS - 1
                span = [o for o in range(-reach, reach + 1) if o]
                for o in span:
                    if j < HC:
                        a3 = lambda t: t.rearrange("p (r w) -> p r w", r=ROWS)
                        lo, hi = max(0, -o), GRID_W - max(0, o)
                        dst, src = a3(vv)[:, :, lo:hi], a3(u2)[:, :, lo + o:hi + o]
                    else:
                        lo, hi = max(0, -o) * GRID_W, T - max(0, o) * GRID_W
                        dst, src = vv[:, lo:hi], u2[:, lo + o * GRID_W:hi + o * GRID_W]
                    ins = v.scalar_tensor_tensor(out=dst, in0=src, scalar=wk(mid + o), in1=dst,
                                                 op0=ALU.mult, op1=ALU.add)
                    if o == span[-1]:
                        ins.then_inc(S["v_ready"], 1)
                        v.wait_ge(S["v_ready"], L.own("v_ready"))
                    else:
                        step(ins)
            for tt in range(NT):
                for b in (4 + 2 * tt, 5 + 2 * tt):
                    v.wait_ge(free["act"][b], marks["vN"][b])
                for h in range(2):
                    step(v.bn_stats(st_bn[:, tt, h, :], vN2[:, tt, h * 512:(h + 1) * 512]))
                step(v.bn_aggr(st_mv[:, tt, :], st_bn[:, tt, :, :]))
                v.tensor_scalar(st_var, st_mv[:, tt, 1:2].to_broadcast([P, 2]), EPS, None,
                                ALU.add).then_inc(S["var_ready"], 1)
                v.wait_ge(S["var_ready"], L.own("var_ready"))
                v.wait_ge(S["rstd_ready"], L.took("rstd_ready"))
                v.tensor_scalar(vN2[:, tt, :], vN2[:, tt, :], st_mv[:, tt, 0:1],
                                st_rstd[:, 0:1], ALU.subtract, ALU.mult).then_inc(S["n_ready"], 1)
                v.wait_ge(S["n_ready"], L.own("n_ready"))
            residual(2, bias=True)
            gains(1, 4, "nf1")
            rms(x, xn, D, "n_ready")
            network("h1")
            residual(3)
            v.wait_ge(S["in_ln"], 16 * 8)
            for tt in range(NT):
                rms(x, xn, D, "v_step", [tt])
                v.tensor_tensor(x[:, tt, :], xn[:, tt, :], bias_row, ALU.mult) \
                    .then_inc(S["out_ready"], 1)
                v.wait_ge(S["out_ready"], L.own("out_ready"))

        def more_scalar(a, L, copy_out, proj_T, proj_N, x_to_T, network):
            def mod_out(dst, scale, bias, chunks=KC, func=ACT.Identity):
                for at in range(0, chunks, 8):
                    for q in range(4):
                        a.wait_ge(full["act"][4 + q], L.filled(4 + q))
                        for c in range(2):
                            k = at + 2 * q + c
                            ins = a.activation(dst[:, k, :], bank[4 + q][:, c * T:(c + 1) * T],
                                               func, scale=scale(k),
                                               **({"bias": bias(k)} if bias else {}))
                            if c:
                                ins.then_inc(free["act"][4 + q], 1)
                                L.freed(4 + q)
                            else:
                                ins.then_inc(S["a_step"], 1)

            def modulated(dst, layer, part, s):
                mod_out(dst, lambda k: modA_v[:, k, s:s + 1],
                        lambda k: mod_col(layer, part, k, s))

            def gate_out():
                for h in range(2):
                    copy_out(4 + h, gate_row[:, h * 512:(h + 1) * 512])

            a.wait_ge(S["mod_ready"], L.took("mod_ready"))
            modulated(sideT, 0, 0, 0)
            modulated(xT, 0, 0, 1)
            a.activation(expA, row[:, ROW["a_log"]], ACT.Exp).then_inc(S["a_step"], 1)
            a.wait_ge(S["abs_ready"], L.took("abs_ready"))
            a.activation(tmp[5], tmp[4], ACT.Exp, scale=-1.0).then_inc(S["e_ready"], 1)
            for j in range(24 + 2):
                if j < 24:
                    copy_out(j % 4, craw[:, j % 4, :])
                if j == 1:
                    a.wait_ge(S["cum_ready"], L.took("cum_ready"))
                    a.activation(eN, cumN, ACT.Exp).then_inc(S["ean_ready"], 1)
                if j >= 2:
                    k = j - 2
                    b = 4 + k % 4
                    if k < 16:
                        copy_out(b, xsN[:, :, k * P:(k + 1) * P],
                                 bank[b][:, :].rearrange("p (n c) -> p n c", n=4))
                    else:
                        copy_out(b, bN[:, :, (k - 16) * P:(k - 15) * P],
                                 bank[b][:, 0:256].rearrange("p (n c) -> p n c", n=2))
                if j < 24:
                    a.wait_ge(S["pre_ready"], L.took("pre_ready"))
                    if j < 16:
                        a.activation(cact[:, j % 4, :], cpre[:, j % 4, :], ACT.Silu) \
                            .then_inc(S["cact_ready"], 1)
                    else:
                        a.activation(bT[:, j - 16, :], cpre[:, j % 4, T:2 * T], ACT.Silu) \
                            .then_inc(S["a_step"], 1)
                        a.activation(cact[:, j % 4, 0:T], cpre[:, j % 4, 0:T], ACT.Silu) \
                            .then_inc(S["cact_ready"], 1)
            for j in range(4):
                copy_out(j, craw[:, j, :])
                a.wait_ge(S["pre_ready"], L.took("pre_ready"))
                a.activation(cT[:, 2 * j:2 * j + 2, :], cpre[:, j, :].rearrange(
             "p (c t) -> p c t", c=2), ACT.Silu).then_inc(S["conv_done" if j == 3 else "a_step"], 1)
            for g in range(SG):
                copy_out(4 + g % 4, h0T[:, g, :])
            for q in range(SH):
                g = q // 4
                a.wait_ge(free["dve"][q % 2], marks["heads2"][q % 2] + q // 2 + 1)
                a.activation(seg[:, q % 2, :], seg[:, q % 2, :], ACT.Exp) \
                    .then_inc(S["dec_ready"], 1)
                if q % 4 == 0:
                    a.wait_ge(full["act"][2], L.filled(2))
                    for n, (lo, hi, at) in enumerate([(0, 256, 0), (384, 512, 256), (0, 128, 384),
                                                      (256, 512, 512)]):
                        ins = a.activation(gT[:, g % 2, at:at + hi - lo], bank[2][:, lo:hi],
                                           ACT.Copy)
                        if n == 3:
                            ins.then_inc(free["act"][2], 1)
                            L.freed(2)
                        else:
                            ins.then_inc(S["a_step"], 1)
                if q % 4 == 1:
                    a.wait_ge(full["act"][3], L.filled(3))
                    a.activation(zN[:, :, g * 256:(g + 1) * 256],
                                 bank[3][:, :].rearrange("p (t c) -> p t c", t=NT),
                                 ACT.Silu).then_inc(free["act"][3], 1)
                    L.freed(3)
            snw = PT["snw"].start
            gate_out()
            mod_out(yT, lambda k: pt[:, snw + k:snw + k + 1], None, 16)
            a.wait_ge(S["mod_ready"], L.took("mod_ready"))
            modulated(xT, 0, 3, 1)
            gate_out()
            network(ACT.Silu, False)
            a.wait_ge(S["mod_ready"], L.took("mod_ready"))
            modulated(xT, 1, 0, 1)
            gate_out()
            pb1 = PT["pb1"].start
            for j in range(KC):
                a.wait_ge(full["act"][j % 4], L.filled(j % 4))
                a.activation(uraw[:, j, 0:T], bank[j % 4][:, 0:T], ACT.Identity,
                             bias=pt[:, pb1 + j:pb1 + j + 1]).then_inc(S["a_step"], 1)
                a.activation(uraw[:, j, T:2 * T], bank[j % 4][:, T:2 * T], ACT.Sigmoid,
                             bias=pt[:, pb1 + 8 + j:pb1 + 9 + j]).then_inc(free["act"][j % 4], 1)
                L.freed(j % 4)
            clg, clb = PT["clg"].start, PT["clb"].start
            for tt in range(NT):
                for q in range(2):
                    b = 4 + 2 * tt + q
                    copy_out(b, vN2[:, tt, q * 512:(q + 1) * 512])
            mod_out(wT, lambda k: pt[:, clg + k:clg + k + 1], lambda k: pt[:, clb + k:clb + k + 1],
                    func=ACT.Silu)
            a.wait_ge(S["mod_ready"], L.took("mod_ready"))
            modulated(xT, 1, 3, 1)
            gate_out()
            network(ACT.Silu, False)

        def more_tensor(pe, L, free_of, frees, fill, slab, begun, col_T, col_N, rows, tokens_to_T,
                        project, for_rounds, mark):
            def to_T(src, chunks=KC):
                for at in range(0, chunks, 8):
                    for b_ in (4, 5, 6, 7):
                        pe.wait_ge(free_of(b_), frees(b_))
                    for tt in range(NT):
                        if at == 0:
                            pe.wait_ge(S["n_ready"], L.took("n_ready"))
                        for q in range(4):
                            for c in range(2):
                                k = at + 2 * q + c
                                ins = pe.transpose(
                                    bank[4 + q][:, c * T + tt * P:c * T + (tt + 1) * P],
                                    src[:, tt, k * P:(k + 1) * P], ident[:, :])
                            if tt:
                                fill(ins, 4 + q, "act")
                for b_ in (4, 5, 6, 7):
                    pe.wait_ge(free_of(b_), frees(b_))

            def gate(layer, part):
                for b_ in (4, 5):
                    pe.wait_ge(free_of(b_), frees(b_))
                for c in range(KC):
                    b = 4 + c // 4
                    ins = pe.matmul(bank[b][:, (c % 4) * P:(c % 4 + 1) * P],
                                    mod_col(layer, part, c, 1).to_broadcast([P, P]), ident[:, :],
                                    start=True, stop=True)
                    if c % 4 == 3:
                        fill(ins, b, "act")
                marks.setdefault("gate", []).append(mark("act"))

            def network(stage):
                for_rounds("act")
                marks[stage] = mark("act")
                with L.rounds(5, {("act", q): 1 for q in range(4)}) as i:
                    for u in range(4):
                        col_T(stage, u, u, "act", xT, i)
                for u in range(2):
                    col_T(stage, u, u, "act", xT, 5)
                pe.wait_ge(S["hT_ready"], L.took("hT_ready", FC))

            to_T(ctxN)
            to_T(xn2)
            pe.wait_ge(S["in_wdt"], 16)
            for s, src in enumerate((sideT, xT)):
                for tt in range(NT):
                    at = (2 * s + tt) * 64
                    for k in range(KC):
                        ins = pe.matmul(bank[4][:, at:at + 64], src[:, k, tt * P:(tt + 1) * P],
                                        wdt[:, k, :], start=(k == 0), stop=(k == KC - 1))
            fill(ins, 4, "dve")
            marks["conv"] = mark("act")
            for j in range(24 + 2):
                if j < 24:
                    if j % 2 == 0:
                        w = slab("sxb", j // 2).rearrange("p (k c) -> p k c", k=KC)
                    pe.wait_ge(free_of(j % 4), frees(j % 4))
                    for k in range(KC):
                        ins = pe.matmul(bank[j % 4][:, :],
                                        w[:, k, (j % 2) * P:(j % 2 + 1) * P],
                                        xt2[:, k, :], start=(k == 0), stop=(k == KC - 1))
                        begun(ins, j % 2 == 0 and k == 0)
                    fill(ins, j % 4, "act")
                if j == 2:
                    pe.wait_ge(S["dA_ready"], L.took("dA_ready"))
                    for b_ in (5, 6):
                        pe.wait_ge(free_of(b_), frees(b_))
                    for n, (stream, masks) in enumerate([(2, (0, 1)), (0, (3, 2))]):
                        for tt in range(NT):
                            for d, mk in enumerate(masks):
                                at = n * 128 + tt * 64 + 32 * d
                                for st in range(NT):
                                    ins = pe.matmul(bank[5][:, at:at + 32],
                                                    tri[:, mk, st, tt * P:(tt + 1) * P],
                                                    dA[:, stream + st, 32 * d:32 * d + 32],
                                                    start=(st == 0), stop=(st == NT - 1))
                    fill(ins, 5, "dve")
                    for d in range(2):
                        for st in range(NT):
                            ins = pe.matmul(bank[6][32 * d:32 * d + 32, 0:T],
                                            dA[:, 2 + st, 32 * d:32 * d + 32], tri[:, d, st, :],
                                            start=(st == 0), stop=(st == NT - 1))
                    fill(ins, 6, "dve")
                if j >= 2:
                    k = j - 2
                    b = 4 + k % 4
                    pe.wait_ge(S["cact_ready"], L.took("cact_ready"))
                    pe.wait_ge(free_of(b), frees(b))
                    for n in range(4 if k < 16 else 2):
                        ins = pe.transpose(bank[b][:, n * P:(n + 1) * P],
                                           cact[:, k % 4, n * P:(n + 1) * P], ident[:, :])
                    fill(ins, b, "act")
            marks["xs"] = mark("act")
            project("T", "sc", xT)
            pe.wait_ge(S["xw_ready"], L.took("xw_ready", 4))
            for g in range(SG):
                b = 4 + g % 4
                pe.wait_ge(free_of(b), frees(b))
                for d in range(2):
                    for st in range(NT):
                        ins = pe.matmul(bank[b][:, d * 256:(d + 1) * 256],
                                        bN[:, st, g * P:(g + 1) * P],
                                        xw[d][:, st, g * 256:(g + 1) * 256],
                                        start=(st == 0), stop=(st == NT - 1))
                fill(ins, b, "act")
            for b_ in (0, 1, 2, 3, 4, 5, 6, 7):
                pe.wait_ge(free_of(b_), frees(b_))
            marks["heads2"], marks["heads_act"] = mark("dve"), mark("act")
            for q in range(SH + 2):
                g, j = q // 4, q % 4
                if q < SH:
                    b = q % 2
                    pe.wait_ge(free_of(b), frees(b))
                    for d in range(2):
                        r = 32 * d + q
                        ins = pe.matmul(bank[b][:, d * T:(d + 1) * T],
                                        ident[0:64, r:r + 1].to_broadcast([64, P]), acT[0:64, :],
                                        start=True, stop=True)
                    fill(ins, b, "dve")
                    if j == 0:
                        pe.wait_ge(free_of(2), frees(2))
                        for st in range(NT):
                            ins = pe.matmul(bank[2][:, st * T:(st + 1) * T],
                                            bT[:, g, st * P:(st + 1) * P], cT[:, g, :],
                                            start=True, stop=True)
                        fill(ins, 2, "act")
                    if j == 1:
                        col_N("sz", g, 3, "act", xT)
                if q >= 2:
                    k = q - 2
                    h, p = k % 4, k % 2
                    pe.wait_ge(S["m_ready"], L.took("m_ready"))
                    if h == 0:
                        pe.wait_ge(free_of(4), frees(4))
                    m = mT[:, p, :]
                    for tt, parts in enumerate([[(0, 0, 0), (1, 0, 384), (1, 1, 512)],
                                                [(0, 0, 128), (0, 1, 256), (1, 1, 640)]]):
                        for n, (d, st, at) in enumerate(parts):
                            xa = st * 256 + h * 64
                            ins = pe.matmul(bank[4][:, tt * 256 + h * 64:tt * 256 + (h + 1) * 64],
                                            m[:, at:at + P], xdt[:, (k // 4) % 2, d, xa:xa + 64],
                                            start=(n == 0), stop=(n == 2))
                    if h == 3:
                        fill(ins, 4, "dve")
                    elif k == SH - 3:
                        ins.then_inc(S["m_used"], 1)
                    if h == 0:
                        for d in range(2):
                            pe.wait_ge(free_of(5 + d), frees(5 + d))
                            for tt in range(NT):
                                ins = pe.matmul(bank[5 + d][:, tt * 256:(tt + 1) * 256],
                                                cT[:, k // 4, tt * P:(tt + 1) * P],
                                                h0T[:, k // 4, d * 256:(d + 1) * 256],
                                                start=True, stop=True)
                            fill(ins, 5 + d, "dve")
            marks["z"] = mark("act")
            gate(0, 2)
            to_T(yN, 16)
            rows("swo", 8, yT)
            to_T(xn)
            gate(0, 5)
            network("h0")
            rows("ho0", 11, hT)
            to_T(xn)
            gate(1, 2)
            marks["pw1"] = mark("act")
            for j in range(KC):
                col_T("pw1", j, j % 4, "act", xT)
            for k in range(KC):
                pe.wait_ge(S["v_ready"], L.took("v_ready"))
                for tt in range(NT):
                    b = 4 + 2 * tt + k // 4
                    if k % 4 == 0:
                        pe.wait_ge(free_of(b), frees(b))
                    ins = pe.transpose(bank[b][:, (k % 4) * P:(k % 4 + 1) * P],
                                       vT[:, k, tt * P:(tt + 1) * P], ident[:, :])
                    if k % 4 == 3:
                        fill(ins, b, "act")
            marks["vN"] = mark("act")
            to_T(vN2)
            rows("pw2", 4, wT)
            to_T(xn)
            gate(1, 5)
            network("h1")
            rows("ho1", 11, hT)

        marks = {}

        @block.sync
        def _(sp):
            for s in range(RING):
                sp.dma_start(ring[:, s, :], slabs[s]).then_inc(landed[s], 16)
            with sp.Fori(1, SLABS // RING) as i:
                for s in range(RING):
                    sp.wait_ge(S["slab_begun"], i * RING + (s + 2 - RING))
                    sp.dma_start(ring[:, s, :], slabs[i * RING + s]).then_inc(landed[s], 16)

        @block.tensor
        def _(pe):
            L = Ledger(pe, S)
            last = {}

            def free_of(b):
                return free[last.get(b, "act")][b]

            def frees(b):
                return L.now((last.get(b, "act"), b))

            def fill(ins, b, first, then=None):
                ins.then_inc(full[first][b], 1)
                last[b] = then or first
                L.up((last[b], b))

            def for_rounds(reader):
                for b in range(4):
                    pe.wait_ge(free_of(b), frees(b))
                    last[b] = reader

            def slab(stage, u, i=0):
                g = FIRST[stage] + u
                pe.wait_ge(landed[g % RING], 16 * (g // RING + 1) + i * 16)
                return ring[:, g % RING, :]

            def begun(ins, first):
                if first:
                    ins.then_inc(S["slab_begun"], 1)

            def col_T(stage, u, b, reader, src, i=0):
                w = slab(stage, u, i).rearrange("p (k c) -> p k c", k=KC)
                pe.wait_ge(free_of(b), frees(b))
                for ch in range(2):
                    for k in range(KC):
                        ins = pe.matmul(bank[b][:, ch * T:(ch + 1) * T],
                                        w[:, k, ch * P:(ch + 1) * P], src[:, k, :],
                                        start=(k == 0), stop=(k == KC - 1))
                        begun(ins, ch == 0 and k == 0)
                fill(ins, b, reader)

            def col_N(stage, u, b, reader, src, i=0):
                w = slab(stage, u, i).rearrange("p (k c) -> p k c", k=KC)
                pe.wait_ge(free_of(b), frees(b))
                for tt in range(NT):
                    for k in range(KC):
                        ins = pe.matmul(bank[b][:, tt * 256:(tt + 1) * 256],
                                        src[:, k, tt * P:(tt + 1) * P], w[:, k, :],
                                        start=(k == 0), stop=(k == KC - 1))
                        begun(ins, tt == 0 and k == 0)
                fill(ins, b, reader)

            def rows(stage, n, src):
                for b_ in (0, 1, 2, 3):
                    pe.wait_ge(free_of(b_), frees(b_))
                for j in range(n):
                    w = slab(stage, j).rearrange("p (k c) -> p k c", k=2)
                    for k in range(2):
                        for tt in range(NT):
                            for h in range(2):
                                ins = pe.matmul(bank[2 * tt + h][:, :],
                                                src[:, 2 * j + k, tt * P:(tt + 1) * P],
                                                w[:, k, h * 512:(h + 1) * 512],
                                                start=(j == 0 and k == 0),
                                                stop=(j == n - 1 and k == 1))
                                begun(ins, k == 0 and tt == 0 and h == 0)
                                if j == n - 1 and k == 1:
                                    fill(ins, 2 * tt + h, "dve")

            def tokens_to_T(src, ready):
                for tt in range(NT):
                    if ready and (ready == "x_ready" or tt == 0):
                        pe.wait_ge(S[ready], L.took(ready))
                    for q in range(2):
                        b = 4 + 2 * tt + q
                        pe.wait_ge(free_of(b), frees(b))
                        for k in range(4):
                            c = 4 * q + k
                            ins = pe.transpose(bank[b][:, k * P:(k + 1) * P],
                                               src[:, tt, c * P:(c + 1) * P], ident[:, :])
                        fill(ins, b, "act")
                for b_ in (4, 5, 6, 7):
                    pe.wait_ge(free_of(b_), frees(b_))

            def project(kind, stage, src):
                for u in range(4):
                    (col_T if kind == "T" else col_N)(stage, u, u, "act", src)

            def cross(layer):
                project("T", f"xk{layer}", sideT)
                project("N", f"xv{layer}", sideT)
                project("T", f"xq{layer}", xT)
                for b_ in (0, 1, 2, 3):
                    pe.wait_ge(free_of(b_), frees(b_))
                for h in range(XH):
                    b = 4 + h
                    pe.wait_ge(free_of(b), frees(b))
                    for tt in range(NT):
                        for c in range(2):
                            ins = pe.matmul(bank[b][:, tt * T:(tt + 1) * T],
                                            qT[:, 2 * h + c, tt * P:(tt + 1) * P],
                                            xkT[:, 2 * h + c, :], start=(c == 0), stop=(c == 1))
                    ins.then_inc(full["dve"][b], 1)
                for h in range(XH):
                    pe.wait_ge(S["a_ready"], L.took("a_ready"))
                    for mt in range(NT):
                        for tt in range(NT):
                            ins = pe.transpose(bank[h][:, mt * T + tt * P:mt * T + (tt + 1) * P],
                                               xP[:, h, tt * T + mt * P:tt * T + (mt + 1) * P],
                                               ident[:, :])
                    fill(ins, h, "act")
                for h in range(XH):
                    pe.wait_ge(free_of(h), frees(h))
                    for e in range(2):
                        for mt in range(NT):
                            c = h * 256 + e * P
                            ins = pe.matmul(bank[4 + h][:, e * T:(e + 1) * T],
                                            xvN[:, mt, c:c + P], xPT[:, h, mt * T:(mt + 1) * T],
                                            start=(mt == 0), stop=(mt == NT - 1))
                    fill(ins, 4 + h, "act")
                for b_ in (4, 5, 6, 7):
                    pe.wait_ge(free_of(b_), frees(b_))
                rows(f"xwo{layer}", 4, oT)
                tokens_to_T(x, "x_ready")

            def ada(stage, u, j, b, i=0):
                w = slab(stage, u, i).rearrange("p (k c) -> p k c", k=KC)
                sc = sc_in.rearrange("p (k s) -> p k s", k=KC)
                for ch in range(2):
                    at = 2 * (2 * j + ch)
                    dst = bank[b][:, at:at + 2] if isinstance(j, int) \
                        else bank[b][:, 0:96][:, bass.ds(at, 2)]
                    for k in range(KC):
                        ins = pe.matmul(dst, w[:, k, ch * P:(ch + 1) * P], sc[:, k, :],
                                        start=(k == 0), stop=(k == KC - 1))
                        begun(ins, ch == 0 and k == 0)
                return ins

            def network(layer, src):
                stage, b = f"f{layer}", 4
                if layer == 0:
                    pe.wait_ge(S["sc_ready"], L.took("sc_ready"))
                pe.wait_ge(free_of(b), frees(b))
                for_rounds("act")
                marks[stage] = {q: L.now(("act", q)) for q in range(8)}
                with L.rounds(5, {("act", q): 1 for q in range(4)}) as i:
                    for u in range(4):
                        col_T(stage, 2 * u, u, "act", src, 2 * i)
                        ada(stage, 2 * u + 1, i * 4 + u, b, 2 * i)
                for u in range(2):
                    col_T(stage, 2 * u, u, "act", src, 10)
                    ada(stage, 2 * u + 1, 20 + u, b, 10)
                ada(stage, 4, 22, b, 10)
                fill(ada(stage, 5, 23, b, 10), b, "dve")
                pe.wait_ge(S["hT_ready"], L.took("hT_ready", FC))
                rows(f"fo{layer}", 11, hT)

            pe.wait_ge(S["consts"], L.took("consts"))
            pe.wait_ge(S["in_xT"], 16)
            pe.wait_ge(S["in_mem"], 16)
            project("T", "dq", xT)
            project("T", "dk", xT)
            project("N", "dv", xT)
            for b_ in (0, 1, 2, 3):
                pe.wait_ge(free_of(b_), frees(b_))
            for h in range(DIFF_HEADS + 2):
                if h < DIFF_HEADS:
                    for c in range(2):
                        b = 4 + 2 * (h % 2) + c
                        pe.wait_ge(free_of(b), frees(b))
                        part = slice(c * HEAD, (c + 1) * HEAD)
                        for tt in range(NT):
                            ins = pe.matmul(bank[b][:, tt * T:(tt + 1) * T],
                                            qT[part, h, tt * P:(tt + 1) * P], kT[part, h, :],
                                            start=True, stop=True)
                        fill(ins, b, "dve")
                if h >= 2:
                    g = h - 2
                    b = 2 + g % 2
                    for b_ in (g % 2, b):
                        pe.wait_ge(free_of(b_), frees(b_))
                    for tt in range(NT):
                        for kt in range(NT):
                            ins = pe.matmul(bank[b][:, tt * P:(tt + 1) * P],
                                            aT[:, g % 2, kt * T + tt * P:kt * T + (tt + 1) * P],
                                            vN[:, kt, g * P:(g + 1) * P],
                                            start=(kt == 0), stop=(kt == NT - 1))
                    fill(ins, b, "act")
                if 0 <= h - 1 < DIFF_HEADS:
                    g = h - 1
                    pe.wait_ge(S["a_ready"], L.took("a_ready"))
                    pe.wait_ge(free_of(g % 2), frees(g % 2))
                    for kt in range(NT):
                        for tt in range(NT):
                            ins = pe.transpose(bank[g % 2][:, kt * T + tt * P:kt * T + (tt + 1) * P],
                                               aS[:, g % 2, tt * T + kt * P:tt * T + (kt + 1) * P],
                                               ident[:, :])
                    fill(ins, g % 2, "act")
            marks["heads"] = {b: L.now(("act", b)) for b in range(8)}
            tokens_to_T(oN, "y_ready")
            rows("dwo", 4, oT)
            tokens_to_T(x, "x_ready")
            cross(0)
            network(0, xT)
            tokens_to_T(x, "x_ready")
            for g in range(GROUPS):
                project("T", f"gq{g}", xT)
                project("T", f"gk{g}", xT)
                project("N", f"gv{g}", xT)
            for b_ in (0, 1, 2, 3):
                pe.wait_ge(free_of(b_), frees(b_))
            for h in range(DIL_HEADS + 2):
                if h < DIL_HEADS:
                    part = slice((h % 2) * HEAD, (h % 2 + 1) * HEAD)
                    for g in range(GROUPS):
                        pe.wait_ge(free_of(g), frees(g))
                        for tt in range(NT):
                            ins = pe.matmul(bank[g][:, tt * T:(tt + 1) * T],
                                            gqT[part, 8 * g + h // 2, tt * P:(tt + 1) * P],
                                            gkT[part, 8 * g + h // 2, :], start=True, stop=True)
                        fill(ins, g, "dve")
                if h >= 2:
                    q = h - 2
                    b = 6 + q % 2
                    for b_ in (3, 4, 5, b):
                        pe.wait_ge(free_of(b_), frees(b_))
                    for tt in range(NT):
                        for kb in range(6):
                            g, kt = kb // 2, kb % 2
                            at = kb * T + tt * P
                            ins = pe.matmul(bank[b][:, tt * HEAD:(tt + 1) * HEAD],
                                            gPT[:, q % 2, at:at + P],
                                            gvN[:, kt, g * D + q * HEAD:g * D + (q + 1) * HEAD],
                                            start=(kb == 0), stop=(kb == 5))
                    fill(ins, b, "act")
                if 0 <= h - 1 < DIL_HEADS:
                    q = h - 1
                    pe.wait_ge(S["r_ready"], L.took("r_ready"))
                    for g in range(GROUPS):
                        pe.wait_ge(free_of(3 + g), frees(3 + g))
                        for kt in range(NT):
                            for tt in range(NT):
                                at = tt * 768 + g * T + kt * P
                                ins = pe.transpose(
                                    bank[3 + g][:, kt * T + tt * P:kt * T + (tt + 1) * P],
                                    gS[:, q % 2, at:at + P], ident[:, :])
                        fill(ins, 3 + g, "act")
            for b_ in (6, 7):
                pe.wait_ge(free_of(b_), frees(b_))
            tokens_to_T(goN, None)
            rows("gwo", 4, goT)
            tokens_to_T(x, "x_ready")
            cross(1)
            network(1, xT)
            more_tensor(pe, L, free_of, frees, fill, slab, begun, col_T, col_N, rows, tokens_to_T,
                        project, for_rounds, lambda r: {b: L.now((r, b)) for b in range(8)})

        @block.gpsimd
        def _(pool):
            L = Ledger(pool, S)
            pool.dma_start(xT, xT_in).then_inc(S["in_xT"], 16)
            pool.dma_start(sideT, memT_in).then_inc(S["in_mem"], 16)
            pool.dma_start(x[:, :, :], x_in).then_inc(S["in_x"], 16)
            pool.dma_start(pt[:, :], pt_in).then_inc(S["in_pt"], 16)
            pool.dma_start(row[:, :], row_in.to_broadcast([P, NROW])).then_inc(S["in_row"], 16)
            pool.iota(diff_i, pattern=[[P, NT], [-1, T]], base=T, channel_multiplier=1) \
                .then_inc(S["iota"], 1)
            pool.wait_ge(S["iota"], L.own("iota"))
            pool.memset(ident[:, :], 0.0).then_inc(S["g_step"], 1)
            pool.wait_ge(S["g_step"], L.own("g_step"))
            pool.affine_select(out=ident[:, :], in_=ident[:, :], compare_op=ALU.not_equal,
                               fill=1.0, base=0, pattern=[[-1, P]], channel_multiplier=1) \
                                   .then_inc(S["consts"], 1)
            pool.wait_ge(S["consts"], L.own("consts"))
            pool.memset(neg_half, -0.5).then_inc(S["g_step"], 1)
            pool.wait_ge(S["g_step"], L.own("g_step"))
            pool.memset(half16, -0.5).then_inc(S["g_step"], 1)
            pool.wait_ge(S["g_step"], L.own("g_step"))
            pool.memset(tri[:, :, :, :], 1.0).then_inc(S["g_step"], 1)
            pool.wait_ge(S["g_step"], L.own("g_step"))
            for m, (op, sign) in enumerate([(ALU.is_ge, 1), (ALU.is_ge, -1),
                                            (ALU.is_gt, 1), (ALU.is_gt, -1)]):
                pool.affine_select(out=tri[:, m, :, :], in_=tri[:, m, :, :], compare_op=op,
                                   fill=0.0, base=0, pattern=[[-sign * P, NT], [sign, T]],
                                   channel_multiplier=-sign).then_inc(S["consts"], 1)
                pool.wait_ge(S["consts"], L.own("consts"))

            def rstd(wide=False):
                pool.wait_ge(S["var_ready"], L.took("var_ready"))
                if wide:
                    ins = pool.tensor_tensor(rs16, ss16, half16, ALU.pow)
                else:
                    ins = pool.tensor_tensor(st_rstd, st_var, neg_half, ALU.pow)
                ins.then_inc(S["rstd_ready"], 1)

            def ln_rows(k):
                if k:
                    pool.wait_ge(S["x_ready"], L.took("x_ready", NT))
                pool.dma_start(lnrow[:, :, :], ln_in[:, 2 * k:2 * k + 2, :].to_broadcast([P, 2, D])
                               ).then_inc(S["in_ln"], 16)

            ln_rows(0)
            rstd(wide=True)
            for k in range(6):
                rstd()
                rstd()
                if k < 5:
                    ln_rows(k + 1)
            more_pool(pool, L, rstd, ln_rows)

        @block.vector
        def _(v):
            L = Ledger(v, S)

            def step(ins):
                ins.then_inc(S["v_step"], 1)
                v.wait_ge(S["v_step"], L.own("v_step"))

            def norm_rows(rows):
                for tt in range(NT):
                    for h in range(2):
                        part = x[:, tt, h * 512:(h + 1) * 512]
                        v.wait_ge(full["dve"][2 * tt + h], L.filled(2 * tt + h))
                        v.scalar_tensor_tensor(out=part, in0=part, scalar=ALPHA,
                                               in1=bank[2 * tt + h][:, :], op0=ALU.mult,
                                               op1=ALU.add).then_inc(free["dve"][2 * tt + h], 1)
                        v.wait_ge(free["dve"][2 * tt + h], L.freed(2 * tt + h))
                        step(v.bn_stats(st_bn[:, tt, h, :], part))
                    step(v.bn_aggr(st_mv[:, tt, :], st_bn[:, tt, :, :]))
                    v.tensor_scalar(st_var, st_mv[:, tt, 1:2].to_broadcast([P, 2]), LN_EPS,
                                    None, ALU.add).then_inc(S["var_ready"], 1)
                    v.wait_ge(S["var_ready"], L.own("var_ready"))
                    if tt == 0:
                        v.wait_ge(S["in_ln"], 16 * (rows + 1))
                    step(v.scalar_tensor_tensor(out=x[:, tt, :], in0=x[:, tt, :],
                                                scalar=st_mv[:, tt, 0:1], in1=lnrow[:, 0, :],
                                                op0=ALU.subtract, op1=ALU.mult))
                    v.wait_ge(S["rstd_ready"], L.took("rstd_ready"))
                    v.scalar_tensor_tensor(out=x[:, tt, :], in0=x[:, tt, :],
                                           scalar=st_rstd[:, 0:1], in1=lnrow[:, 1, :],
                                           op0=ALU.mult, op1=ALU.add).then_inc(S["x_ready"], 1)
                    v.wait_ge(S["x_ready"], L.own("x_ready"))

            def cross():
                for h in range(XH):
                    v.wait_ge(full["dve"][4 + h], L.filled(4 + h))
                    s = bank[4 + h][:, :].rearrange("p (t k) -> p t k", t=NT)
                    m = slice(2 * h, 2 * h + 2)
                    step(v.tensor_reduce(mx[:, m], s, AX.X, ALU.max))
                    v.tensor_scalar(nmx[:, m], mx[:, m], -1.0 / 16, None, ALU.mult) \
                        .then_inc(S["s_ready"], 1)
                    v.wait_ge(S["s_ready"], L.own("s_ready"))
                for h in range(XH):
                    v.wait_ge(S["p_ready"], L.took("p_ready"))
                    m = slice(2 * h, 2 * h + 2)
                    step(v.reciprocal(rs[:, m], sm[:, m]))
                    for tt in range(NT):
                        part = xP[:, h, tt * T:(tt + 1) * T]
                        ins = v.tensor_scalar(part, part, rs[:, 2 * h + tt:2 * h + tt + 1], None,
                                              ALU.mult)
                        if tt == 0:
                            step(ins)
                        else:
                            ins.then_inc(S["a_ready"], 1)
                            v.wait_ge(S["a_ready"], L.own("a_ready"))

            def gated(i, u, conv):
                b = u
                v.wait_ge(free["act"][b], L.up(("raw", b)))
                gate, val = raw[:, u, 0:T], raw[:, u, T:2 * T]
                j = i * 4 + u
                if conv is not None:
                    w = lambda t: pt_col(PT[f"cw{conv}"].start + t * FC, j)
                    p = pre[:, u, :]
                    step(v.tensor_scalar(p, gate, w(1), pt_col(PT[f"cb{conv}"].start, j), ALU.mult,
                                         ALU.add))
                    step(v.scalar_tensor_tensor(out=p[:, 1:T], in0=gate[:, 0:T - 1], scalar=w(0),
                                                in1=p[:, 1:T], op0=ALU.mult, op1=ALU.add))
                    v.scalar_tensor_tensor(out=p[:, 0:T - 1], in0=gate[:, 1:T], scalar=w(2),
                                           in1=p[:, 0:T - 1], op0=ALU.mult, op1=ALU.add) \
                                               .then_inc(S["pre_ready"], 1)
                    v.wait_ge(S["pre_ready"], L.own("pre_ready"))
                v.wait_ge(S["act_ready"], L.took("act_ready"))
                v.tensor_tensor(hT[:, j, :], act[:, u, :], val, ALU.mult).then_inc(S["hT_ready"], 1)
                v.wait_ge(S["hT_ready"], L.own("hT_ready"))

            def pt_col(start, j):
                return pt[:, start + j:start + j + 1] if isinstance(j, int) \
                    else pt[:, start:start + FC][:, bass.ds(j, 1)]

            def network(stage, conv=None):
                L.n.update({("raw", b): marks[stage][b] for b in range(4)})
                one = {("own", "hT_ready"): 1, ("took", "act_ready"): 1}
                if conv is not None:
                    one |= {("own", "v_step"): 2, ("own", "pre_ready"): 1}
                per = {k: 4 * n for k, n in one.items()} | {("raw", b): 1 for b in range(4)}
                with L.rounds(5, per) as i:
                    for u in range(4):
                        gated(i, u, conv)
                for u in range(2):
                    gated(5, u, conv)

            v.wait_ge(S["iota"], L.took("iota"))
            step(v.tensor_scalar(tmpN[:, 0, 0:512], diff_i, -float(T), None, ALU.add))
            step(v.tensor_scalar(tmpN[:, 0, 512:1024], tmpN[:, 0, 0:512], -1.0, None, ALU.mult))
            step(v.tensor_tensor(tmpN[:, 0, 0:512], tmpN[:, 0, 0:512], tmpN[:, 0, 512:1024], ALU.max))
            step(v.tensor_scalar(dist0[:, :], tmpN[:, 0, 0:512], 8.0, None, ALU.mult))
            step(v.tensor_scalar(dist[:, 0, :], tmpN[:, 0, 0:512], float(HALF), NEG, ALU.is_gt,
                                 ALU.mult))
            for g in (1, 2):
                assert HALF * DILATION[g] >= T
                step(v.tensor_scalar(mask_i, diff_i, DILATION[g] - 1, None, ALU.bitwise_and))
                step(v.tensor_scalar(dist[:, g, :], mask_i, 0.0, NEG, ALU.is_gt, ALU.mult))
            for g in range(GROUPS):
                step(v.tensor_tensor(dist[:, g, :], dist[:, g, :], dist0[:, :], ALU.add))
            v.wait_ge(S["in_row"], 16)
            lr = row[:, ROW["lambda"]].rearrange("p (a b c) -> p a b c", a=2, b=2)
            lp = lamp.rearrange("p (a c) -> p a c", a=2)
            step(v.tensor_tensor(lp, lr[:, :, 0, :], lr[:, :, 1, :], ALU.mult))
            v.tensor_reduce(lam2[:, 0:2], lp, AX.X, ALU.add).then_inc(S["lam_ready"], 1)
            v.wait_ge(S["lam_ready"], L.own("lam_ready"))
            v.wait_ge(S["exp_ready"], L.took("exp_ready"))
            step(v.tensor_tensor(lam2[:, 0:1], lam2[:, 3:4], lam2[:, 2:3], ALU.subtract))
            step(v.tensor_scalar(nlam, lam2[:, 0:1], -LAMBDA_INIT, None, ALU.add))

            for h in range(DIFF_HEADS + 1):
                if h < DIFF_HEADS:
                    slope = 2.0 ** (-8.0 * (h + 1) / DIFF_HEADS)
                    base = 4 * (h % 2)
                    for c in range(2):
                        b = 4 + 2 * (h % 2) + c
                        v.wait_ge(full["dve"][b], L.filled(b))
                        s = sS[:, h % 2, c * 512:(c + 1) * 512]
                        v.scalar_tensor_tensor(out=s, in0=dist0[:, :], scalar=-slope,
                                               in1=bank[b][:, :], op0=ALU.mult,
                                               op1=ALU.add).then_inc(free["dve"][b], 1)
                        v.wait_ge(free["dve"][b], L.freed(b))
                    step(v.tensor_reduce(mx[:, base:base + 4],
                                         sS[:, h % 2, :].rearrange("p (r k) -> p r k", k=T),
                                         AX.X, ALU.max))
                    v.tensor_scalar(nmx[:, base:base + 4], mx[:, base:base + 4], -0.125,
                                    None, ALU.mult).then_inc(S["s_ready"], 1)
                    v.wait_ge(S["s_ready"], L.own("s_ready"))
                if h > 0:
                    g = h - 1
                    base = 4 * (g % 2)
                    v.wait_ge(S["p_ready"], L.took("p_ready"))
                    step(v.reciprocal(rs[:, base:base + 4], sm[:, base:base + 4]))
                    step(v.tensor_scalar(rs[:, base + 2:base + 4], rs[:, base + 2:base + 4],
                                         nlam, None, ALU.mult))
                    for tt in range(NT):
                        a = aS[:, g % 2, tt * T:(tt + 1) * T]
                        p0 = sS[:, g % 2, tt * T:(tt + 1) * T]
                        p1 = sS[:, g % 2, (2 + tt) * T:(3 + tt) * T]
                        step(v.tensor_scalar(a, p1, rs[:, base + 2 + tt:base + 3 + tt], None,
                                             ALU.mult))
                        ins = v.scalar_tensor_tensor(out=a, in0=p0,
                                                     scalar=rs[:, base + tt:base + tt + 1],
                                                     in1=a, op0=ALU.mult, op1=ALU.add)
                        if tt == 0:
                            step(ins)
                        else:
                            ins.then_inc(S["a_ready"], 1)
                            v.wait_ge(S["a_ready"], L.own("a_ready"))
            for b in (2, 3):
                v.wait_ge(free["act"][b], marks["heads"][b])
            o4 = oN[:, :, :].rearrange("p t (h e) -> p (t h) e", h=DIFF_HEADS)
            t4 = tmpN[:, :, :].rearrange("p t (h e) -> p (t h) e", h=DIFF_HEADS)
            step(v.tensor_tensor(t4, o4, o4, ALU.mult))
            step(v.tensor_reduce(ss16, t4, AX.X, ALU.add))
            v.tensor_scalar(ss16, ss16, 1.0 / 128, LN_EPS, ALU.mult, ALU.add) \
                .then_inc(S["var_ready"], 1)
            v.wait_ge(S["var_ready"], L.own("var_ready"))
            step(v.tensor_tensor(t4, o4, row[:, ROW["subln"]].unsqueeze(1).to_broadcast([P, 16, 128]),
                                 ALU.mult))
            v.wait_ge(S["rstd_ready"], L.took("rstd_ready"))
            step(v.tensor_scalar(rs16, rs16, 1.0 - LAMBDA_INIT, None, ALU.mult))
            v.tensor_tensor(o4, t4, rs16.unsqueeze(2).to_broadcast([P, 16, 128]), ALU.mult) \
                .then_inc(S["y_ready"], 1)
            v.wait_ge(S["y_ready"], L.own("y_ready"))
            v.wait_ge(S["in_x"], 16)
            v.wait_ge(S["in_pt"], 16)
            norm_rows(0)
            cross()
            norm_rows(1)
            network("f0", conv=0)
            modulation(v, L, 0)
            norm_rows(2)

            for h in range(DIL_HEADS + 1):
                if h < DIL_HEADS:
                    slope = 2.0 ** (-8.0 * (h + 1) / DIL_HEADS)
                    s3 = gS[:, h % 2, :].rearrange("p (t k) -> p t k", t=NT)
                    m = slice(2 * (h % 2), 2 * (h % 2) + 2)
                    for g in range(GROUPS):
                        v.wait_ge(full["dve"][g], L.filled(g))
                        v.scalar_tensor_tensor(
                    out=s3[:, :, g * T:(g + 1) * T],
                    in0=dist[:, g, :].rearrange("p (t k) -> p t k", t=NT), scalar=-slope,
                    in1=bank[g][:, :].rearrange("p (t k) -> p t k", t=NT), op0=ALU.mult,
                    op1=ALU.add).then_inc(free["dve"][g], 1)
                        v.wait_ge(free["dve"][g], L.freed(g))
                    step(v.tensor_reduce(mx[:, m], s3, AX.X, ALU.max))
                    v.tensor_scalar(nmx[:, m], mx[:, m], -0.125, None, ALU.mult) \
                        .then_inc(S["s_ready"], 1)
                    v.wait_ge(S["s_ready"], L.own("s_ready"))
                if h > 0:
                    m = slice(2 * ((h - 1) % 2), 2 * ((h - 1) % 2) + 2)
                    v.wait_ge(S["p_ready"], L.took("p_ready"))
                    r = slice(2 * ((h - 1) % 4), 2 * ((h - 1) % 4) + 2)
                    v.reciprocal(rs[:, r], sm[:, m]).then_inc(S["r_ready"], 1)
                    v.wait_ge(S["r_ready"], L.own("r_ready"))
            norm_rows(3)
            cross()
            norm_rows(4)
            network("f1", conv=1)
            modulation(v, L, 1)
            norm_rows(5)
            more_vector(v, L, step, network)

        @block.scalar
        def _(a):
            L = Ledger(a, S)

            def copy_out(b, dst, src=None, **kw):
                a.wait_ge(full["act"][b], L.filled(b))
                a.activation(dst, bank[b][:, :] if src is None else src,
                             ACT.Copy if not kw else ACT.Identity, **kw).then_inc(free["act"][b], 1)
                L.freed(b)

            def proj_T(dst):
                for u in range(4):
                    copy_out(u, dst[:, 2 * u:2 * u + 2, :])

            def proj_N(dst):
                for u in range(4):
                    copy_out(u, dst[:, :, 256 * u:256 * (u + 1)],
                             bank[u][:, :].rearrange("p (t c) -> p t c", t=NT))

            def x_to_T(dst=None):
                dst = xT if dst is None else dst
                for tt in range(NT):
                    for q in range(2):
                        b = 4 + 2 * tt + q
                        copy_out(b, dst[:, 4 * q:4 * q + 4, tt * P:(tt + 1) * P],
                                 bank[b][:, :].rearrange("p (k c) -> p k c", k=4))

            def cross():
                proj_T(xkT)
                proj_N(xvN)
                proj_T(qT)
                for h in range(XH):
                    a.wait_ge(S["s_ready"], L.took("s_ready"))
                    for tt in range(NT):
                        i = 2 * h + tt
                        ins = a.activation(xP[:, h, tt * T:(tt + 1) * T],
                                           bank[4 + h][:, tt * T:(tt + 1) * T], ACT.Exp,
                                           bias=nmx[:, i:i + 1], scale=1.0 / 16,
                                           accum_out=sm[:, i:i + 1])
                        if tt == 0:
                            ins.then_inc(S["a_step"], 1)
                        else:
                            ins.then_inc(S["p_ready"], 1)
                for h in range(XH):
                    copy_out(h, xPT[:, h, :])
                for h in range(XH):
                    copy_out(4 + h, oT[:, 2 * h:2 * h + 2, :])

            def network(func, conv):
                def one(i, u):
                    if not conv:
                        a.wait_ge(S["hT_ready"], L.n["hidden"] + (i * 4 + (u + 1 - 4)))
                    copy_out(u, raw[:, u, :])
                    if conv:
                        a.wait_ge(S["pre_ready"], L.took("pre_ready"))
                        src = pre[:, u, :]
                    else:
                        a.wait_ge(free["act"][u], L.now(("freed", u)))
                        src = raw[:, u, 0:T]
                    a.activation(act[:, u, :], src, func).then_inc(S["act_ready"], 1)
                per = {("bank", b): 1 for b in range(4)} | {("freed", b): 1 for b in range(4)}
                if conv:
                    per |= {("took", "pre_ready"): 4}
                with L.rounds(5, per) as i:
                    for u in range(4):
                        one(i, u)
                for u in range(2):
                    one(5, u)
                L.up("hidden", FC)

            a.wait_ge(S["in_pt"], 16)
            a.activation(sc_in, pt[:, PT["c"]], ACT.Silu).then_inc(S["sc_ready"], 1)
            a.wait_ge(S["lam_ready"], L.took("lam_ready"))
            a.activation(lam2[:, 2:4], lam2[:, 0:2], ACT.Exp).then_inc(S["exp_ready"], 1)
            proj_T(qT)
            proj_T(kT)
            proj_N(vN)
            for h in range(DIFF_HEADS + 2):
                if h < DIFF_HEADS:
                    a.wait_ge(S["s_ready"], L.took("s_ready"))
                    base = 4 * (h % 2)
                    for r in range(4):
                        part = sS[:, h % 2, r * T:(r + 1) * T]
                        ins = a.activation(part, part, ACT.Exp, bias=nmx[:, base + r:base + r + 1],
                                           scale=0.125, accum_out=sm[:, base + r:base + r + 1])
                        ins.then_inc(S["p_ready" if r == 3 else "a_step"], 1)
                if 0 <= h - 1 < DIFF_HEADS:
                    copy_out((h - 1) % 2, aT[:, (h - 1) % 2, :])
                if h >= 2:
                    g = h - 2
                    b = 2 + g % 2
                    a.wait_ge(full["act"][b], L.filled(b))
                    a.activation(oN[:, :, g * P:(g + 1) * P],
                                 bank[b][:, 0:256].rearrange("p (t e) -> p t e", t=NT),
                                 ACT.Copy).then_inc(free["act"][b], 1)
                    L.freed(b)
            x_to_T(oT)
            x_to_T()
            cross()
            x_to_T()
            network(ACT.Gelu, True)
            x_to_T()
            for g in range(GROUPS):
                proj_T(gqT[:, 8 * g:8 * g + 8, :])
                proj_T(gkT[:, 8 * g:8 * g + 8, :])
                proj_N(gvN[:, :, D * g:D * (g + 1)])
            for h in range(DIL_HEADS + 2):
                if h < DIL_HEADS:
                    a.wait_ge(S["s_ready"], L.took("s_ready"))
                    for tt in range(NT):
                        part = gS[:, h % 2, tt * 768:(tt + 1) * 768]
                        i = 2 * (h % 2) + tt
                        ins = a.activation(part, part, ACT.Exp, bias=nmx[:, i:i + 1], scale=0.125,
                                           accum_out=sm[:, i:i + 1])
                        ins.then_inc(S["p_ready" if tt else "a_step"], 1)
                if 0 <= h - 1 < DIL_HEADS:
                    for g in range(GROUPS):
                        copy_out(3 + g, gPT[:, (h - 1) % 2, g * 512:(g + 1) * 512])
                    a.wait_ge(S["r_ready"], L.took("r_ready"))
                if h >= 2:
                    g = h - 2
                    b = 6 + g % 2
                    a.wait_ge(full["act"][b], L.filled(b))
                    for tt in range(NT):
                        i = 2 * (g % 4) + tt
                        ins = a.activation(goN[:, tt, g * HEAD:(g + 1) * HEAD],
                                           bank[b][:, tt * HEAD:(tt + 1) * HEAD], ACT.Copy,
                                           scale=rs[:, i:i + 1])
                        if tt == 0:
                            ins.then_inc(S["a_step"], 1)
                        else:
                            ins.then_inc(free["act"][b], 1)
                            L.freed(b)
            x_to_T(goT)
            x_to_T()
            cross()
            x_to_T()
            network(ACT.Gelu, True)
            more_scalar(a, L, copy_out, proj_T, proj_N, x_to_T, network)


def kernel(**inputs):
    import concourse.bacc as bacc
    from concourse.bass_utils import run_bass_kernel_spmd

    a = {k: np.asarray(v) for k, v in inputs.items()}

    def cols(w, *starts):
        w = w.reshape(KC, P, w.shape[1] // P, P)
        pick = [c for s in starts for c in s]
        w = w[:, :, pick, :].reshape(KC, P, len(pick) // 2, 2 * P)
        return w.transpose(2, 1, 0, 3).reshape(-1, P, SLAB)

    def span(at, n):
        return range(at // P, (at + n) // P)

    def rows(w):
        return w.reshape(-1, 2, P, D).transpose(0, 2, 1, 3).reshape(-1, P, SLAB)

    def gated(w):
        return cols(w, [c for j in range(FC) for c in (j, FC + j)])

    def with_ada(w, ada):
        net, ada = gated(w), cols(ada, span(0, 6 * D))
        pairs = np.stack([net, ada[:FC]], 1).reshape(-1, P, SLAB)
        return np.concatenate([pairs, ada[FC:]])

    dil, ssd = a["dil_w_qkv"][0], a["ssd_w_in_2"][0]
    pieces = [cols(a["diff_w_qkv"][0], span(0, 3 * D)), rows(a["diff_w_o"][0])]
    for layer in range(2):
        if layer == 1:
            pieces += [cols(dil, span(0, 9 * D)), rows(a["dil_w_o"][0])]
        pieces += [cols(a["xatt_w_kv"][layer], span(0, 2 * D)),
                   cols(a["xatt_w_q"][layer], span(0, D)), rows(a["xatt_w_o"][layer]),
                   with_ada(a["ffn_w_in"][layer], a["ada_w_2"][layer]), rows(a["ffn_w_out"][layer])]
    pieces += [cols(ssd[:, :DI + 2 * DI], span(DI, 3 * D), span(DI + 3 * D, D), span(0, DI)),
               rows(a["ssd_w_out_2"][0]),
               gated(a["ffn_w_in_2"][0]), rows(a["ffn_w_out_2"][0]),
               cols(a["conf_w_pw1_2"][0], [c for j in range(KC) for c in (j, KC + j)]),
               rows(a["conf_w_pw2_2"][0]),
               gated(a["ffn_w_in_2"][1]), rows(a["ffn_w_out_2"][1])]
    slabs = np.concatenate(pieces)
    assert slabs.shape == (SLABS, P, SLAB)

    def T_of(t):
        return np.ascontiguousarray(t.T.reshape(KC, P, T).transpose(1, 0, 2))

    def col(v):
        return v.reshape(-1, P).T

    pt = {"ada_b0": col(a["ada_b_2"][0]), "ada_b1": col(a["ada_b_2"][1]),
          "cw0": col(a["ffn_conv_w"][0]), "cw1": col(a["ffn_conv_w"][1]),
          "cb0": col(a["ffn_conv_b"][0]), "cb1": col(a["ffn_conv_b"][1]),
          "nm0": col(a["norm_mix_g_2"][0]), "nm1": col(a["norm_mix_g_2"][1]),
          "nf0": col(a["norm_ffn_g_2"][0]), "nf1": col(a["norm_ffn_g_2"][1]),
          "scw": col(a["ssd_conv_w_2"][0]), "scb": col(a["ssd_conv_b_2"][0]),
          "snw": col(a["ssd_norm_w_2"][0]), "pb1": col(a["conf_b_pw1_2"][0]),
          "dww": col(a["conf_dw_w_2"][0]), "dwb": col(a["conf_dw_b_2"][0]),
          "clg": col(a["conf_ln_g_2"][0]), "clb": col(a["conf_ln_b_2"][0]),
          "c": np.stack([col(a["c_ctx_2"]), col(a["c_2"][0])], 2).reshape(P, 16)}
    rowv = {"lambda": a["diff_lambda"][0].reshape(-1), "subln": a["diff_subln"][0],
            "dt_bias": np.concatenate([a["ssd_dt_bias_f_2"][0], a["ssd_dt_bias_b_2"][0]]),
            "a_log": np.concatenate([a["ssd_a_log_f_2"][0], a["ssd_a_log_b_2"][0]]),
            "d_skip": a["ssd_d_skip_2"][0]}
    ln = np.stack([t[l, k] for l in range(2) for k in range(3) for t in (a["ln_g"], a["ln_b"])]
                  + [a["conf_b_pw2_2"][0], a["final_norm_g_2"]])
    arrays = {
        "slabs": slabs,
        "x": np.ascontiguousarray(a["x"][0].reshape(NT, P, D).transpose(1, 0, 2)),
        "xT": T_of(a["x"][0]), "memT": T_of(a["mem"][0]),
        "ctx": np.ascontiguousarray(a["ctx_2"][0].reshape(NT, P, D).transpose(1, 0, 2)),
        "pt": np.concatenate([pt[k] for k in PT], 1),
        "row": np.concatenate([rowv[k] for k in ROW])[None, :],
        "ln": ln[None],
        "wdt": np.ascontiguousarray(ssd[:, 3 * DI:].reshape(KC, P, 64).transpose(1, 0, 2)),
    }
    nc = bacc.Bacc("TRN2", target_bir_lowering=False, num_devices=1)
    args = [nc.dram_tensor(f"{k}_dram", t.shape, F32, kind="ExternalInput").ap() for k, t in arrays.items()]
    res = nc.dram_tensor("res", (P, NT, D), F32, kind="ExternalOutput").ap()
    build(nc, *args, res)
    got = run_bass_kernel_spmd(nc, [{f"{k}_dram": t for k, t in arrays.items()}], core_ids=[0]).results[0]["res"]
    return np.asarray(got).transpose(1, 0, 2).reshape(1, T, D)
```

```python
import math
from contextlib import ExitStack, contextmanager

import concourse.bass as bass
import numpy as np
from concourse import mybir

F32 = mybir.dt.float32
F32R = mybir.dt.float32r
I32 = mybir.dt.int32
ALU = mybir.AluOpType
ACT = mybir.ActivationFunctionType
AX = mybir.AxisListType

P = 128
D = 1024
T = 256
NT = T // P
KC = D // P
SLAB = 2048
RING = 4
FF = 2816
FC = FF // P
HEAD = 64
DIFF_HEADS = 8
DIL_HEADS = 16
GROUPS = 3
DILATION = (1, 4, 16)
HALF = 64
XH = 4
ALPHA = 4 ** 0.25
LN_EPS = 1e-5
EPS = 1e-6
LAMBDA_INIT = 0.8 - 0.6 * math.exp(-0.3 * 0)
NEG = 1e30
DI = 2048
SH = 32
SG = 8
CONF_K = 31
GRID_W = 64
ROWS = T // GRID_W
HC = KC // 2
PE_CONV = 2

STAGES = [("dq", 4), ("dk", 4), ("dv", 4), ("dwo", 4),
          ("xk0", 4), ("xv0", 4), ("xq0", 4), ("xwo0", 4), ("f0", 46), ("fo0", 11),
          ("gq0", 4), ("gk0", 4), ("gv0", 4), ("gq1", 4), ("gk1", 4), ("gv1", 4),
          ("gq2", 4), ("gk2", 4), ("gv2", 4), ("gwo", 4),
          ("xk1", 4), ("xv1", 4), ("xq1", 4), ("xwo1", 4), ("f1", 46), ("fo1", 11),
          ("sxb", 12), ("sc", 4), ("sz", 8), ("swo", 8),
          ("h0", 22), ("ho0", 11),
          ("pw1", 8), ("pw2", 4), ("h1", 22), ("ho1", 11)]
FIRST = {}
_at = 0
for _name, _n in STAGES:
    FIRST[_name] = _at
    _at += _n
SLABS = _at
assert SLABS % RING == 0

RUNS = [("dq", "xk0"), ("xk0", "f0"), ("gq0", "gwo"), ("xk1", "f1")]

PT = {}
_at = 0
for _name, _n in [("ada_b0", 48), ("ada_b1", 48), ("cw0", 3 * FC), ("cw1", 3 * FC), ("cb0", FC),
                  ("cb1", FC), ("nm0", 8), ("nm1", 8), ("nf0", 8), ("nf1", 8), ("scw", 5 * 32),
                  ("scb", 32), ("snw", 16), ("pb1", 16), ("dww", CONF_K * 8), ("dwb", 8),
                  ("clg", 8), ("clb", 8), ("c", 16)]:
    PT[_name] = slice(_at, _at + _n)
    _at += _n
NPT = _at

ROW = {}
_at = 0
for _name, _n in [("lambda", 256), ("subln", 128), ("dt_bias", 64), ("a_log", 64), ("d_skip", 32)]:
    ROW[_name] = slice(_at, _at + _n)
    _at += _n
NROW = _at
LNROWS = 14
MORE_SEMS = ["in_ctx", "in_wdt", "mod_ready", "n_ready", "abs_ready", "e_ready", "dA_ready",
             "cum_ready", "ean_ready", "cact_ready", "conv_done", "xw_ready", "dec_ready",
             "m_ready", "m_used", "v_ready", "row_used", "out_ready"]


class Ledger:

    def __init__(self, eng, sems):
        self.eng, self.sems = eng, sems
        self.n, self.local, self.per, self.i = {}, {}, None, None

    def now(self, key):
        base = self.n.get(key, 0)
        if self.per is None:
            return base
        step = self.per.get(key, 0)
        here = base + self.local.get(key, 0)
        return here + self.i * step if step else here

    def up(self, key, k=1):
        if self.per is None:
            self.n[key] = self.n.get(key, 0) + k
        else:
            assert key in self.per, f"{key} is not declared for this loop"
            self.local[key] = self.local.get(key, 0) + k
        return self.now(key)

    @contextmanager
    def rounds(self, count, per):
        with self.eng.Fori(0, count) as i:
            self.i, self.per, self.local = i, per, {}
            yield i
            assert self.local == per, (self.local, per)
        self.i, self.per = None, None
        for key, k in per.items():
            self.n[key] = self.n.get(key, 0) + k * count

    def took(self, name, k=1):
        return self.up(("took", name), k)

    def own(self, name):
        return self.up(("own", name))

    def filled(self, b):
        return self.up(("bank", b))

    def freed(self, b):
        return self.up(("freed", b))


def build(nc, slabs, x_in, xT_in, memT_in, ctx_in, pt_in, row_in, ln_in, wdt_in, out):
    with ExitStack() as ctx:
        def sb(name, shape, dt=F32):
            return ctx.enter_context(nc.sbuf_tensor(name, shape, dt))

        SEMS = ["v_step", "a_step", "g_step", "slab_begun", "in_x", "in_xT", "in_mem", "in_pt",
                "in_row", "in_ln", "iota", "consts", "x_ready", "y_ready", "var_ready",
                "rstd_ready", "lam_ready", "exp_ready", "s_ready", "p_ready", "r_ready", "a_ready",
                "pre_ready", "act_ready", "pick_ready", "hi_ready", "lo_ready", "x_split", "o_split", "u_ready", "diag_ready", "mem_split", "hT_ready", "sc_ready", "stored"] + MORE_SEMS
        S = {name: ctx.enter_context(nc.semaphore(name)) for name in SEMS}
        landed = [ctx.enter_context(nc.semaphore(f"slab_landed{s}")) for s in range(RING)]
        full = {r: [ctx.enter_context(nc.semaphore(f"full_{r}{b}")) for b in range(8)]
                for r in ("act", "dve")}
        free = {r: [ctx.enter_context(nc.semaphore(f"free_{r}{b}")) for b in range(8)]
                for r in ("act", "dve")}

        bank = [ctx.enter_context(nc.psum_tensor(f"bank{b}", [P, 512], F32)) for b in range(8)]

        def aligned():
            return -(-nc.sbuf_base // 32) * 32

        ring_at = aligned()
        ring = sb("ring", [P, RING, SLAB])
        x = sb("x", [P, NT, D])
        xt2 = sb("xt2", [P, KC, 2 * T])
        xT = xt2[:, :, T:2 * T]
        sideT = xt2[:, :, 0:T]
        ident = sb("ident", [P, P])
        dist0 = sb("dist0", [P, 2 * T])
        dist = sb("dist", [P, GROUPS, 2 * T])
        tri_at = aligned()
        tri = sb("tri", [P, 4, NT, T])
        lnrow = sb("lnrow", [P, 2, D])
        pt = sb("pt", [P, NPT])
        row = sb("row", [P, NROW])
        small = sb("small", [P, 640])
        mod = sb("mod", [P, 2, 6, 8, 2])
        sc_in = sb("sc_in", [P, KC, 32])
        arena_at = aligned()
        arena = sb("arena", [P, 28800])

        def cut(at, *dims):
            n = int(np.prod(dims))
            assert at + n <= 28800, (at, dims)
            v = arena[:, at:at + n]
            if len(dims) == 2:
                return v.rearrange("p (a b) -> p a b", a=dims[0])
            if len(dims) == 3:
                return v.rearrange("p (a b c) -> p a b c", a=dims[0], b=dims[1])
            return v

        st_bn = small[:, 0:24].rearrange("p (t s c) -> p t s c", t=2, s=2)
        st_mv = small[:, 24:28].rearrange("p (t c) -> p t c", t=2)
        st_var = small[:, 28:30]
        st_rstd = small[:, 30:32]
        neg_half = small[:, 32:34]
        nlam = small[:, 34:35]
        lam2 = small[:, 35:39]
        mx = small[:, 40:56]
        nmx = small[:, 56:72]
        sm = small[:, 72:88]
        rs = small[:, 88:104]
        ss16 = small[:, 104:120]
        rs16 = small[:, 120:136]
        half16 = small[:, 136:152]
        pick = small[:, 152:154]
        modA = small[:, 168:184]
        lamp = small[:, 184:312]
        dtn = small[:, 312:568].rearrange("p (t h) -> p t h", t=4)
        epsb = small[:, 568:569]

        qT = cut(0, 8, T)
        kT = cut(2048, 8, T)
        vN = cut(4096, NT, D)
        sS = cut(6144, 2, 1024)
        aS = cut(16384, 3, 512)
        aT = cut(9216, 2, 512)
        oN = cut(10240, NT, D)
        oT = cut(12288, 8, T)
        tmpN = cut(14336, NT, D)
        xkT = cut(16384, 8, T)
        xvN = cut(6144, NT, D)
        xP = cut(2048, XH, 512)
        xPT = cut(4096, XH, 512)
        gqT = cut(0, 24, T)
        gkT = cut(6144, 24, T)
        gvN = cut(12288, NT, 3 * D)
        gS = cut(18432, 3, 1536)
        gPT = cut(23040, 2, 1536)
        goT = tri[:, :, :, :].rearrange("p a b c -> p (a b c)").rearrange("p (a b) -> p a b", a=8)
        modR = cut(15360, 4, 256)
        raw = cut(11264, 4, 512)
        pre = cut(13312, 4, T)
        act = cut(14336, 4, T)
        xn = cut(10240, NT, D)

        def part(name, at, *dims):
            return nc.alloc_sbuf_tensor_at(name, [P, *dims], F32R, offset=at)

        w_lo = part("w_lo", ring_at, RING, SLAB)
        w_hi = part("w_hi", arena_at + 4 * 20480, RING, SLAB)
        x_hi = part("x_hi", arena_at + 4 * 18432, KC, T)
        x_lo = part("x_lo", tri_at, KC, T)
        m_hi = part("m_hi", arena_at + 4 * 2048, KC, T)
        m_lo = part("m_lo", arena_at + 4 * 4096, KC, T)
        o_hi = part("o_hi", arena_at + 4 * 8192, KC, T)
        o_lo = part("o_lo", arena_at + 4 * 14336, KC, T)
        h_hi = part("h_hi", arena_at, FC, T)
        h_lo = part("h_lo", arena_at + 4 * FC * T, FC, T)

        diff_i = cut(15360, 512).bitcast(I32)
        mask_i = cut(15872, 512).bitcast(I32)

        block = ctx.enter_context(nc.Block())

        xsN = cut(0, 4, DI)
        xs_ctx, xs_lat = xsN[:, 0:2, :], xsN[:, 2:4, :]
        zN = cut(0, NT, DI)
        bN = cut(8192, NT, D)
        xdt = cut(8192, 2, 2, 512)
        bT = cut(10240, SG, T)
        cT = cut(12288, SG, T)
        h0T = cut(14336, SG, 512)
        yT = cut(14336, 16, T)
        craw = cut(18432, 4, 512)
        xw = [cut(18432, NT, DI), cut(22528, NT, DI)]
        yN = cut(18432, NT, DI)
        ctxN = cut(20480, NT, D)
        wdt = cut(22528, KC, 64)
        xn2 = cut(23040, NT, D)
        cpre = cut(23040, 4, 512)
        cact = cut(25088, 4, 512)
        seg = cut(22528, 2, 768)
        mT = cut(24064, 2, 768)
        gT = cut(25600, 2, 768)
        t1 = dist[:, 0, :]
        t2 = dist[:, 1, :]
        dA = cut(27136, 4, 64)
        cumN = cut(27392, 256)
        eN = cut(27648, 256)
        nac = cut(27904, NT, 64)
        acT = cut(28032, 256)
        expA = cut(28288, 64)
        wend = cut(28352, NT, 64)
        tmp = [cut(12288 + 256 * i, 4, 64) for i in range(6)]
        acc = small[:, 570:571]
        squares = dist[:, 0:2, :].rearrange("p a b -> p (a b)")
        uraw = cut(0, 8, 512)
        uT = cut(4096, KC, T)
        diag = [cut(at, CONF_K, P) for at in (14336, 20480)]
        vT = cut(6144, KC, T)
        vN2 = cut(8192, NT, D)
        wT = cut(12288, KC, T)
        gate_row, bias_row = lnrow[:, 0, :], lnrow[:, 1, :]

        def along_row(t, lo, hi):
            return t.rearrange("p (r w) -> p r w", r=ROWS)[:, :, lo:hi]

        def mod_col(layer, part, c, s):
            return mod[:, layer, part, c, s:s + 1]

        modA_v = modA.rearrange("p (c s) -> p c s", s=2)

        def modulation(v, L, layer):
            v.wait_ge(full["dve"][4], L.filled(4))
            bias = pt[:, PT[f"ada_b{layer}"]].unsqueeze(2).to_broadcast([P, 48, 2])
            v.tensor_tensor(mod[:, layer, :, :, :].rearrange("p a c s -> p (a c) s"),
                            bank[4][:, 0:96].rearrange("p (a s) -> p a s", s=2), bias,
                            ALU.add).then_inc(free["dve"][4], 1)
            v.wait_ge(free["dve"][4], L.freed(4))

        def more_pool(pool, L, rstd, ln_rows, lo, los):
            pool.dma_start(ctxN[:, :, :], ctx_in).then_inc(S["in_ctx"], 16)
            pool.dma_start(wdt[:, :, :], wdt_in).then_inc(S["in_wdt"], 16)
            pool.memset(tri[:, :, :, :], 1.0).then_inc(S["g_step"], 1)
            pool.wait_ge(S["g_step"], L.own("g_step"))
            for m, (op, sign) in enumerate([(ALU.is_ge, 1), (ALU.is_ge, -1),
                                            (ALU.is_gt, 1), (ALU.is_gt, -1)]):
                pool.affine_select(out=tri[:, m, :, :], in_=tri[:, m, :, :], compare_op=op,
                                   fill=0.0, base=0, pattern=[[-sign * P, NT], [sign, T]],
                                   channel_multiplier=-sign).then_inc(S["consts"], 1)
                pool.wait_ge(S["consts"], L.own("consts"))
            pool.wait_ge(S["x_ready"], L.took("x_ready", NT))

            def bias_load(k):
                pool.dma_start(lnrow[:, 1:2, :], ln_in[:, k:k + 1, :].to_broadcast([P, 1, D])
                               ).then_inc(S["in_ln"], 16)
            bias_load(12)
            for n in range(5):
                rstd()
                rstd()
                if n == 2:
                    lo("h0", 0)
                    lo("h0", 1)
                if n == 3:
                    los("h0", 2, 1)
                    for j in range(11):
                        lo("ho0", j)
                    lo("pw1", 0)
                    lo("pw1", 1)
                if n == 4:
                    for j in range(2, KC):
                        lo("pw1", j)
            rstd()
            rstd()
            lo("h1", 0)
            lo("h1", 1)
            pool.wait_ge(S["row_used"], L.took("row_used"))
            bias_load(13)
            rstd()
            rstd()
            los("h1", 2, 1)
            for j in range(11):
                lo("ho1", j)
            for tt in range(NT):
                rstd()
                pool.wait_ge(S["out_ready"], L.took("out_ready"))
                pool.dma_start(out[:, tt, :], x[:, tt, :]).then_inc(S["stored"], 16)
            pool.wait_ge(S["stored"], 16 * NT)

        def more_vector(v, L, step, network, split_x, by_chunks):
            def rms(src, dst, width, ready, tiles=range(NT), junk=None):
                for tt in tiles:
                    step(v.scalar_tensor_tensor(out=squares if junk is None else junk, in0=src[:, tt, :],
                                                scalar=1.0 / width, in1=src[:, tt, :],
                                                op0=ALU.mult, op1=ALU.mult, accum_out=acc))
                    v.tensor_scalar(st_var, acc.to_broadcast([P, 2]), EPS, None, ALU.add) \
                        .then_inc(S["var_ready"], 1)
                    v.wait_ge(S["var_ready"], L.own("var_ready"))
                    v.wait_ge(S["rstd_ready"], L.took("rstd_ready"))
                    v.tensor_scalar(dst[:, tt, :], src[:, tt, :], st_rstd[:, 0:1], None,
                                    ALU.mult).then_inc(S[ready], 1)
                    v.wait_ge(S[ready], L.own(ready))

            def gains(layer, part, name):
                g = pt[:, PT[name]].unsqueeze(2).to_broadcast([P, KC, 2])
                v.scalar_tensor_tensor(out=modA_v, in0=mod[:, layer, part, :, :], scalar=1.0,
                                       in1=g, op0=ALU.add, op1=ALU.mult).then_inc(S["mod_ready"], 1)
                v.wait_ge(S["mod_ready"], L.own("mod_ready"))

            def residual(n, bias=False):
                for b in (4, 5):
                    v.wait_ge(free["act"][b], marks["gate"][n][b])
                if bias:
                    v.wait_ge(S["in_ln"], 16 * 7)
                for tt in range(NT):
                    for h in range(2):
                        b = 2 * tt + h
                        c = slice(h * 512, (h + 1) * 512)
                        v.wait_ge(full["dve"][b], L.filled(b))
                        t = dist[:, h, :]
                        if bias:
                            v.tensor_tensor(t, bank[b][:, :], bias_row[:, c], ALU.add) \
                                .then_inc(free["dve"][b], 1)
                            v.wait_ge(free["dve"][b], L.freed(b))
                            step(v.tensor_tensor(t, t, gate_row[:, c], ALU.mult))
                        else:
                            v.tensor_tensor(t, bank[b][:, :], gate_row[:, c], ALU.mult) \
                                .then_inc(free["dve"][b], 1)
                            v.wait_ge(free["dve"][b], L.freed(b))
                        ins = v.tensor_tensor(x[:, tt, c], x[:, tt, c], t, ALU.add)
                        if bias and b == 3:
                            ins.then_inc(S["row_used"], 1)
                            v.wait_ge(S["row_used"], L.own("row_used"))
                        else:
                            step(ins)

            gains(0, 1, "nm0")
            rms(x, xn2, D, "n_ready")
            v.wait_ge(S["in_ctx"], 16)
            rms(ctxN, ctxN, D, "n_ready")
            v.wait_ge(full["dve"][4], L.filled(4))
            u, m, z, z2, s, e = tmp
            v.tensor_tensor(u, bank[4][:, 0:256].rearrange("p (t h) -> p t h", t=4),
                            row[:, ROW["dt_bias"]].unsqueeze(1).to_broadcast([P, 4, 64]),
                            ALU.add).then_inc(free["dve"][4], 1)
            v.wait_ge(free["dve"][4], L.freed(4))
            step(v.tensor_scalar(m, u, 0.0, None, ALU.max))
            step(v.tensor_scalar(s, u, -1.0, None, ALU.mult))
            v.tensor_tensor(s, s, u, ALU.max).then_inc(S["abs_ready"], 1)
            v.wait_ge(S["abs_ready"], L.own("abs_ready"))
            v.wait_ge(S["e_ready"], L.took("e_ready"))
            step(v.tensor_scalar(z2, e, 2.0, None, ALU.add))
            step(v.reciprocal(z2, z2))
            step(v.tensor_tensor(z, e, z2, ALU.mult))
            step(v.tensor_tensor(z2, z, z, ALU.mult))
            step(v.tensor_scalar(s, z2, 1.0 / 17, None, ALU.mult))
            for k in (15, 13, 11, 9, 7, 5, 3):
                step(v.scalar_tensor_tensor(out=s, in0=s, scalar=1.0 / k, in1=z2, op0=ALU.add,
                                            op1=ALU.mult))
            step(v.scalar_tensor_tensor(out=s, in0=s, scalar=1.0, in1=z, op0=ALU.add, op1=ALU.mult))
            step(v.scalar_tensor_tensor(out=dtn, in0=s, scalar=2.0, in1=m, op0=ALU.mult, op1=ALU.add))
            v.scalar_tensor_tensor(out=dA, in0=dtn, scalar=-1.0,
                                   in1=expA.unsqueeze(1).to_broadcast([P, 4, 64]),
                                   op0=ALU.mult, op1=ALU.mult).then_inc(S["dA_ready"], 1)
            v.wait_ge(S["dA_ready"], L.own("dA_ready"))

            def taps(dst, src, n, w, b):
                d3 = dst.rearrange("p (n t) -> p n t", n=n)
                s3 = src.rearrange("p (n t) -> p n t", n=n)
                step(v.tensor_scalar(dst, src, w(2), b, ALU.mult, ALU.add))
                for k in (0, 1, 3, 4):
                    o = k - 2
                    lo, hi = max(0, -o), T - max(0, o)
                    ins = v.scalar_tensor_tensor(out=d3[:, :, lo:hi], in0=s3[:, :, lo + o:hi + o],
                                                 scalar=w(k), in1=d3[:, :, lo:hi], op0=ALU.mult,
                                                 op1=ALU.add)
                    if k < 4:
                        step(ins)
                return ins

            def wcol(j):
                scw, scb = PT["scw"].start, PT["scb"].start
                return (lambda k: pt[:, scw + k * 32 + j:scw + k * 32 + j + 1]), \
                    pt[:, scb + j:scb + j + 1]

            for j in range(24):
                if j == 1:
                    v.wait_ge(full["dve"][5], L.filled(5))
                    v.tensor_copy(cumN, bank[5][:, 0:256]).then_inc(free["dve"][5], 1)
                    v.wait_ge(free["dve"][5], L.freed(5))
                    v.tensor_scalar(nac, cumN[:, 0:128].rearrange("p (t h) -> p t h", t=NT),
                                    -1.0, None, ALU.mult).then_inc(S["cum_ready"], 1)
                    v.wait_ge(S["cum_ready"], L.own("cum_ready"))
                    v.wait_ge(full["dve"][6], L.filled(6))
                    v.tensor_copy(acT[0:64, :], bank[6][0:64, 0:T]).then_inc(free["dve"][6], 1)
                    v.wait_ge(free["dve"][6], L.freed(6))
                    v.wait_ge(S["ean_ready"], L.took("ean_ready"))
                    step(v.tensor_tensor(wend, dtn[:, 0:2, :],
                                         eN[:, 128:256].rearrange("p (t h) -> p t h", t=NT),
                                         ALU.mult))
                v.wait_ge(free["act"][j % 4], marks["conv"][j % 4] + j // 4 + 1)
                w, b = wcol(j)
                taps(cpre[:, j % 4, :], craw[:, j % 4, :], 2, w, b).then_inc(S["pre_ready"], 1)
                v.wait_ge(S["pre_ready"], L.own("pre_ready"))
            for j in range(4):
                v.wait_ge(free["act"][j], marks["conv"][j] + 6 + 1)
                for c in range(2):
                    w, b = wcol(24 + 2 * j + c)
                    part = slice(c * T, (c + 1) * T)
                    ins = taps(cpre[:, j, part], craw[:, j, part], 1, w, b)
                    if c == 0:
                        step(ins)
                    else:
                        ins.then_inc(S["pre_ready"], 1)
                        v.wait_ge(S["pre_ready"], L.own("pre_ready"))
            step(v.tensor_scalar(tri[:, 0:2, :, :], tri[:, 0:2, :, :], 1.0, NEG, ALU.subtract,
                                 ALU.mult))
            for b in range(4, 8):
                v.wait_ge(free["act"][b], marks["xs"][b])
            v.wait_ge(S["conv_done"], L.took("conv_done"))
            for d in range(2):
                for tt in range(NT):
                    wv = wend[:, tt, 32 * d:32 * d + 32].unsqueeze(2).to_broadcast([P, 32, 64])
                    v.tensor_tensor(xw[d][:, tt, :].rearrange("p (h e) -> p h e", e=64),
                                    xs_ctx[:, tt, :].rearrange("p (h e) -> p h e", e=64),
                                    wv, ALU.mult).then_inc(S["xw_ready"], 1)
                    v.wait_ge(S["xw_ready"], L.own("xw_ready"))

            def heads4(ap):
                return ap.rearrange("p t (h e) -> p t h e", h=4)

            def combine(g):
                c4 = slice(g * 256, (g + 1) * 256)
                y = yN[:, :, c4]
                ea = eN[:, 0:128].rearrange("p (t h) -> p t h", t=NT)
                for d, t in ((0, t1), (1, t2)):
                    b = 5 + d
                    v.wait_ge(full["dve"][b], L.filled(b))
                    w = ea[:, :, 32 * d + 4 * g:32 * d + 4 * g + 4].unsqueeze(3) \
                        .to_broadcast([P, NT, 4, 64])
                    v.tensor_tensor(
                t.rearrange("p (t h e) -> p t h e", t=NT, h=4),
                bank[b][:, :].rearrange("p (t h e) -> p t h e", t=NT, h=4), w,
                ALU.mult).then_inc(free["dve"][b], 1)
                    v.wait_ge(free["dve"][b], L.freed(b))
                step(v.tensor_tensor(t1, t1, t2, ALU.add))
                v.wait_ge(full["dve"][4], L.filled(4))
                v.tensor_tensor(y, bank[4][:, :].rearrange("p (t c) -> p t c", t=NT),
                                t1.rearrange("p (t c) -> p t c", t=NT), ALU.add) \
                                    .then_inc(free["dve"][4], 1)
                v.wait_ge(free["dve"][4], L.freed(4))
                w = row[:, ROW["d_skip"]][:, 4 * g:4 * g + 4].unsqueeze(1).unsqueeze(3) \
                    .to_broadcast([P, NT, 4, 64])
                step(v.tensor_tensor(t2.rearrange("p (t h e) -> p t h e", t=NT, h=4),
                                     heads4(xs_lat[:, :, c4]), w, ALU.mult))
                step(v.tensor_tensor(y, y, t2.rearrange("p (t c) -> p t c", t=NT), ALU.add))

            blocks = [(0, 0, 0, T, 0), (0, 1, P, T, 256), (1, 0, 0, P, 384), (1, 1, 0, T, 512)]
            for q in range(SH + 2):
                g, j = q // 4, q % 4
                if q < SH:
                    b = q % 2
                    v.wait_ge(full["dve"][b], L.filled(b))
                    for n, (d, st, lo, hi, at) in enumerate(blocks):
                        ins = v.scalar_tensor_tensor(
                            out=seg[:, q % 2, at:at + hi - lo],
                            in0=bank[b][:, d * T + lo:d * T + hi],
                            scalar=nac[:, st, 32 * d + q:32 * d + q + 1],
                            in1=tri[:, d, st, lo:hi], op0=ALU.add, op1=ALU.min)
                        if n < 3:
                            step(ins)
                        else:
                            ins.then_inc(free["dve"][b], 1)
                            v.wait_ge(free["dve"][b], L.freed(b))
                    if j == 0:
                        for d in range(2):
                            w = dtn[:, 2:4, 32 * d + q:32 * d + q + 4].unsqueeze(3) \
                                .to_broadcast([P, NT, 4, 64])
                            step(v.tensor_tensor(
                                xdt[:, g % 2, d, :].rearrange("p (t h e) -> p t h e", t=NT, h=4),
                                heads4(xs_lat[:, :, g * 256:(g + 1) * 256]), w, ALU.mult))
                if 1 <= q <= SH:
                    k = q - 1
                    v.wait_ge(S["dec_ready"], L.took("dec_ready"))
                    if k == SH - 1:
                        v.wait_ge(S["m_used"], L.took("m_used"))
                    v.wait_ge(free["act"][2], marks["heads_act"][2] + k // 4 + 1)
                    v.tensor_tensor(mT[:, k % 2, :], seg[:, k % 2, :],
                                    gT[:, (k // 4) % 2, :], ALU.mult).then_inc(S["m_ready"], 1)
                    v.wait_ge(S["m_ready"], L.own("m_ready"))
                if q % 4 == 1 and q > 1:
                    combine(g - 1)
            v.wait_ge(free["act"][3], marks["z"][3])
            for tt in range(NT):
                step(v.tensor_tensor(yN[:, tt, :], yN[:, tt, :], zN[:, tt, :], ALU.mult))
                rms(yN, yN, DI, "n_ready", [tt], zN[:, tt, :])
            residual(0)
            gains(0, 4, "nf0")
            rms(x, xn, D, "n_ready")
            network("h0")
            residual(1)
            gains(1, 1, "nm1")
            rms(x, xn, D, "n_ready")
            split_x("pw1", by_chunks)
            dww, dwb = PT["dww"].start, PT["dwb"].start
            for j in range(KC):
                v.wait_ge(free["act"][j % 4], marks["pw1"][j % 4] + j // 4 + 1)
                u2 = uT[:, j, :]
                ins = v.tensor_tensor(u2, uraw[:, j, 0:T], uraw[:, j, T:2 * T], ALU.mult)
                if j < PE_CONV:
                    ins.then_inc(S["u_ready"], 1)
                    continue
                step(ins)
                vv = vT[:, j, :]
                wk = lambda k: pt[:, dww + k * KC + j:dww + k * KC + j + 1]
                mid = CONF_K // 2
                step(v.tensor_scalar(vv, u2, wk(mid), pt[:, dwb + j:dwb + j + 1], ALU.mult, ALU.add))
                reach = mid if j < HC else ROWS - 1
                span = [o for o in range(-reach, reach + 1) if o]
                for o in span:
                    if j < HC:
                        lo, hi = max(0, -o), GRID_W - max(0, o)
                        dst, src = along_row(vv, lo, hi), along_row(u2, lo + o, hi + o)
                    else:
                        lo, hi = max(0, -o) * GRID_W, T - max(0, o) * GRID_W
                        dst, src = vv[:, lo:hi], u2[:, lo + o * GRID_W:hi + o * GRID_W]
                    ins = v.scalar_tensor_tensor(out=dst, in0=src, scalar=wk(mid + o), in1=dst,
                                                 op0=ALU.mult, op1=ALU.add)
                    if o == span[-1]:
                        ins.then_inc(S["v_ready"], 1)
                        v.wait_ge(S["v_ready"], L.own("v_ready"))
                    else:
                        step(ins)
            for tt in range(NT):
                for b in (4 + 2 * tt, 5 + 2 * tt):
                    v.wait_ge(free["act"][b], marks["vN"][b])
                for h in range(2):
                    step(v.bn_stats(st_bn[:, tt, h, :], vN2[:, tt, h * 512:(h + 1) * 512]))
                step(v.bn_aggr(st_mv[:, tt, :], st_bn[:, tt, :, :]))
                v.tensor_scalar(st_var, st_mv[:, tt, 1:2].to_broadcast([P, 2]), EPS, None,
                                ALU.add).then_inc(S["var_ready"], 1)
                v.wait_ge(S["var_ready"], L.own("var_ready"))
                v.wait_ge(S["rstd_ready"], L.took("rstd_ready"))
                v.tensor_scalar(vN2[:, tt, :], vN2[:, tt, :], st_mv[:, tt, 0:1],
                                st_rstd[:, 0:1], ALU.subtract, ALU.mult).then_inc(S["n_ready"], 1)
                v.wait_ge(S["n_ready"], L.own("n_ready"))
            residual(2, bias=True)
            gains(1, 4, "nf1")
            rms(x, xn, D, "n_ready")
            network("h1")
            residual(3)
            v.wait_ge(S["in_ln"], 16 * 8)
            for tt in range(NT):
                rms(x, xn, D, "v_step", [tt])
                v.tensor_tensor(x[:, tt, :], xn[:, tt, :], bias_row, ALU.mult) \
                    .then_inc(S["out_ready"], 1)
                v.wait_ge(S["out_ready"], L.own("out_ready"))

        def more_scalar(a, L, copy_out, proj_T, proj_N, x_to_T, network, hi):
            def mod_out(dst, scale, bias, chunks=KC, func=ACT.Identity):
                for at in range(0, chunks, 8):
                    for q in range(4):
                        a.wait_ge(full["act"][4 + q], L.filled(4 + q))
                        for c in range(2):
                            k = at + 2 * q + c
                            ins = a.activation(dst[:, k, :], bank[4 + q][:, c * T:(c + 1) * T],
                                               func, scale=scale(k),
                                               **({"bias": bias(k)} if bias else {}))
                            if c:
                                ins.then_inc(free["act"][4 + q], 1)
                                L.freed(4 + q)
                            else:
                                ins.then_inc(S["a_step"], 1)

            def modulated(dst, layer, part, s):
                mod_out(dst, lambda k: modA_v[:, k, s:s + 1],
                        lambda k: mod_col(layer, part, k, s))

            def gate_out():
                for h in range(2):
                    copy_out(4 + h, gate_row[:, h * 512:(h + 1) * 512])

            a.wait_ge(S["mod_ready"], L.took("mod_ready"))
            modulated(xT, 0, 0, 1)
            modulated(sideT, 0, 0, 0)
            a.activation(expA, row[:, ROW["a_log"]], ACT.Exp).then_inc(S["a_step"], 1)
            a.wait_ge(S["abs_ready"], L.took("abs_ready"))
            a.activation(tmp[5], tmp[4], ACT.Exp, scale=-1.0).then_inc(S["e_ready"], 1)
            for j in range(24 + 2):
                if j < 24:
                    copy_out(j % 4, craw[:, j % 4, :])
                if j == 1:
                    a.wait_ge(S["cum_ready"], L.took("cum_ready"))
                    a.activation(eN, cumN, ACT.Exp).then_inc(S["ean_ready"], 1)
                if j >= 2:
                    k = j - 2
                    b = 4 + k % 4
                    if k < 16:
                        copy_out(b, xsN[:, :, k * P:(k + 1) * P],
                                 bank[b][:, :].rearrange("p (n c) -> p n c", n=4))
                    else:
                        copy_out(b, bN[:, :, (k - 16) * P:(k - 15) * P],
                                 bank[b][:, 0:256].rearrange("p (n c) -> p n c", n=2))
                if j < 24:
                    a.wait_ge(S["pre_ready"], L.took("pre_ready"))
                    if j < 16:
                        a.activation(cact[:, j % 4, :], cpre[:, j % 4, :], ACT.Silu) \
                            .then_inc(S["cact_ready"], 1)
                    else:
                        a.activation(bT[:, j - 16, :], cpre[:, j % 4, T:2 * T], ACT.Silu) \
                            .then_inc(S["a_step"], 1)
                        a.activation(cact[:, j % 4, 0:T], cpre[:, j % 4, 0:T], ACT.Silu) \
                            .then_inc(S["cact_ready"], 1)
            for j in range(4):
                copy_out(j, craw[:, j, :])
                a.wait_ge(S["pre_ready"], L.took("pre_ready"))
                a.activation(cT[:, 2 * j:2 * j + 2, :], cpre[:, j, :].rearrange(
             "p (c t) -> p c t", c=2), ACT.Silu).then_inc(S["conv_done" if j == 3 else "a_step"], 1)
            for g in range(SG):
                copy_out(4 + g % 4, h0T[:, g, :])
            for q in range(SH):
                g = q // 4
                a.wait_ge(free["dve"][q % 2], marks["heads2"][q % 2] + q // 2 + 1)
                a.activation(seg[:, q % 2, :], seg[:, q % 2, :], ACT.Exp) \
                    .then_inc(S["dec_ready"], 1)
                if q % 4 == 0:
                    a.wait_ge(full["act"][2], L.filled(2))
                    for n, (c0, c1, at) in enumerate([(0, 256, 0), (384, 512, 256), (0, 128, 384),
                                                      (256, 512, 512)]):
                        ins = a.activation(gT[:, g % 2, at:at + c1 - c0], bank[2][:, c0:c1],
                                           ACT.Copy)
                        if n == 3:
                            ins.then_inc(free["act"][2], 1)
                            L.freed(2)
                        else:
                            ins.then_inc(S["a_step"], 1)
                if q % 4 == 1:
                    a.wait_ge(full["act"][3], L.filled(3))
                    a.activation(zN[:, :, g * 256:(g + 1) * 256],
                                 bank[3][:, :].rearrange("p (t c) -> p t c", t=NT),
                                 ACT.Silu).then_inc(free["act"][3], 1)
                    L.freed(3)
            snw = PT["snw"].start
            gate_out()
            mod_out(yT, lambda k: pt[:, snw + k:snw + k + 1], None, 16)
            hi("h0", 0)
            hi("h0", 1)
            a.wait_ge(S["mod_ready"], L.took("mod_ready"))
            modulated(xT, 0, 3, 1)
            gate_out()
            network(ACT.Silu, False, 0)
            hi("pw1", 0)
            hi("pw1", 1)

            def diagonals(j):
                for k in range(CONF_K):
                    w = pt[:, PT["dww"].start + k * KC + j:PT["dww"].start + k * KC + j + 1]
                    ins = a.activation(diag[j][:, k, :], ident[:, :], ACT.Copy, scale=w)
                    ins.then_inc(S["diag_ready" if k == CONF_K - 1 else "a_step"], 1)

            a.wait_ge(S["hT_ready"], L.now("hidden"))
            diagonals(0)
            a.wait_ge(S["mod_ready"], L.took("mod_ready"))
            modulated(xT, 1, 0, 1)
            gate_out()
            pb1 = PT["pb1"].start
            for j in range(KC):
                if j + 2 < KC:
                    hi("pw1", j + 2)
                a.wait_ge(full["act"][j % 4], L.filled(j % 4))
                a.activation(uraw[:, j, 0:T], bank[j % 4][:, 0:T], ACT.Identity,
                             bias=pt[:, pb1 + j:pb1 + j + 1]).then_inc(S["a_step"], 1)
                a.activation(uraw[:, j, T:2 * T], bank[j % 4][:, T:2 * T], ACT.Sigmoid,
                             bias=pt[:, pb1 + 8 + j:pb1 + 9 + j]).then_inc(free["act"][j % 4], 1)
                L.freed(j % 4)
            diagonals(1)
            for j in range(PE_CONV):
                b = PT["dwb"].start + j
                copy_out(j, vT[:, j, :], bank[j][:, 0:T], bias=pt[:, b:b + 1])
            clg, clb = PT["clg"].start, PT["clb"].start
            for tt in range(NT):
                for q in range(2):
                    b = 4 + 2 * tt + q
                    copy_out(b, vN2[:, tt, q * 512:(q + 1) * 512])
            mod_out(wT, lambda k: pt[:, clg + k:clg + k + 1], lambda k: pt[:, clb + k:clb + k + 1],
                    func=ACT.Silu)
            hi("h1", 0)
            hi("h1", 1)
            a.wait_ge(S["mod_ready"], L.took("mod_ready"))
            modulated(xT, 1, 3, 1)
            gate_out()
            network(ACT.Silu, False, 1)

        def more_tensor(pe, L, free_of, frees, fill, slab, begun, col_T, col_T_split, col_N, rows,
                        rows_split, tokens_to_T, project, for_rounds, mark):
            def to_T(src, chunks=KC):
                for at in range(0, chunks, 8):
                    for b_ in (4, 5, 6, 7):
                        pe.wait_ge(free_of(b_), frees(b_))
                    for tt in range(NT):
                        if at == 0:
                            pe.wait_ge(S["n_ready"], L.took("n_ready"))
                        for q in range(4):
                            for c in range(2):
                                k = at + 2 * q + c
                                ins = pe.transpose(
                                    bank[4 + q][:, c * T + tt * P:c * T + (tt + 1) * P],
                                    src[:, tt, k * P:(k + 1) * P], ident[:, :])
                            if tt:
                                fill(ins, 4 + q, "act")
                for b_ in (4, 5, 6, 7):
                    pe.wait_ge(free_of(b_), frees(b_))

            def gate(layer, part):
                for b_ in (4, 5):
                    pe.wait_ge(free_of(b_), frees(b_))
                for c in range(KC):
                    b = 4 + c // 4
                    ins = pe.matmul(bank[b][:, (c % 4) * P:(c % 4 + 1) * P],
                                    mod_col(layer, part, c, 1).to_broadcast([P, P]), ident[:, :],
                                    start=True, stop=True)
                    if c % 4 == 3:
                        fill(ins, b, "act")
                marks.setdefault("gate", []).append(mark("act"))

            def network(stage):
                for_rounds("act")
                marks[stage] = mark("act")
                pe.wait_ge(S["x_split"], L.took("x_split", 4))
                with L.rounds(5, {("act", q): 1 for q in range(4)} | {("took", "lo_ready"): 8}):
                    for u in range(4):
                        col_T_split(stage, u, u)
                for u in range(2):
                    col_T_split(stage, 20 + u, u)

            to_T(xn2)
            to_T(ctxN)
            pe.wait_ge(S["in_wdt"], 16)
            for s, src in enumerate((sideT, xT)):
                for tt in range(NT):
                    at = (2 * s + tt) * 64
                    for k in range(KC):
                        ins = pe.matmul(bank[4][:, at:at + 64], src[:, k, tt * P:(tt + 1) * P],
                                        wdt[:, k, :], start=(k == 0), stop=(k == KC - 1))
            fill(ins, 4, "dve")
            marks["conv"] = mark("act")
            for j in range(24 + 2):
                if j < 24:
                    if j % 2 == 0:
                        w = slab("sxb", j // 2).rearrange("p (k c) -> p k c", k=KC)
                    pe.wait_ge(free_of(j % 4), frees(j % 4))
                    for k in range(KC):
                        ins = pe.matmul(bank[j % 4][:, :],
                                        w[:, k, (j % 2) * P:(j % 2 + 1) * P],
                                        xt2[:, k, :], start=(k == 0), stop=(k == KC - 1))
                        begun(ins, j % 2 == 0 and k == 0)
                    fill(ins, j % 4, "act")
                if j == 2:
                    pe.wait_ge(S["dA_ready"], L.took("dA_ready"))
                    pe.wait_ge(S["consts"], L.took("consts", 4))
                    for b_ in (5, 6):
                        pe.wait_ge(free_of(b_), frees(b_))
                    for n, (stream, masks) in enumerate([(2, (0, 1)), (0, (3, 2))]):
                        for tt in range(NT):
                            for d, mk in enumerate(masks):
                                at = n * 128 + tt * 64 + 32 * d
                                for st in range(NT):
                                    ins = pe.matmul(bank[5][:, at:at + 32],
                                                    tri[:, mk, st, tt * P:(tt + 1) * P],
                                                    dA[:, stream + st, 32 * d:32 * d + 32],
                                                    start=(st == 0), stop=(st == NT - 1))
                    fill(ins, 5, "dve")
                    for d in range(2):
                        for st in range(NT):
                            ins = pe.matmul(bank[6][32 * d:32 * d + 32, 0:T],
                                            dA[:, 2 + st, 32 * d:32 * d + 32], tri[:, d, st, :],
                                            start=(st == 0), stop=(st == NT - 1))
                    fill(ins, 6, "dve")
                if j >= 2:
                    k = j - 2
                    b = 4 + k % 4
                    pe.wait_ge(S["cact_ready"], L.took("cact_ready"))
                    pe.wait_ge(free_of(b), frees(b))
                    for n in range(4 if k < 16 else 2):
                        ins = pe.transpose(bank[b][:, n * P:(n + 1) * P],
                                           cact[:, k % 4, n * P:(n + 1) * P], ident[:, :])
                    fill(ins, b, "act")
            marks["xs"] = mark("act")
            project("T", "sc", xT)
            pe.wait_ge(S["xw_ready"], L.took("xw_ready", 4))
            for g in range(SG):
                b = 4 + g % 4
                pe.wait_ge(free_of(b), frees(b))
                for d in range(2):
                    for st in range(NT):
                        ins = pe.matmul(bank[b][:, d * 256:(d + 1) * 256],
                                        bN[:, st, g * P:(g + 1) * P],
                                        xw[d][:, st, g * 256:(g + 1) * 256],
                                        start=(st == 0), stop=(st == NT - 1))
                fill(ins, b, "act")
            for b_ in (0, 1, 2, 3, 4, 5, 6, 7):
                pe.wait_ge(free_of(b_), frees(b_))
            marks["heads2"], marks["heads_act"] = mark("dve"), mark("act")
            for q in range(SH + 2):
                g, j = q // 4, q % 4
                if q < SH:
                    b = q % 2
                    pe.wait_ge(free_of(b), frees(b))
                    for d in range(2):
                        r = 32 * d + q
                        ins = pe.matmul(bank[b][:, d * T:(d + 1) * T],
                                        ident[0:64, r:r + 1].to_broadcast([64, P]), acT[0:64, :],
                                        start=True, stop=True)
                    fill(ins, b, "dve")
                    if j == 0:
                        pe.wait_ge(free_of(2), frees(2))
                        for st in range(NT):
                            ins = pe.matmul(bank[2][:, st * T:(st + 1) * T],
                                            bT[:, g, st * P:(st + 1) * P], cT[:, g, :],
                                            start=True, stop=True)
                        fill(ins, 2, "act")
                    if j == 1:
                        col_N("sz", g, 3, "act", xT)
                if q >= 2:
                    k = q - 2
                    h, p = k % 4, k % 2
                    pe.wait_ge(S["m_ready"], L.took("m_ready"))
                    if h == 0:
                        pe.wait_ge(free_of(4), frees(4))
                    m = mT[:, p, :]
                    for tt, parts in enumerate([[(0, 0, 0), (1, 0, 384), (1, 1, 512)],
                                                [(0, 0, 128), (0, 1, 256), (1, 1, 640)]]):
                        for n, (d, st, at) in enumerate(parts):
                            xa = st * 256 + h * 64
                            ins = pe.matmul(bank[4][:, tt * 256 + h * 64:tt * 256 + (h + 1) * 64],
                                            m[:, at:at + P], xdt[:, (k // 4) % 2, d, xa:xa + 64],
                                            start=(n == 0), stop=(n == 2))
                    if h == 3:
                        fill(ins, 4, "dve")
                    elif k == SH - 3:
                        ins.then_inc(S["m_used"], 1)
                    if h == 0:
                        for d in range(2):
                            pe.wait_ge(free_of(5 + d), frees(5 + d))
                            for tt in range(NT):
                                ins = pe.matmul(bank[5 + d][:, tt * 256:(tt + 1) * 256],
                                                cT[:, k // 4, tt * P:(tt + 1) * P],
                                                h0T[:, k // 4, d * 256:(d + 1) * 256],
                                                start=True, stop=True)
                            fill(ins, 5 + d, "dve")
            marks["z"] = mark("act")
            gate(0, 2)
            to_T(yN, 16)
            rows("swo", 8, yT)
            to_T(xn)
            marks["xh0"] = mark("act")
            gate(0, 5)
            network("h0")
            rows_split("ho0")
            to_T(xn)
            marks["xpw1"] = mark("act")
            gate(1, 2)
            pe.wait_ge(S["x_split"], L.took("x_split", 4))
            marks["pw1"] = mark("act")
            for j in range(KC):
                col_T_split("pw1", j, j % 4)
            for j in range(PE_CONV):
                pe.wait_ge(S["u_ready"], L.took("u_ready"))
                pe.wait_ge(S["diag_ready"], L.took("diag_ready"))
                pe.wait_ge(free_of(j), frees(j))
                mid = CONF_K // 2
                for n, o in enumerate([0] + [o for o in range(-mid, mid + 1) if o]):
                    lo, hi = max(0, -o), GRID_W - max(0, o)
                    ins = pe.matmul(along_row(bank[j][:, 0:T], lo, hi), diag[j][:, mid + o, :],
                                    along_row(uT[:, j, :], lo + o, hi + o), start=(n == 0),
                                    stop=(n == CONF_K - 1))
                fill(ins, j, "act")
            for k in range(KC):
                if k < PE_CONV:
                    pe.wait_ge(free_of(k), frees(k))
                else:
                    pe.wait_ge(S["v_ready"], L.took("v_ready"))
                for tt in range(NT):
                    b = 4 + 2 * tt + k // 4
                    if k % 4 == 0:
                        pe.wait_ge(free_of(b), frees(b))
                    ins = pe.transpose(bank[b][:, (k % 4) * P:(k % 4 + 1) * P],
                                       vT[:, k, tt * P:(tt + 1) * P], ident[:, :])
                    if k % 4 == 3:
                        fill(ins, b, "act")
            marks["vN"] = mark("act")
            to_T(vN2)
            rows("pw2", 4, wT)
            to_T(xn)
            marks["xh1"] = mark("act")
            gate(1, 5)
            network("h1")
            rows_split("ho1")

        marks = {}

        @block.sync
        def _(sp):
            sp.dma_start(xT, xT_in).then_inc(S["in_xT"], 16)
            for s in range(RING):
                sp.dma_start(ring[:, s, :], slabs[s]).then_inc(landed[s], 16)
            with sp.Fori(1, SLABS // RING) as i:
                for s in range(RING):
                    sp.wait_ge(S["slab_begun"], i * RING + (s + 2 - RING))
                    sp.dma_start(ring[:, s, :], slabs[i * RING + s]).then_inc(landed[s], 16)

        @block.tensor
        def _(pe):
            L = Ledger(pe, S)
            last = {}

            def free_of(b):
                return free[last.get(b, "act")][b]

            def frees(b):
                return L.now((last.get(b, "act"), b))

            def fill(ins, b, first, then=None):
                ins.then_inc(full[first][b], 1)
                last[b] = then or first
                L.up((last[b], b))

            def for_rounds(reader):
                for b in range(4):
                    pe.wait_ge(free_of(b), frees(b))
                    last[b] = reader

            def slab(stage, u, i=0):
                g = FIRST[stage] + u
                pe.wait_ge(landed[g % RING], 16 * (g // RING + 1) + i * 16)
                return ring[:, g % RING, :]

            def begun(ins, first, slabs=1):
                if first and slabs:
                    ins.then_inc(S["slab_begun"], slabs)

            def col_T(stage, u, b, reader, src, i=0):
                w = slab(stage, u, i).rearrange("p (k c) -> p k c", k=KC)
                pe.wait_ge(free_of(b), frees(b))
                for ch in range(2):
                    for k in range(KC):
                        ins = pe.matmul(bank[b][:, ch * T:(ch + 1) * T],
                                        w[:, k, ch * P:(ch + 1) * P], src[:, k, :],
                                        start=(k == 0), stop=(k == KC - 1))
                        begun(ins, ch == 0 and k == 0)
                fill(ins, b, reader)

            def col_N(stage, u, b, reader, src, i=0):
                w = slab(stage, u, i).rearrange("p (k c) -> p k c", k=KC)
                pe.wait_ge(free_of(b), frees(b))
                for tt in range(NT):
                    for k in range(KC):
                        ins = pe.matmul(bank[b][:, tt * 256:(tt + 1) * 256],
                                        src[:, k, tt * P:(tt + 1) * P], w[:, k, :],
                                        start=(k == 0), stop=(k == KC - 1))
                        begun(ins, tt == 0 and k == 0)
                fill(ins, b, reader)

            def pair(stage, u):
                pe.wait_ge(S["lo_ready"], L.took("lo_ready", 2))
                return (FIRST[stage] + u) % RING

            def col_T_split(stage, u, b, src=(x_hi, x_lo)):
                s = pair(stage, u)
                wh = w_hi[:, s, :].rearrange("p (k c) -> p k c", k=KC)
                early = stage in ("f0", "f1")
                wl = (w_hi[:, (s - 1) % RING, :] if early else w_lo[:, s, :]) \
                    .rearrange("p (k c) -> p k c", k=KC)
                pe.wait_ge(free_of(b), frees(b))
                for ch in range(2):
                    dst, c = bank[b][:, ch * T:(ch + 1) * T], slice(ch * P, (ch + 1) * P)
                    for k in range(KC):
                        ins = pe.matmul(dst, wh[:, k, c], src[0][:, k, :], start=(k == 0), stop=False)
                        begun(ins, ch == 0 and k == 0, 2 if early else 1)
                        pe.matmul(dst, wh[:, k, c], src[1][:, k, :], start=False, stop=False)
                        ins = pe.matmul(dst, wl[:, k, c], src[0][:, k, :], start=False,
                                        stop=(k == KC - 1))
                fill(ins, b, "act")

            def col_N_split(stage, u, b, src=(x_hi, x_lo)):
                s = pair(stage, u)
                wh = w_hi[:, s, :].rearrange("p (k c) -> p k c", k=KC)
                wl = w_lo[:, s, :].rearrange("p (k c) -> p k c", k=KC)
                pe.wait_ge(free_of(b), frees(b))
                for tt in range(NT):
                    dst, t = bank[b][:, tt * 256:(tt + 1) * 256], slice(tt * P, (tt + 1) * P)
                    for k in range(KC):
                        ins = pe.matmul(dst, src[0][:, k, t], wh[:, k, :], start=(k == 0), stop=False)
                        begun(ins, tt == 0 and k == 0)
                        pe.matmul(dst, src[0][:, k, t], wl[:, k, :], start=False, stop=False)
                        ins = pe.matmul(dst, src[1][:, k, t], wh[:, k, :], start=False,
                                        stop=(k == KC - 1))
                fill(ins, b, "act")

            def rows_split(stage, src=(h_hi, h_lo), n_slabs=FC // 2, ready=("hT_ready", 2)):
                for b_ in (0, 1, 2, 3):
                    pe.wait_ge(free_of(b_), frees(b_))
                for j in range(n_slabs):
                    if ready:
                        pe.wait_ge(S[ready[0]], L.took(*ready))
                    s = pair(stage, j)
                    wh = w_hi[:, s, :].rearrange("p (k c) -> p k c", k=2)
                    wl = w_lo[:, s, :].rearrange("p (k c) -> p k c", k=2)
                    for k in range(2):
                        for tt in range(NT):
                            t = slice(tt * P, (tt + 1) * P)
                            sh, sl = src[0][:, 2 * j + k, t], src[1][:, 2 * j + k, t]
                            first, end = j == 0 and k == 0, j == n_slabs - 1 and k == 1
                            for n, (st, w) in enumerate([(sh, wh), (sh, wl), (sl, wh)]):
                                for h in range(2):
                                    ins = pe.matmul(bank[2 * tt + h][:, :], st,
                                                    w[:, k, h * 512:(h + 1) * 512],
                                                    start=(first and n == 0), stop=(end and n == 2))
                                    begun(ins, k == 0 and tt == 0 and n == 0 and h == 0)
                                    if end and n == 2:
                                        fill(ins, 2 * tt + h, "dve")

            def rows(stage, n, src):
                for b_ in (0, 1, 2, 3):
                    pe.wait_ge(free_of(b_), frees(b_))
                for j in range(n):
                    w = slab(stage, j).rearrange("p (k c) -> p k c", k=2)
                    for k in range(2):
                        for tt in range(NT):
                            for h in range(2):
                                ins = pe.matmul(bank[2 * tt + h][:, :],
                                                src[:, 2 * j + k, tt * P:(tt + 1) * P],
                                                w[:, k, h * 512:(h + 1) * 512],
                                                start=(j == 0 and k == 0),
                                                stop=(j == n - 1 and k == 1))
                                begun(ins, k == 0 and tt == 0 and h == 0)
                                if j == n - 1 and k == 1:
                                    fill(ins, 2 * tt + h, "dve")

            def tokens_to_T(src, ready, used_up=False):
                for tt in range(NT):
                    if ready and (ready == "x_ready" or tt == 0):
                        pe.wait_ge(S[ready], L.took(ready))
                    for q in range(2):
                        b = 4 + 2 * tt + q
                        pe.wait_ge(free_of(b), frees(b))
                        for k in range(4):
                            c = 4 * q + k
                            ins = pe.transpose(bank[b][:, k * P:(k + 1) * P],
                                               src[:, tt, c * P:(c + 1) * P], ident[:, :])
                            begun(ins, used_up and tt == 0 and c == 0)
                        fill(ins, b, "act")
                for b_ in (4, 5, 6, 7):
                    pe.wait_ge(free_of(b_), frees(b_))

            def project(kind, stage, src):
                for u in range(4):
                    (col_T if kind == "T" else col_N)(stage, u, u, "act", src)

            def project_split(kind, stage, src=(x_hi, x_lo)):
                for u in range(4):
                    (col_T_split if kind == "T" else col_N_split)(stage, u, u, src)

            def cross(layer):
                marks[f"xxq{layer}"] = {b: L.now(("act", b)) for b in range(8)}
                pe.wait_ge(S["mem_split"], L.took("mem_split"))
                project_split("T", f"xk{layer}", (m_hi, m_lo))
                project_split("N", f"xv{layer}", (m_hi, m_lo))
                pe.wait_ge(S["x_split"], L.took("x_split", 4))
                project_split("T", f"xq{layer}")
                for b_ in (0, 1, 2, 3):
                    pe.wait_ge(free_of(b_), frees(b_))
                for h in range(XH):
                    b = 4 + h
                    pe.wait_ge(free_of(b), frees(b))
                    for tt in range(NT):
                        for c in range(2):
                            ins = pe.matmul(bank[b][:, tt * T:(tt + 1) * T],
                                            qT[:, 2 * h + c, tt * P:(tt + 1) * P],
                                            xkT[:, 2 * h + c, :], start=(c == 0), stop=(c == 1))
                    ins.then_inc(full["dve"][b], 1)
                for h in range(XH):
                    pe.wait_ge(S["a_ready"], L.took("a_ready"))
                    for mt in range(NT):
                        for tt in range(NT):
                            ins = pe.transpose(bank[h][:, mt * T + tt * P:mt * T + (tt + 1) * P],
                                               xP[:, h, tt * T + mt * P:tt * T + (mt + 1) * P],
                                               ident[:, :])
                    fill(ins, h, "act")
                for h in range(XH):
                    pe.wait_ge(free_of(h), frees(h))
                    for e in range(2):
                        for mt in range(NT):
                            c = h * 256 + e * P
                            ins = pe.matmul(bank[4 + h][:, e * T:(e + 1) * T],
                                            xvN[:, mt, c:c + P], xPT[:, h, mt * T:(mt + 1) * T],
                                            start=(mt == 0), stop=(mt == NT - 1))
                    fill(ins, 4 + h, "act")
                for b_ in (4, 5, 6, 7):
                    pe.wait_ge(free_of(b_), frees(b_))
                marks[f"oxwo{layer}"] = {b: L.now(("act", b)) for b in range(8)}
                rows_split(f"xwo{layer}", (o_hi, o_lo), 4, ("o_split", 1))
                tokens_to_T(x, "x_ready", used_up=True)

            def ada(stage, u, r, i=0, last_one=False):
                w = slab(stage, u, i).rearrange("p (k c) -> p k c", k=KC)
                b = 5 + r % 2
                pe.wait_ge(free_of(b), frees(b))
                for k in range(KC):
                    q = 32 * (k % 4)
                    ins = pe.matmul(bank[b][q:q + 32, 0:256], sc_in[:, k, :], w[:, k, :],
                                    start=(k < 4), stop=(k >= 4))
                    begun(ins, k == 0 and last_one)
                fill(ins, b, "act")

            def ada_T(j, r):
                pe.wait_ge(free_of(5 + r % 2), frees(5 + r % 2))
                for ch in range(2):
                    at = 2 * (2 * j + ch)
                    dst = bank[4][:, at:at + 2] if isinstance(j, int) \
                        else bank[4][:, 0:96][:, bass.ds(at, 2)]
                    ins = pe.matmul(dst, modR[:, r, ch * P:(ch + 1) * P], pick, start=True,
                                    stop=True)
                return ins

            def network(layer):
                stage = f"f{layer}"
                if layer == 0:
                    pe.wait_ge(S["sc_ready"], L.took("sc_ready"))
                    pe.wait_ge(S["pick_ready"], L.took("pick_ready"))
                pe.wait_ge(free_of(4), frees(4))
                for_rounds("act")
                marks[stage] = {q: L.now(("act", q)) for q in range(8)}
                marks["x" + stage] = marks[stage]
                pe.wait_ge(S["x_split"], L.took("x_split", 4))
                per = {("act", q): 2 if q > 4 else 1 for q in (0, 1, 2, 3, 5, 6)}
                with L.rounds(5, per | {("took", "lo_ready"): 8}) as i:
                    for u in range(4):
                        ada(stage, 2 * u, u, 2 * i)
                        col_T_split(stage, 2 * u + 1, u)
                        ada_T(i * 4 + u, u)
                for u in range(2):
                    ada(stage, 2 * u, u, 10)
                    col_T_split(stage, 2 * u + 41, u)
                    ada_T(20 + u, u)
                ada(stage, 4, 2, 10)
                ada(stage, 5, 3, 10, last_one=True)
                ada_T(22, 2)
                fill(ada_T(23, 3), 4, "dve")
                rows_split(f"fo{layer}")

            pe.wait_ge(S["consts"], L.took("consts"))
            pe.wait_ge(S["x_split"], L.took("x_split", 4))
            project_split("T", "dq")
            project_split("T", "dk")
            project_split("N", "dv")
            for b_ in (0, 1, 2, 3):
                pe.wait_ge(free_of(b_), frees(b_))
            for h in range(DIFF_HEADS + 3):
                if h < DIFF_HEADS:
                    for c in range(2):
                        b = 4 + 2 * (h % 2) + c
                        pe.wait_ge(free_of(b), frees(b))
                        part = slice(c * HEAD, (c + 1) * HEAD)
                        for tt in range(NT):
                            ins = pe.matmul(bank[b][:, tt * T:(tt + 1) * T],
                                            qT[part, h, tt * P:(tt + 1) * P], kT[part, h, :],
                                            start=True, stop=True)
                        fill(ins, b, "dve")
                if h >= 3:
                    g = h - 3
                    b = 2 + g % 2
                    for b_ in (g % 2, b):
                        pe.wait_ge(free_of(b_), frees(b_))
                    for tt in range(NT):
                        for kt in range(NT):
                            ins = pe.matmul(bank[b][:, tt * P:(tt + 1) * P],
                                            aT[:, g % 2, kt * T + tt * P:kt * T + (tt + 1) * P],
                                            vN[:, kt, g * P:(g + 1) * P],
                                            start=(kt == 0), stop=(kt == NT - 1))
                    fill(ins, b, "act")
                if 0 <= h - 2 < DIFF_HEADS:
                    g = h - 2
                    pe.wait_ge(S["a_ready"], L.took("a_ready"))
                    pe.wait_ge(free_of(g % 2), frees(g % 2))
                    for kt in range(NT):
                        for tt in range(NT):
                            ins = pe.transpose(bank[g % 2][:, kt * T + tt * P:kt * T + (tt + 1) * P],
                                               aS[:, g % 3, tt * T + kt * P:tt * T + (kt + 1) * P],
                                               ident[:, :])
                    fill(ins, g % 2, "act")
            marks["heads"] = {b: L.now(("act", b)) for b in range(8)}
            tokens_to_T(oN, "y_ready")
            marks["odwo"] = {b: L.now(("act", b)) for b in range(8)}
            pe.wait_ge(S["o_split"], L.took("o_split", 4))
            rows_split("dwo", (o_hi, o_lo), 4, None)
            tokens_to_T(x, "x_ready")
            cross(0)
            network(0)
            tokens_to_T(x, "x_ready")
            marks["xgq0"] = {b: L.now(("act", b)) for b in range(8)}
            pe.wait_ge(S["x_split"], L.took("x_split", 4))
            for g in range(GROUPS):
                project_split("T", f"gq{g}")
                project_split("T", f"gk{g}")
                project_split("N", f"gv{g}")
            for b_ in (0, 1, 2, 3):
                pe.wait_ge(free_of(b_), frees(b_))
            for h in range(DIL_HEADS + 3):
                if h < DIL_HEADS:
                    part = slice((h % 2) * HEAD, (h % 2 + 1) * HEAD)
                    for g in range(GROUPS):
                        pe.wait_ge(free_of(g), frees(g))
                        for tt in range(NT):
                            ins = pe.matmul(bank[g][:, tt * T:(tt + 1) * T],
                                            gqT[part, 8 * g + h // 2, tt * P:(tt + 1) * P],
                                            gkT[part, 8 * g + h // 2, :], start=True, stop=True)
                        fill(ins, g, "dve")
                if h >= 3:
                    q = h - 3
                    b = 6 + q % 2
                    for b_ in (3, 4, 5, b):
                        pe.wait_ge(free_of(b_), frees(b_))
                    pair_at = q // 2 * P
                    for kb in range(6):
                        g, kt = kb // 2, kb % 2
                        ins = pe.matmul(bank[b][:, 0:T],
                                        gvN[:, kt, g * D + pair_at:g * D + pair_at + P],
                                        gPT[:, q % 2, kb * T:(kb + 1) * T],
                                        start=(kb == 0), stop=(kb == 5))
                    fill(ins, b, "act")
                if 0 <= h - 2 < DIL_HEADS:
                    q = h - 2
                    pe.wait_ge(S["r_ready"], L.took("r_ready"))
                    for g in range(GROUPS):
                        pe.wait_ge(free_of(3 + g), frees(3 + g))
                        for kt in range(NT):
                            for tt in range(NT):
                                at = tt * 768 + g * T + kt * P
                                ins = pe.transpose(
                                    bank[3 + g][:, kt * T + tt * P:kt * T + (tt + 1) * P],
                                    gS[:, q % 3, at:at + P], ident[:, :])
                        fill(ins, 3 + g, "act")
            for b_ in (6, 7):
                pe.wait_ge(free_of(b_), frees(b_))
            rows("gwo", 4, goT)
            tokens_to_T(x, "x_ready")
            cross(1)
            network(1)
            more_tensor(pe, L, free_of, frees, fill, slab, begun, col_T, col_T_split, col_N, rows,
                        rows_split, tokens_to_T, project, for_rounds, lambda r: {b: L.now((r, b)) for b in range(8)})

        @block.gpsimd
        def _(pool):
            L = Ledger(pool, S)
            pool.dma_start(sideT, memT_in).then_inc(S["in_mem"], 16)
            pool.dma_start(x[:, :, :], x_in).then_inc(S["in_x"], 16)
            pool.dma_start(pt[:, :], pt_in).then_inc(S["in_pt"], 16)
            pool.dma_start(row[:, :], row_in.to_broadcast([P, NROW])).then_inc(S["in_row"], 16)
            pool.iota(diff_i, pattern=[[P, NT], [-1, T]], base=T, channel_multiplier=1) \
                .then_inc(S["iota"], 1)
            pool.wait_ge(S["iota"], L.own("iota"))
            pool.memset(sc_in[:, :, :], 0.0).then_inc(S["g_step"], 1)
            pool.wait_ge(S["g_step"], L.own("g_step"))
            pool.memset(ident[:, :], 0.0).then_inc(S["g_step"], 1)
            pool.wait_ge(S["g_step"], L.own("g_step"))
            pool.affine_select(out=ident[:, :], in_=ident[:, :], compare_op=ALU.not_equal,
                               fill=1.0, base=0, pattern=[[-1, P]], channel_multiplier=1) \
                                   .then_inc(S["consts"], 1)
            pool.wait_ge(S["consts"], L.own("consts"))
            pool.memset(neg_half, -0.5).then_inc(S["g_step"], 1)
            pool.wait_ge(S["g_step"], L.own("g_step"))
            pool.memset(half16, -0.5).then_inc(S["g_step"], 1)
            pool.wait_ge(S["g_step"], L.own("g_step"))

            def rstd(wide=False):
                pool.wait_ge(S["var_ready"], L.took("var_ready"))
                if wide:
                    ins = pool.tensor_tensor(rs16, ss16, half16, ALU.pow)
                else:
                    ins = pool.tensor_tensor(st_rstd, st_var, neg_half, ALU.pow)
                ins.then_inc(S["rstd_ready"], 1)

            def ln_rows(k):
                if k:
                    pool.wait_ge(S["x_ready"], L.took("x_ready", NT))
                pool.dma_start(lnrow[:, :, :], ln_in[:, 2 * k:2 * k + 2, :].to_broadcast([P, 2, D])
                               ).then_inc(S["in_ln"], 16)

            def lo(stage, u, i=0):
                s = (FIRST[stage] + u) % RING
                dst = w_hi[:, (s - 1) % RING, :] if stage in ("f0", "f1") else w_lo[:, s, :]
                for h in range(2):
                    c = slice(h * SLAB // 2, (h + 1) * SLAB // 2)
                    pool.wait_ge(S["hi_ready"], L.took("hi_ready"))
                    pool.tensor_tensor(dst[:, c], ring[:, s, c], w_hi[:, s, c].bitcast(F32),
                                       ALU.subtract).then_inc(S["lo_ready"], 1)

            def los(stage, first, slabs_per):
                at = lambda n: n * slabs_per + slabs_per - 1
                with L.rounds(5, {("took", "hi_ready"): 8}) as i:
                    for u in range(4):
                        lo(stage, at(first + u), i)
                for n in range(first + 20, FC):
                    lo(stage, at(n))

            def run_of(first, last):
                for u in range(2, FIRST[last] - FIRST[first]):
                    lo(first, u)

            lo("dq", 0)
            lo("dq", 1)
            run_of("dq", "dwo")
            lo("dwo", 0)
            lo("dwo", 1)
            ln_rows(0)
            rstd(wide=True)
            lo("dwo", 2)
            lo("dwo", 3)
            for k in range(6):
                if k in (0, 3):
                    lo(f"xk{k // 3}", 0)
                    lo(f"xk{k // 3}", 1)
                if k in (1, 4):
                    lo(f"f{k // 4}", 1)
                if k == 2:
                    lo("gq0", 0)
                    lo("gq0", 1)
                rstd()
                rstd()
                if k < 5:
                    ln_rows(k + 1)
                if k in (1, 4):
                    los(f"f{k // 4}", 1, 2)
                    for j in range(11):
                        lo(f"fo{k // 4}", j)
                if k == 2:
                    run_of("gq0", "gwo")
                if k in (0, 3):
                    run_of(f"xk{k // 3}", f"f{k // 3}")
            more_pool(pool, L, rstd, ln_rows, lo, los)

        @block.vector
        def _(v):
            L = Ledger(v, S)

            def step(ins):
                ins.then_inc(S["v_step"], 1)
                v.wait_ge(S["v_step"], L.own("v_step"))

            def norm_rows(rows):
                for tt in range(NT):
                    for h in range(2):
                        part = x[:, tt, h * 512:(h + 1) * 512]
                        v.wait_ge(full["dve"][2 * tt + h], L.filled(2 * tt + h))
                        v.scalar_tensor_tensor(out=part, in0=part, scalar=ALPHA,
                                               in1=bank[2 * tt + h][:, :], op0=ALU.mult,
                                               op1=ALU.add).then_inc(free["dve"][2 * tt + h], 1)
                        v.wait_ge(free["dve"][2 * tt + h], L.freed(2 * tt + h))
                        step(v.bn_stats(st_bn[:, tt, h, :], part))
                    step(v.bn_aggr(st_mv[:, tt, :], st_bn[:, tt, :, :]))
                    v.tensor_scalar(st_var, st_mv[:, tt, 1:2].to_broadcast([P, 2]), LN_EPS,
                                    None, ALU.add).then_inc(S["var_ready"], 1)
                    v.wait_ge(S["var_ready"], L.own("var_ready"))
                    if tt == 0:
                        v.wait_ge(S["in_ln"], 16 * (rows + 1))
                    step(v.scalar_tensor_tensor(out=x[:, tt, :], in0=x[:, tt, :],
                                                scalar=st_mv[:, tt, 0:1], in1=lnrow[:, 0, :],
                                                op0=ALU.subtract, op1=ALU.mult))
                    v.wait_ge(S["rstd_ready"], L.took("rstd_ready"))
                    v.scalar_tensor_tensor(out=x[:, tt, :], in0=x[:, tt, :],
                                           scalar=st_rstd[:, 0:1], in1=lnrow[:, 1, :],
                                           op0=ALU.mult, op1=ALU.add).then_inc(S["x_ready"], 1)
                    v.wait_ge(S["x_ready"], L.own("x_ready"))

            def cross():
                for h in range(XH):
                    v.wait_ge(full["dve"][4 + h], L.filled(4 + h))
                    s = bank[4 + h][:, :].rearrange("p (t k) -> p t k", t=NT)
                    m = slice(2 * h, 2 * h + 2)
                    step(v.tensor_reduce(mx[:, m], s, AX.X, ALU.max))
                    v.tensor_scalar(nmx[:, m], mx[:, m], -1.0 / 16, None, ALU.mult) \
                        .then_inc(S["s_ready"], 1)
                    v.wait_ge(S["s_ready"], L.own("s_ready"))
                for h in range(XH):
                    v.wait_ge(S["p_ready"], L.took("p_ready"))
                    m = slice(2 * h, 2 * h + 2)
                    step(v.reciprocal(rs[:, m], sm[:, m]))
                    for tt in range(NT):
                        part = xP[:, h, tt * T:(tt + 1) * T]
                        ins = v.tensor_scalar(part, part, rs[:, 2 * h + tt:2 * h + tt + 1], None,
                                              ALU.mult)
                        if tt == 0:
                            step(ins)
                        else:
                            ins.then_inc(S["a_ready"], 1)
                            v.wait_ge(S["a_ready"], L.own("a_ready"))

            def gated(i, u, conv):
                b = u
                v.wait_ge(free["act"][b], L.up(("raw", b)))
                gate, val = raw[:, u, 0:T], raw[:, u, T:2 * T]
                j = i * 4 + u
                if conv is not None:
                    w = lambda t: pt_col(PT[f"cw{conv}"].start + t * FC, j)
                    p = pre[:, u, :]
                    step(v.tensor_scalar(p, gate, w(1), pt_col(PT[f"cb{conv}"].start, j), ALU.mult,
                                         ALU.add))
                    step(v.scalar_tensor_tensor(out=p[:, 1:T], in0=gate[:, 0:T - 1], scalar=w(0),
                                                in1=p[:, 1:T], op0=ALU.mult, op1=ALU.add))
                    v.scalar_tensor_tensor(out=p[:, 0:T - 1], in0=gate[:, 1:T], scalar=w(2),
                                           in1=p[:, 0:T - 1], op0=ALU.mult, op1=ALU.add) \
                                               .then_inc(S["pre_ready"], 1)
                    v.wait_ge(S["pre_ready"], L.own("pre_ready"))
                v.wait_ge(S["act_ready"], L.took("act_ready"))
                step(v.tensor_tensor(act[:, u, :], act[:, u, :], val, ALU.mult))
                step(v.tensor_copy(h_hi[:, j, :], act[:, u, :]))
                v.tensor_tensor(h_lo[:, j, :], act[:, u, :], h_hi[:, j, :].bitcast(F32),
                                ALU.subtract).then_inc(S["hT_ready"], 1)
                v.wait_ge(S["hT_ready"], L.own("hT_ready"))

            def pt_col(start, j):
                return pt[:, start + j:start + j + 1] if isinstance(j, int) \
                    else pt[:, start:start + FC][:, bass.ds(j, 1)]

            def split_mem():
                v.wait_ge(S["in_mem"], 16)
                step(v.tensor_copy(m_hi[:, :, :], sideT))
                v.tensor_tensor(m_lo[:, :, :], sideT, m_hi[:, :, :].bitcast(F32), ALU.subtract) \
                    .then_inc(S["mem_split"], 1)
                v.wait_ge(S["mem_split"], L.own("mem_split"))

            def split_x(stage, pieces):
                for b, p in pieces:
                    if stage == "dq":
                        v.wait_ge(S["in_xT"], 16)
                    else:
                        v.wait_ge(free["act"][b], marks["x" + stage][b])
                    step(v.tensor_copy(x_hi[p], xT[p]))
                    v.tensor_tensor(x_lo[p], xT[p], x_hi[p].bitcast(F32), ALU.subtract) \
                        .then_inc(S["x_split"], 1)
                    v.wait_ge(S["x_split"], L.own("x_split"))

            def split_o(stage, pieces):
                for b, p in pieces:
                    v.wait_ge(free["act"][b], marks["o" + stage][b])
                    step(v.tensor_copy(o_hi[p], oT[p]))
                    v.tensor_tensor(o_lo[p], oT[p], o_hi[p].bitcast(F32), ALU.subtract) \
                        .then_inc(S["o_split"], 1)
                    v.wait_ge(S["o_split"], L.own("o_split"))

            by_tile = [(4 + 2 * tt + q, (slice(0, P), slice(4 * q, 4 * q + 4),
                                         slice(tt * P, (tt + 1) * P)))
                       for tt in range(NT) for q in range(2)]
            by_chunks = [(4 + q, (slice(0, P), slice(2 * q, 2 * q + 2), slice(0, T)))
                         for q in range(4)]

            def network(stage, conv=None):
                split_x(stage, by_chunks if conv is None else by_tile)
                L.n.update({("raw", b): marks[stage][b] for b in range(4)})
                one = {("own", "hT_ready"): 1, ("took", "act_ready"): 1, ("own", "v_step"): 2}
                if conv is not None:
                    one |= {("own", "v_step"): 4, ("own", "pre_ready"): 1}
                per = {k: 4 * n for k, n in one.items()} | {("raw", b): 1 for b in range(4)}
                with L.rounds(5, per) as i:
                    for u in range(4):
                        gated(i, u, conv)
                for u in range(2):
                    gated(5, u, conv)

            split_x("dq", by_chunks)
            v.wait_ge(S["iota"], L.took("iota"))
            step(v.tensor_scalar(tmpN[:, 0, 0:512], diff_i, -float(T), None, ALU.add))
            step(v.tensor_scalar(tmpN[:, 0, 512:1024], tmpN[:, 0, 0:512], -1.0, None, ALU.mult))
            step(v.tensor_tensor(tmpN[:, 0, 0:512], tmpN[:, 0, 0:512], tmpN[:, 0, 512:1024], ALU.max))
            step(v.tensor_scalar(dist0[:, :], tmpN[:, 0, 0:512], 8.0, None, ALU.mult))
            step(v.tensor_scalar(dist[:, 0, :], tmpN[:, 0, 0:512], float(HALF), NEG, ALU.is_gt,
                                 ALU.mult))
            for g in (1, 2):
                assert HALF * DILATION[g] >= T
                step(v.tensor_scalar(mask_i, diff_i, DILATION[g] - 1, None, ALU.bitwise_and))
                step(v.tensor_scalar(dist[:, g, :], mask_i, 0.0, NEG, ALU.is_gt, ALU.mult))
            for g in range(GROUPS):
                step(v.tensor_tensor(dist[:, g, :], dist[:, g, :], dist0[:, :], ALU.add))
            v.wait_ge(S["in_row"], 16)
            lr = row[:, ROW["lambda"]].rearrange("p (a b c) -> p a b c", a=2, b=2)
            lp = lamp.rearrange("p (a c) -> p a c", a=2)
            step(v.tensor_tensor(lp, lr[:, :, 0, :], lr[:, :, 1, :], ALU.mult))
            v.tensor_reduce(lam2[:, 0:2], lp, AX.X, ALU.add).then_inc(S["lam_ready"], 1)
            v.wait_ge(S["lam_ready"], L.own("lam_ready"))
            v.wait_ge(S["exp_ready"], L.took("exp_ready"))
            step(v.tensor_tensor(lam2[:, 0:1], lam2[:, 3:4], lam2[:, 2:3], ALU.subtract))
            step(v.tensor_scalar(nlam, lam2[:, 0:1], -LAMBDA_INIT, None, ALU.add))

            v.wait_ge(S["consts"], L.took("consts"))
            v.tensor_reduce(pick, ident.rearrange("p (q c) -> p c q", q=4)[:, 0:2, :], AX.X,
                            ALU.add).then_inc(S["pick_ready"], 1)
            v.wait_ge(S["pick_ready"], L.own("pick_ready"))

            for h in range(DIFF_HEADS + 1):
                if h < DIFF_HEADS:
                    slope = 2.0 ** (-8.0 * (h + 1) / DIFF_HEADS)
                    base = 4 * (h % 2)
                    for c in range(2):
                        b = 4 + 2 * (h % 2) + c
                        v.wait_ge(full["dve"][b], L.filled(b))
                        s = sS[:, h % 2, c * 512:(c + 1) * 512]
                        v.scalar_tensor_tensor(out=s, in0=dist0[:, :], scalar=-slope,
                                               in1=bank[b][:, :], op0=ALU.mult,
                                               op1=ALU.add).then_inc(free["dve"][b], 1)
                        v.wait_ge(free["dve"][b], L.freed(b))
                    step(v.tensor_reduce(mx[:, base:base + 4],
                                         sS[:, h % 2, :].rearrange("p (r k) -> p r k", k=T),
                                         AX.X, ALU.max))
                    v.tensor_scalar(nmx[:, base:base + 4], mx[:, base:base + 4], -0.125,
                                    None, ALU.mult).then_inc(S["s_ready"], 1)
                    v.wait_ge(S["s_ready"], L.own("s_ready"))
                if h > 0:
                    g = h - 1
                    base = 4 * (g % 2)
                    v.wait_ge(S["p_ready"], L.took("p_ready"))
                    step(v.reciprocal(rs[:, base:base + 4], sm[:, base:base + 4]))
                    step(v.tensor_scalar(rs[:, base + 2:base + 4], rs[:, base + 2:base + 4],
                                         nlam, None, ALU.mult))
                    for tt in range(NT):
                        a = aS[:, g % 3, tt * T:(tt + 1) * T]
                        p0 = sS[:, g % 2, tt * T:(tt + 1) * T]
                        p1 = sS[:, g % 2, (2 + tt) * T:(3 + tt) * T]
                        step(v.tensor_scalar(a, p1, rs[:, base + 2 + tt:base + 3 + tt], None,
                                             ALU.mult))
                        ins = v.scalar_tensor_tensor(out=a, in0=p0,
                                                     scalar=rs[:, base + tt:base + tt + 1],
                                                     in1=a, op0=ALU.mult, op1=ALU.add)
                        if tt == 0:
                            step(ins)
                        else:
                            ins.then_inc(S["a_ready"], 1)
                            v.wait_ge(S["a_ready"], L.own("a_ready"))
            for b in (2, 3):
                v.wait_ge(free["act"][b], marks["heads"][b])
            o4 = oN[:, :, :].rearrange("p t (h e) -> p (t h) e", h=DIFF_HEADS)
            t4 = tmpN[:, :, :].rearrange("p t (h e) -> p (t h) e", h=DIFF_HEADS)
            step(v.tensor_tensor(t4, o4, o4, ALU.mult))
            step(v.tensor_reduce(ss16, t4, AX.X, ALU.add))
            v.tensor_scalar(ss16, ss16, 1.0 / 128, LN_EPS, ALU.mult, ALU.add) \
                .then_inc(S["var_ready"], 1)
            v.wait_ge(S["var_ready"], L.own("var_ready"))
            step(v.tensor_tensor(t4, o4, row[:, ROW["subln"]].unsqueeze(1).to_broadcast([P, 16, 128]),
                                 ALU.mult))
            v.wait_ge(S["rstd_ready"], L.took("rstd_ready"))
            step(v.tensor_scalar(rs16, rs16, 1.0 - LAMBDA_INIT, None, ALU.mult))
            v.tensor_tensor(o4, t4, rs16.unsqueeze(2).to_broadcast([P, 16, 128]), ALU.mult) \
                .then_inc(S["y_ready"], 1)
            v.wait_ge(S["y_ready"], L.own("y_ready"))
            v.wait_ge(S["in_x"], 16)
            v.wait_ge(S["in_pt"], 16)
            split_o("dwo", by_tile)
            split_mem()
            norm_rows(0)
            split_x("xq0", by_tile)
            cross()
            split_o("xwo0", by_chunks)
            norm_rows(1)
            network("f0", conv=0)
            modulation(v, L, 0)
            norm_rows(2)

            split_x("gq0", by_tile)

            for h in range(DIL_HEADS + 1):
                if h < DIL_HEADS:
                    slope = 2.0 ** (-8.0 * (h + 1) / DIL_HEADS)
                    s3 = gS[:, h % 3, :].rearrange("p (t k) -> p t k", t=NT)
                    m = slice(2 * (h % 2), 2 * (h % 2) + 2)
                    for g in range(GROUPS):
                        v.wait_ge(full["dve"][g], L.filled(g))
                        v.scalar_tensor_tensor(
                    out=s3[:, :, g * T:(g + 1) * T],
                    in0=dist[:, g, :].rearrange("p (t k) -> p t k", t=NT), scalar=-slope,
                    in1=bank[g][:, :].rearrange("p (t k) -> p t k", t=NT), op0=ALU.mult,
                    op1=ALU.add).then_inc(free["dve"][g], 1)
                        v.wait_ge(free["dve"][g], L.freed(g))
                    step(v.tensor_reduce(mx[:, m], s3, AX.X, ALU.max))
                    v.tensor_scalar(nmx[:, m], mx[:, m], -0.125, None, ALU.mult) \
                        .then_inc(S["s_ready"], 1)
                    v.wait_ge(S["s_ready"], L.own("s_ready"))
                if h > 0:
                    m = slice(2 * ((h - 1) % 2), 2 * ((h - 1) % 2) + 2)
                    v.wait_ge(S["p_ready"], L.took("p_ready"))
                    r = slice(2 * ((h - 1) % 4), 2 * ((h - 1) % 4) + 2)
                    step(v.reciprocal(rs[:, r], sm[:, m]))
                    for tt in range(NT):
                        part = gS[:, (h - 1) % 3, tt * 768:(tt + 1) * 768]
                        ins = v.tensor_scalar(part, part, rs[:, r.start + tt:r.start + tt + 1],
                                              None, ALU.mult)
                        if tt == 0:
                            step(ins)
                        else:
                            ins.then_inc(S["r_ready"], 1)
                            v.wait_ge(S["r_ready"], L.own("r_ready"))
            split_mem()
            norm_rows(3)
            split_x("xq1", by_tile)
            cross()
            split_o("xwo1", by_chunks)
            norm_rows(4)
            network("f1", conv=1)
            modulation(v, L, 1)
            norm_rows(5)
            more_vector(v, L, step, network, split_x, by_chunks)

        @block.scalar
        def _(a):
            L = Ledger(a, S)

            def copy_out(b, dst, src=None, **kw):
                a.wait_ge(full["act"][b], L.filled(b))
                a.activation(dst, bank[b][:, :] if src is None else src,
                             ACT.Copy if not kw else ACT.Identity, **kw).then_inc(free["act"][b], 1)
                L.freed(b)

            def ahead_of(stage, u):
                for first, last in RUNS:
                    if FIRST[first] <= FIRST[stage] + u and FIRST[stage] + u + 2 < FIRST[last]:
                        hi(stage, u + 2)

            def proj_T(dst, stage):
                for u in range(4):
                    ahead_of(stage, u)
                    copy_out(u, dst[:, 2 * u:2 * u + 2, :])

            def proj_N(dst, stage):
                for u in range(4):
                    ahead_of(stage, u)
                    copy_out(u, dst[:, :, 256 * u:256 * (u + 1)],
                             bank[u][:, :].rearrange("p (t c) -> p t c", t=NT))

            def x_to_T(dst=None):
                dst = xT if dst is None else dst
                for tt in range(NT):
                    for q in range(2):
                        b = 4 + 2 * tt + q
                        copy_out(b, dst[:, 4 * q:4 * q + 4, tt * P:(tt + 1) * P],
                                 bank[b][:, :].rearrange("p (k c) -> p k c", k=4))

            def hi(stage, u, i=0):
                g = FIRST[stage] + u
                a.wait_ge(landed[g % RING], 16 * (g // RING + 1) + i * 16)
                for h in range(2):
                    c = slice(h * SLAB // 2, (h + 1) * SLAB // 2)
                    a.activation(w_hi[:, g % RING, c], ring[:, g % RING, c], ACT.Copy) \
                        .then_inc(S["hi_ready"], 1)

            def cross(layer):
                proj_T(xkT, f"xk{layer}")
                proj_N(xvN, f"xv{layer}")
                proj_T(qT, f"xq{layer}")
                for h in range(XH):
                    a.wait_ge(S["s_ready"], L.took("s_ready"))
                    for tt in range(NT):
                        i = 2 * h + tt
                        ins = a.activation(xP[:, h, tt * T:(tt + 1) * T],
                                           bank[4 + h][:, tt * T:(tt + 1) * T], ACT.Exp,
                                           bias=nmx[:, i:i + 1], scale=1.0 / 16,
                                           accum_out=sm[:, i:i + 1])
                        if tt == 0:
                            ins.then_inc(S["a_step"], 1)
                        else:
                            ins.then_inc(S["p_ready"], 1)
                for h in range(XH):
                    copy_out(h, xPT[:, h, :])
                for h in range(XH):
                    copy_out(4 + h, oT[:, 2 * h:2 * h + 2, :])
                hi(f"xwo{layer}", 2)
                hi(f"xwo{layer}", 3)
                hi(f"f{layer}", 1)

            def network(func, conv, layer):
                net, out_ = (f"f{layer}", f"fo{layer}") if conv else (f"h{layer}", f"ho{layer}")

                def ada_out(u):
                    copy_out(5 + u % 2, modR[:, u, :], bank[5 + u % 2][:, 0:256])

                def ahead(n, i=0):
                    if conv:
                        if n < FC - 2:
                            hi(net, 2 * (n + 2) + 1, 2 * i)
                        elif n == FC - 1:
                            hi(out_, 0)
                    else:
                        hi(net, n + 2, i) if n < FC - 2 else hi(out_, n + 2 - FC)

                def one(i, u):
                    if conv:
                        ada_out(u)
                    else:
                        ahead(4 * i + u) if isinstance(i, int) else ahead(u, i)
                        a.wait_ge(S["hT_ready"], L.n["hidden"] + (i * 4 + (u + 1 - 4)))
                    copy_out(u, raw[:, u, :])
                    if conv:
                        ahead(4 * i + u) if isinstance(i, int) else ahead(u, i)
                        a.wait_ge(S["pre_ready"], L.took("pre_ready"))
                        src = pre[:, u, :]
                    else:
                        a.wait_ge(free["act"][u], L.now(("freed", u)))
                        src = raw[:, u, 0:T]
                    a.activation(act[:, u, :], src, func).then_inc(S["act_ready"], 1)
                per = {("bank", b): 1 for b in range(4)} | {("freed", b): 1 for b in range(4)}
                if conv:
                    per |= {("took", "pre_ready"): 4} | {(k, b): 2 for k in ("bank", "freed") for b in (5, 6)}
                if conv:
                    hi(net, 3)
                with L.rounds(5, per) as i:
                    for u in range(4):
                        one(i, u)
                for u in range(2):
                    one(5, u)
                if conv:
                    for u in (2, 3):
                        ada_out(u)
                for j in range(1 if conv else 2, 11):
                    hi(out_, j)
                L.up("hidden", FC)

            hi("dq", 0)
            hi("dq", 1)
            proj_T(qT, "dq")
            proj_T(kT, "dk")
            proj_N(vN, "dv")
            a.wait_ge(S["in_pt"], 16)
            a.wait_ge(S["consts"], L.took("consts"))
            a.activation(sc_in[:, :, 0:2], pt[:, PT["c"]].rearrange("p (k s) -> p k s", s=2),
                         ACT.Silu).then_inc(S["sc_ready"], 1)
            a.wait_ge(S["lam_ready"], L.took("lam_ready"))
            a.activation(lam2[:, 2:4], lam2[:, 0:2], ACT.Exp).then_inc(S["exp_ready"], 1)
            for h in range(DIFF_HEADS + 3):
                if h < DIFF_HEADS:
                    a.wait_ge(S["s_ready"], L.took("s_ready"))
                    base = 4 * (h % 2)
                    for r in range(4):
                        part = sS[:, h % 2, r * T:(r + 1) * T]
                        ins = a.activation(part, part, ACT.Exp, bias=nmx[:, base + r:base + r + 1],
                                           scale=0.125, accum_out=sm[:, base + r:base + r + 1])
                        ins.then_inc(S["p_ready" if r == 3 else "a_step"], 1)
                if 0 <= h - 2 < DIFF_HEADS:
                    copy_out(h % 2, aT[:, h % 2, :])
                if h >= 3:
                    g = h - 3
                    b = 2 + g % 2
                    a.wait_ge(full["act"][b], L.filled(b))
                    a.activation(oN[:, :, g * P:(g + 1) * P],
                                 bank[b][:, 0:256].rearrange("p (t e) -> p t e", t=NT),
                                 ACT.Copy).then_inc(free["act"][b], 1)
                    L.freed(b)
            x_to_T(oT)
            hi("dwo", 2)
            hi("dwo", 3)
            hi("xk0", 0)
            hi("xk0", 1)
            x_to_T()
            cross(0)
            x_to_T()
            network(ACT.Gelu, True, 0)
            hi("gq0", 0)
            hi("gq0", 1)
            x_to_T()
            for g in range(GROUPS):
                proj_T(gqT[:, 8 * g:8 * g + 8, :], f"gq{g}")
                proj_T(gkT[:, 8 * g:8 * g + 8, :], f"gk{g}")
                proj_N(gvN[:, :, D * g:D * (g + 1)], f"gv{g}")
            for h in range(DIL_HEADS + 3):
                if h < DIL_HEADS:
                    a.wait_ge(S["s_ready"], L.took("s_ready"))
                    for tt in range(NT):
                        part = gS[:, h % 3, tt * 768:(tt + 1) * 768]
                        i = 2 * (h % 2) + tt
                        ins = a.activation(part, part, ACT.Exp, bias=nmx[:, i:i + 1], scale=0.125,
                                           accum_out=sm[:, i:i + 1])
                        ins.then_inc(S["p_ready" if tt else "a_step"], 1)
                if 0 <= h - 2 < DIL_HEADS:
                    for g in range(GROUPS):
                        copy_out(3 + g, gPT[:, h % 2, g * 512:(g + 1) * 512])
                if h >= 3:
                    g = h - 3
                    b = 6 + g % 2
                    part = slice((g % 2) * HEAD, (g % 2 + 1) * HEAD)
                    copy_out(b, goT[part, g // 2, :], bank[b][part, 0:T])
            hi("xk1", 0)
            hi("xk1", 1)
            x_to_T()
            cross(1)
            x_to_T()
            network(ACT.Gelu, True, 1)
            more_scalar(a, L, copy_out, proj_T, proj_N, x_to_T, network, hi)


def kernel(**inputs):
    import concourse.bacc as bacc
    from concourse.bass_utils import run_bass_kernel_spmd

    a = {k: np.asarray(v) for k, v in inputs.items()}

    def cols(w, *starts):
        w = w.reshape(KC, P, w.shape[1] // P, P)
        pick = [c for s in starts for c in s]
        w = w[:, :, pick, :].reshape(KC, P, len(pick) // 2, 2 * P)
        return w.transpose(2, 1, 0, 3).reshape(-1, P, SLAB)

    def span(at, n):
        return range(at // P, (at + n) // P)

    def rows(w):
        return w.reshape(-1, 2, P, D).transpose(0, 2, 1, 3).reshape(-1, P, SLAB)

    def gated(w):
        return cols(w, [c for j in range(FC) for c in (j, FC + j)])

    def with_ada(w, ada):
        net, ada = gated(w), cols(ada, span(0, 6 * D))
        pairs = np.stack([ada[:FC], net], 1).reshape(-1, P, SLAB)
        return np.concatenate([pairs, ada[FC:]])

    dil, ssd = a["dil_w_qkv"][0], a["ssd_w_in_2"][0]
    pieces = [cols(a["diff_w_qkv"][0], span(0, 3 * D)), rows(a["diff_w_o"][0])]
    for layer in range(2):
        if layer == 1:
            pieces += [cols(dil, span(0, 9 * D)), rows(a["dil_w_o"][0])]
        pieces += [cols(a["xatt_w_kv"][layer], span(0, 2 * D)),
                   cols(a["xatt_w_q"][layer], span(0, D)), rows(a["xatt_w_o"][layer]),
                   with_ada(a["ffn_w_in"][layer], a["ada_w_2"][layer]), rows(a["ffn_w_out"][layer])]
    pieces += [cols(ssd[:, :DI + 2 * DI], span(DI, 3 * D), span(DI + 3 * D, D), span(0, DI)),
               rows(a["ssd_w_out_2"][0]),
               gated(a["ffn_w_in_2"][0]), rows(a["ffn_w_out_2"][0]),
               cols(a["conf_w_pw1_2"][0], [c for j in range(KC) for c in (j, KC + j)]),
               rows(a["conf_w_pw2_2"][0]),
               gated(a["ffn_w_in_2"][1]), rows(a["ffn_w_out_2"][1])]
    slabs = np.concatenate(pieces)
    assert slabs.shape == (SLABS, P, SLAB)

    def T_of(t):
        return np.ascontiguousarray(t.T.reshape(KC, P, T).transpose(1, 0, 2))

    def col(v):
        return v.reshape(-1, P).T

    pt = {"ada_b0": col(a["ada_b_2"][0]), "ada_b1": col(a["ada_b_2"][1]),
          "cw0": col(a["ffn_conv_w"][0]), "cw1": col(a["ffn_conv_w"][1]),
          "cb0": col(a["ffn_conv_b"][0]), "cb1": col(a["ffn_conv_b"][1]),
          "nm0": col(a["norm_mix_g_2"][0]), "nm1": col(a["norm_mix_g_2"][1]),
          "nf0": col(a["norm_ffn_g_2"][0]), "nf1": col(a["norm_ffn_g_2"][1]),
          "scw": col(a["ssd_conv_w_2"][0]), "scb": col(a["ssd_conv_b_2"][0]),
          "snw": col(a["ssd_norm_w_2"][0]), "pb1": col(a["conf_b_pw1_2"][0]),
          "dww": col(a["conf_dw_w_2"][0]), "dwb": col(a["conf_dw_b_2"][0]),
          "clg": col(a["conf_ln_g_2"][0]), "clb": col(a["conf_ln_b_2"][0]),
          "c": np.stack([col(a["c_ctx_2"]), col(a["c_2"][0])], 2).reshape(P, 16)}
    rowv = {"lambda": a["diff_lambda"][0].reshape(-1), "subln": a["diff_subln"][0],
            "dt_bias": np.concatenate([a["ssd_dt_bias_f_2"][0], a["ssd_dt_bias_b_2"][0]]),
            "a_log": np.concatenate([a["ssd_a_log_f_2"][0], a["ssd_a_log_b_2"][0]]),
            "d_skip": a["ssd_d_skip_2"][0]}
    ln = np.stack([t[l, k] for l in range(2) for k in range(3) for t in (a["ln_g"], a["ln_b"])]
                  + [a["conf_b_pw2_2"][0], a["final_norm_g_2"]])
    arrays = {
        "slabs": slabs,
        "x": np.ascontiguousarray(a["x"][0].reshape(NT, P, D).transpose(1, 0, 2)),
        "xT": T_of(a["x"][0]), "memT": T_of(a["mem"][0]),
        "ctx": np.ascontiguousarray(a["ctx_2"][0].reshape(NT, P, D).transpose(1, 0, 2)),
        "pt": np.concatenate([pt[k] for k in PT], 1),
        "row": np.concatenate([rowv[k] for k in ROW])[None, :],
        "ln": ln[None],
        "wdt": np.ascontiguousarray(ssd[:, 3 * DI:].reshape(KC, P, 64).transpose(1, 0, 2)),
    }
    nc = bacc.Bacc("TRN2", target_bir_lowering=False, num_devices=1)
    args = [nc.dram_tensor(f"{k}_dram", t.shape, F32, kind="ExternalInput").ap() for k, t in arrays.items()]
    res = nc.dram_tensor("res", (P, NT, D), F32, kind="ExternalOutput").ap()
    build(nc, *args, res)
    got = run_bass_kernel_spmd(nc, [{f"{k}_dram": t for k, t in arrays.items()}], core_ids=[0]).results[0]["res"]
    return np.asarray(got).transpose(1, 0, 2).reshape(1, T, D)
```
